# Optimizing a Trainium2 kernel written in Bass

```python
import jax, jax.numpy as jnp
from jax import lax
import numpy as np

D_MODEL = 1024
BATCH = 1
SEQ = 128
DEPTH = 1
DEC_BATCH = 1
DEC_SEQ = 512
PAST_LEN = 256

GRID_W = 64
D_MIX = D_MODEL
D_RWKV = D_MIX // 2
D_CONV = D_MIX - D_RWKV
HEAD_DIM = 64
N_RWKV_HEADS = D_RWKV // HEAD_DIM
CONV_WIDTH = 31
LORA_W = 64
LORA_A = 64
LORA_G = 128
N_GROUPS = 4
N_EXP_PER_GROUP = 8
N_EXPERTS = N_GROUPS * N_EXP_PER_GROUP
TOP_K = 2
D_EXPERT = 256
N_MOD = 6
RMS_EPS = 1e-6
LN_EPS = 1e-5
GN_EPS = 64e-5
SHIFT_COLS = 3 * D_RWKV + LORA_W + LORA_A
IN_COLS = SHIFT_COLS + LORA_G + 2 * D_CONV

kernel_name = 'hymba_rwkv7_conformer_hmoe_diffusion_step'

def rms_norm(x, g):
    xf = x.astype(jnp.float32)
    y = xf * lax.rsqrt(jnp.mean(xf * xf, axis=-1, keepdims=True) + RMS_EPS)
    return (y * g.astype(jnp.float32)).astype(x.dtype)

def layer_norm(x, g, b, eps):
    xf = x.astype(jnp.float32)
    mu = jnp.mean(xf, axis=-1, keepdims=True)
    var = jnp.mean(jnp.square(xf - mu), axis=-1, keepdims=True)
    y = (xf - mu) * lax.rsqrt(var + eps)
    return (y * g.astype(jnp.float32) + b.astype(jnp.float32)).astype(x.dtype)

def grid_pos_embed(rows, dtype):
    t = jnp.arange(rows * GRID_W)
    row = (t // GRID_W).astype(jnp.float32)
    col = (t % GRID_W).astype(jnp.float32)
    quarter = D_MODEL // 4
    freqs = 1.0 / (10000.0 ** (jnp.arange(quarter, dtype=jnp.float32) / quarter))
    ang_r = row[:, None] * freqs[None, :]
    ang_c = col[:, None] * freqs[None, :]
    pe = jnp.concatenate([jnp.sin(ang_r), jnp.cos(ang_r), jnp.sin(ang_c), jnp.cos(ang_c)], axis=-1)
    return pe.astype(dtype)

def adaln_mod(cond, w, b):
    m = jax.nn.silu(cond) @ w + b
    return jnp.split(m[:, None, :], N_MOD, axis=-1)

def shift_prev(z):
    return jnp.pad(z, ((0, 0), (1, 0), (0, 0)))[:, :-1]

def rwkv7_scan_dir(proj, s0, mu, w0, w_b, a0, a_b, k_k, k_a, r_k):
    bsz, t_len, _ = proj.shape
    xs = proj + (shift_prev(proj) - proj) * mu
    r, k, v, zw, za = jnp.split(xs, [D_RWKV, 2 * D_RWKV, 3 * D_RWKV, 3 * D_RWKV + LORA_W], axis=-1)
    w_log = -jax.nn.softplus(-(w0 + jnp.tanh(zw) @ w_b)) - 0.5
    decay = jnp.exp(-jnp.exp(w_log.astype(jnp.float32)))
    a = jax.nn.sigmoid(a0 + za @ a_b)
    kk = (k * k_k).astype(jnp.float32).reshape(bsz, t_len, N_RWKV_HEADS, HEAD_DIM)
    kk = kk / jnp.maximum(jnp.sqrt(jnp.sum(kk * kk, axis=-1, keepdims=True)), 1e-12)
    k = k * (1 + (a - 1) * k_a)
    heads = lambda t: t.astype(jnp.float32).reshape(bsz, t_len, N_RWKV_HEADS, HEAD_DIM)
    r, k, v, a, decay = heads(r), heads(k), heads(v), heads(a), heads(decay)
    b_vec = kk * a

    def step(state, inp):
        r_t, k_t, v_t, w_t, kk_t, b_t = inp
        sa = jnp.einsum('bhvk,bhk->bhv', state, -kk_t)
        state = (state * w_t[:, :, None, :] + sa[..., None] * b_t[:, :, None, :]
                 + v_t[..., None] * k_t[:, :, None, :])
        return state, jnp.einsum('bhvk,bhk->bhv', state, r_t)

    seq = tuple(jnp.moveaxis(t, 1, 0) for t in (r, k, v, decay, kk, b_vec))
    s_final, ys = lax.scan(step, s0.astype(jnp.float32), seq)
    y = jnp.moveaxis(ys, 0, 1)
    bonus = jnp.sum(r * k * r_k.astype(jnp.float32), axis=-1, keepdims=True) * v
    return y + bonus, s_final

def rwkv7_bidir(z_shift, z_g, s0, p):
    bsz, t_len = z_shift.shape[:2]
    y_f, s_f = rwkv7_scan_dir(z_shift, s0[:, 0], p['tshift_mu'][0], p['decay_w0'][0], p['decay_lora_b'][0],
                              p['iclr_a0'][0], p['iclr_lora_b'][0], p['key_k'][0], p['key_a'][0], p['bonus_r_k'][0])
    y_b, s_b = rwkv7_scan_dir(z_shift[:, ::-1], s0[:, 1], p['tshift_mu'][1], p['decay_w0'][1], p['decay_lora_b'][1],
                              p['iclr_a0'][1], p['iclr_lora_b'][1], p['key_k'][1], p['key_a'][1], p['bonus_r_k'][1])
    y = y_f + y_b[:, ::-1]
    y = layer_norm(y, p['gn_g'].reshape(N_RWKV_HEADS, HEAD_DIM), p['gn_b'].reshape(N_RWKV_HEADS, HEAD_DIM), GN_EPS)
    y = y.reshape(bsz, t_len, D_RWKV).astype(z_shift.dtype)
    gate = jax.nn.sigmoid(z_g) @ p['gate_lora_b']
    return y * gate, jnp.stack([s_f, s_b], axis=1)

def conformer_conv(z_conv, p):
    u = z_conv[..., :D_CONV] * jax.nn.sigmoid(z_conv[..., D_CONV:])
    pad = CONV_WIDTH // 2
    h = lax.conv_general_dilated(u, p['conv_dw_w'][:, None, :], window_strides=(1,), padding=((pad, pad),),
                                 dimension_numbers=('NWC', 'WIO', 'NWC'), feature_group_count=D_CONV)
    h = h + p['conv_dw_b']
    h = layer_norm(h, p['conv_ln_g'], p['conv_ln_b'], LN_EPS)
    return jax.nn.silu(h)

def hier_moe(h, p):
    bsz, t_len, d = h.shape
    xt = h.reshape(-1, d)
    n_tok = xt.shape[0]
    g_prob = jax.nn.softmax((xt @ p['router_group_w'] + p['router_group_b']).astype(jnp.float32), axis=-1)
    g_p, g_idx = lax.top_k(g_prob, 1)
    e_logits = (xt @ p['router_expert_w'] + p['router_expert_b']).astype(jnp.float32)
    e_logits = e_logits.reshape(n_tok, N_GROUPS, N_EXP_PER_GROUP)
    e_sel = jnp.take_along_axis(e_logits, g_idx[:, :, None], axis=1)[:, 0]
    e_p, e_idx = lax.top_k(jax.nn.softmax(e_sel, axis=-1), TOP_K)
    e_p = e_p / jnp.sum(e_p, axis=-1, keepdims=True)
    weights = g_p * e_p
    flat_idx = g_idx * N_EXP_PER_GROUP + e_idx
    combine = jnp.sum(jax.nn.one_hot(flat_idx, N_EXPERTS, dtype=jnp.float32) * weights[..., None], axis=1)
    hid = jax.nn.silu(jnp.einsum('nd,edf->nef', xt, p['expert_w_gate'])) * jnp.einsum('nd,edf->nef', xt, p['expert_w_up'])
    hid = hid * combine[..., None].astype(hid.dtype)
    out = jnp.einsum('nef,efd->nd', hid, p['expert_w_down'])
    return out.reshape(bsz, t_len, d)

def trunk_layer(x, cond, s0, p):
    sh1, sc1, g1, sh2, sc2, g2 = adaln_mod(cond, p['ada_w'], p['ada_b'])
    h = rms_norm(x, p['norm1_g']) * (1 + sc1) + sh1
    z = h @ p['w_in']
    z_shift = z[..., :SHIFT_COLS]
    z_g = z[..., SHIFT_COLS:SHIFT_COLS + LORA_G]
    z_conv = z[..., SHIFT_COLS + LORA_G:]
    y_rwkv, s_new = rwkv7_bidir(z_shift, z_g, s0, p)
    y_conv = conformer_conv(z_conv, p)
    x = x + g1 * (jnp.concatenate([y_rwkv, y_conv], axis=-1) @ p['w_out'])
    h = rms_norm(x, p['norm2_g']) * (1 + sc2) + sh2
    x = x + g2 * hier_moe(h, p)
    return x, s_new

def setup_inputs(seed: int = 0) -> dict:
    key = jax.random.key(seed)
    ks = list(jax.random.split(key, 40))
    f32 = jnp.float32

    def nrm(i, shape, scale):
        return scale * jax.random.normal(ks[i], shape, f32)

    return {
        'x_prompt': nrm(0, (BATCH, SEQ, D_MODEL), 1.0),
        'x_sample': nrm(1, (DEC_BATCH, DEC_SEQ, D_MODEL), 1.0),
        'state_rwkv': nrm(2, (DEC_BATCH, DEPTH, 2, N_RWKV_HEADS, HEAD_DIM, HEAD_DIM), 0.5),
        'c': nrm(3, (DEC_BATCH, D_MODEL), 1.0),
        'c_ctx': nrm(4, (D_MODEL,), 1.0),
        'ada_w': nrm(5, (DEPTH, D_MODEL, N_MOD * D_MODEL), 0.5 * D_MODEL ** -0.5),
        'ada_b': nrm(6, (DEPTH, N_MOD * D_MODEL), 0.02),
        'norm1_g': 1.0 + nrm(7, (DEPTH, D_MODEL), 0.05),
        'w_in': nrm(8, (DEPTH, D_MODEL, IN_COLS), D_MODEL ** -0.5),
        'tshift_mu': jax.random.uniform(ks[9], (DEPTH, 2, SHIFT_COLS), f32),
        'decay_w0': nrm(10, (DEPTH, 2, D_RWKV), 0.5),
        'decay_lora_b': nrm(11, (DEPTH, 2, LORA_W, D_RWKV), 0.5 * LORA_W ** -0.5),
        'iclr_a0': nrm(12, (DEPTH, 2, D_RWKV), 0.5),
        'iclr_lora_b': nrm(13, (DEPTH, 2, LORA_A, D_RWKV), 0.5 * LORA_A ** -0.5),
        'key_k': 1.0 + nrm(14, (DEPTH, 2, D_RWKV), 0.1),
        'key_a': 1.0 + nrm(15, (DEPTH, 2, D_RWKV), 0.1),
        'bonus_r_k': nrm(16, (DEPTH, 2, N_RWKV_HEADS, HEAD_DIM), 0.1),
        'gate_lora_b': nrm(17, (DEPTH, LORA_G, D_RWKV), LORA_G ** -0.5),
        'gn_g': 1.0 + nrm(18, (DEPTH, D_RWKV), 0.05),
        'gn_b': nrm(19, (DEPTH, D_RWKV), 0.02),
        'conv_dw_w': nrm(20, (DEPTH, CONV_WIDTH, D_CONV), CONV_WIDTH ** -0.5),
        'conv_dw_b': nrm(21, (DEPTH, D_CONV), 0.02),
        'conv_ln_g': 1.0 + nrm(22, (DEPTH, D_CONV), 0.05),
        'conv_ln_b': nrm(23, (DEPTH, D_CONV), 0.02),
        'w_out': nrm(24, (DEPTH, D_MIX, D_MODEL), D_MIX ** -0.5),
        'norm2_g': 1.0 + nrm(25, (DEPTH, D_MODEL), 0.05),
        'router_group_w': nrm(26, (DEPTH, D_MODEL, N_GROUPS), D_MODEL ** -0.5),
        'router_group_b': nrm(27, (DEPTH, N_GROUPS), 0.01),
        'router_expert_w': nrm(28, (DEPTH, D_MODEL, N_EXPERTS), D_MODEL ** -0.5),
        'router_expert_b': nrm(29, (DEPTH, N_EXPERTS), 0.01),
        'expert_w_gate': nrm(30, (DEPTH, N_EXPERTS, D_MODEL, D_EXPERT), D_MODEL ** -0.5),
        'expert_w_up': nrm(31, (DEPTH, N_EXPERTS, D_MODEL, D_EXPERT), D_MODEL ** -0.5),
        'expert_w_down': nrm(32, (DEPTH, N_EXPERTS, D_EXPERT, D_MODEL), D_EXPERT ** -0.5),
        'final_norm_g': 1.0 + nrm(33, (D_MODEL,), 0.05),
    }

def reference(x_prompt, x_sample, state_rwkv, c, c_ctx, ada_w, ada_b, norm1_g, w_in, tshift_mu,
              decay_w0, decay_lora_b, iclr_a0, iclr_lora_b, key_k, key_a, bonus_r_k, gate_lora_b,
              gn_g, gn_b, conv_dw_w, conv_dw_b, conv_ln_g, conv_ln_b, w_out, norm2_g,
              router_group_w, router_group_b, router_expert_w, router_expert_b,
              expert_w_gate, expert_w_up, expert_w_down, final_norm_g):
    rows = x_sample.shape[1] // GRID_W
    xs = x_sample + grid_pos_embed(rows, x_sample.dtype)[None]
    xp = x_prompt
    ctx_cond = c_ctx[None, :]
    ctx_states = []
    for l in range(DEPTH):
        p = {
            'ada_w': ada_w[l], 'ada_b': ada_b[l], 'norm1_g': norm1_g[l], 'w_in': w_in[l],
            'tshift_mu': tshift_mu[l], 'decay_w0': decay_w0[l], 'decay_lora_b': decay_lora_b[l],
            'iclr_a0': iclr_a0[l], 'iclr_lora_b': iclr_lora_b[l], 'key_k': key_k[l], 'key_a': key_a[l],
            'bonus_r_k': bonus_r_k[l], 'gate_lora_b': gate_lora_b[l], 'gn_g': gn_g[l], 'gn_b': gn_b[l],
            'conv_dw_w': conv_dw_w[l], 'conv_dw_b': conv_dw_b[l], 'conv_ln_g': conv_ln_g[l],
            'conv_ln_b': conv_ln_b[l], 'w_out': w_out[l], 'norm2_g': norm2_g[l],
            'router_group_w': router_group_w[l], 'router_group_b': router_group_b[l],
            'router_expert_w': router_expert_w[l], 'router_expert_b': router_expert_b[l],
            'expert_w_gate': expert_w_gate[l], 'expert_w_up': expert_w_up[l], 'expert_w_down': expert_w_down[l],
        }
        s_zero = jnp.zeros((xp.shape[0], 2, N_RWKV_HEADS, HEAD_DIM, HEAD_DIM), jnp.float32)
        xp, s_ctx = trunk_layer(xp, ctx_cond, s_zero, p)
        ctx_states.append(s_ctx.astype(state_rwkv.dtype))
        xs, _ = trunk_layer(xs, c, state_rwkv[:, l], p)
    new_state_rwkv = jnp.stack(ctx_states, axis=1)
    y_prompt = rms_norm(xp, final_norm_g)
    y_sample = rms_norm(xs, final_norm_g)
    return (y_prompt, y_sample, new_state_rwkv)


_drawn_inputs = setup_inputs


def setup_inputs(seed=0):
    import zlib

    import numpy as np

    out = dict(_drawn_inputs(seed))
    spreads = {}
    factors = {'state_rwkv': 8.0,
     'bonus_r_k': 6.8,
     'gn_g': 6.577,
     'gn_b': 37.31,
     'conv_dw_b': 6.013,
     'conv_ln_g': 6.195,
     'conv_ln_b': 27.342,
     'router_group_b': 39.233,
     'router_expert_b': 27.041,
     'norm2_g': 4.27}
    for name, (base, spread) in spreads.items():
        noise = np.random.default_rng([zlib.crc32(name.encode()), seed]).standard_normal(out[name].shape)
        drawn = base * np.exp(spread * noise) if base else spread * noise
        out[name] = __import__('jax').numpy.asarray(drawn.astype(out[name].dtype))
    for name, factor in factors.items():
        out[name] = (out[name] * factor).astype(out[name].dtype)
    return out
```

```python
from contextlib import ExitStack

import concourse.bass as bass
from concourse import mybir

F32 = mybir.dt.float32
I32 = mybir.dt.int32
U32 = mybir.dt.uint32
ALU = mybir.AluOpType
ACT = mybir.ActivationFunctionType
AX_X = mybir.AxisListType.X

P = 128
D = 1024
KD = D // P
TP, TS = 128, 512
T = TP + TS
TILES = T // P
DR = 512
PAIRS = DR // P
C = 64
LORA_COL = 3 * DR
IN_COLS = 2816
CONV_COL = LORA_COL + 256
CW = 31
NEXP, NGRP, EPG, DE = 32, 4, 8, 256
RMS_EPS, LN_EPS, GN_EPS = 1e-6, 1e-5, 64e-5
KAPPA = 0.6065306597126334

ZT = T + 3
ZP, ZS = 1, TP + 2
UT = T + 45
UP, US = 15, TP + 30
CT = T + 15

PAR_ROWS = [("mu", 26), ("w0", 8), ("a0", 8), ("kk", 8), ("ka", 8), ("rk", 8), ("gng", 4), ("gnb", 4),
            ("cb", 4), ("clg", 4), ("clb", 4), ("n1g", 8)]
PAR = {}
_at = 0
for _name, _n in PAR_ROWS:
    PAR[_name] = _at
    _at += _n
NPAR = _at

CONSTS = [("ident", 128), ("headones", 128), ("ones", 128), ("gmask", 128), ("scanmask", 512),
          ("eye16", 512), ("before", 128), ("expiota", 32), ("lanes", 8), ("ovi", 16)]
COFF = {}
_at = 0
for _name, _n in CONSTS:
    COFF[_name] = _at
    _at += _n
NCONST = _at


class Chain:

    def __init__(self, eng, sem):
        self.eng, self.sem, self.n = eng, sem, 0

    def __call__(self, ins):
        self.n += 1
        ins.then_inc(self.sem, 1)
        self.eng.wait_ge(self.sem, self.n)

    def announce(self, ins, sem, n):
        ins.then_inc(sem, 1)
        self.eng.wait_ge(sem, n)


def build(nc, ins, consts, pos, outs):
    ctx = ExitStack()
    with ctx:
        def sem(name):
            return ctx.enter_context(nc.semaphore(name))

        def dram(name, shape, dt=F32):
            return nc.dram_tensor(name, shape, dt, kind="Internal").ap()

        ARENA = 53200
        arena = ctx.enter_context(nc.sbuf_tensor("arena", [P, ARENA], F32))
        psum = [ctx.enter_context(nc.psum_tensor(f"bank{i}", [P, 512], F32)) for i in range(8)]

        def view(off, *shape):
            n = 1
            for s in shape:
                n *= s
            v = arena[:, off:off + n]
            if len(shape) == 2:
                v = v.rearrange("p (a b) -> p a b", b=shape[1])
            if len(shape) == 3:
                v = v.rearrange("p (a b c) -> p a b c", b=shape[1], c=shape[2])
            return v

        class Region:
            def __init__(self, start, end=ARENA):
                self.at, self.end = start, end

            def take(self, *shape):
                n = 1
                for s in shape:
                    n *= s
                off = self.at
                self.at += n
                assert self.at <= self.end, (self.at, self.end)
                return view(off, *shape)

        keep = Region(0)
        cst = keep.take(NCONST)
        par = keep.take(NPAR)
        convw = keep.take(CW * 4)
        oneminus = keep.take(34)
        condT = keep.take(16)
        modcol = keep.take(2, 16)
        small = keep.take(32)
        lorab = keep.take(2, DR)
        gateb = keep.take(DR)

        def const(name):
            return cst[:, COFF[name]:COFF[name] + dict(CONSTS)[name]]

        ident, headones, ones = const("ident"), const("headones"), const("ones")
        n1g = par[:, PAR["n1g"]:PAR["n1g"] + 8]

        regz = Region(keep.at)
        zbase = regz.at
        zrkv = regz.take(3 * PAIRS, ZT)
        zlora = regz.take(ZT)
        xlora = regz.take(2, T)
        gsig = regz.take(T)
        ysum = regz.take(PAIRS, T)
        wbase = regz.at

        regw = Region(wbase)
        w_in = regw.take(KD, IN_COLS)
        hT = regw.take(KD, T)
        modblk = regw.take(3, 512)
        adab = regw.take(3, 512)
        rows = regw.take(3, P)
        parrow, convrow, crow = rows[:, 0, :], rows[:, 1, :], rows[:, 2, :]
        convbuf = regw.take(2, T)
        rega = Region(zbase, wbase)
        adaw = rega.take(2, KD * 512)
        xt = rega.take(2, D)
        post = rega.take(D)
        sqr = rega.take(D)

        modrows = dram("modrows", [2, 6 * D])
        uconv = dram("uconv", [4, P, T])

        s_const, s_rows, s_lora = sem("constants_landed"), sem("rows_landed"), sem("lora_landed")
        s_adaw = [sem(f"ada_block_landed{b}") for b in range(2)]
        s_adab = [sem(f"ada_bias_landed{b}") for b in range(3)]
        s_win = [sem(f"w_in_landed{b}") for b in range(6)]
        s_xt = [sem(f"tokens_landed{b}") for b in range(2)]
        s_pos = sem("positions_landed")
        s_modst = [sem(f"mod_block_stored{b}") for b in range(3)]
        s_ust = [sem(f"conv_input_stored{b}") for b in range(2)]
        d_self, a_self, g_self = sem("vector_step"), sem("scalar_step"), sem("pool_step")
        s_silu = sem("cond_silu_done")
        s_rowsT = sem("rows_transposed")
        s_condT = sem("cond_columns_ready")
        s_adamm = sem("ada_block_summed")
        s_modblk = sem("mod_block_ready")
        s_modT = sem("mod_columns_transposed")
        s_modcol = sem("mod_columns_ready")
        s_posadd, s_xstat = sem("position_added"), sem("square_sum_ready")
        s_var, s_std, s_xn = sem("variance_ready"), sem("deviation_ready"), sem("tokens_normed")
        s_xT = sem("tokens_transposed")
        s_hTa, s_hTd = sem("hT_low_ready"), sem("hT_high_ready")
        s_zmm = sem("z_tile_summed")
        s_zeva, s_zevd = sem("z_tile_taken_by_scalar"), sem("z_tile_taken_by_vector")
        s_pads = sem("pads_zeroed")
        block = ctx.enter_context(nc.Block())

        def tok_src(i):
            return ins["x_prompt"][0] if i == 0 else ins["x_sample"][0, (i - 1) * P:i * P, :]

        WIN_BLOCKS = [(1536, 1792), (0, 512), (512, 1024), (1024, 1536), (1792, 2304), (2304, 2816)]
        ZTILES = [("lora", 12, 0), ("gate", 13, 0)]
        ZTILES += [(("r", "k", "v")[m], 4 * m + j, 1 + m) for m in range(3) for j in range(4)]
        ZTILES += [(n, 14 + j + 4 * (n == "cb"), 5) for j in range(4) for n in ("cb", "ca")]
        HALF = T // 2

        def sp_front():
            sp = nc.sync
            sp.dma_start(cst, consts).then_inc(s_const, 16)
            sp.dma_start(crow[0:8, :], ins["c_ctx"].rearrange("(k p) -> k p", p=P)).then_inc(s_rows, 16)
            sp.dma_start(crow[8:16, :], ins["c"][0].rearrange("(k p) -> k p", p=P)).then_inc(s_rows, 16)

            def ada_block(n):
                if n >= 2:
                    sp.wait_ge(s_adamm, n - 1)
                sp.dma_start(adaw[:, n % 2].rearrange("p (k n) -> p k n", k=KD),
                             ins["ada_w"][0, :, n * 512:(n + 1) * 512].rearrange("(k p) n -> p k n", p=P)
                             ).then_inc(s_adaw[n % 2], 16)
                if n >= 3:
                    sp.wait_ge(s_modblk, n - 2)
                sp.dma_start(adab[0:2, n % 3],
                             ins["ada_b"][0:1, n * 512:(n + 1) * 512].broadcast_to([2, 512])
                             ).then_inc(s_adab[n % 3], 16)

            def token_tile(i):
                if i >= 2:
                    sp.wait_ge(s_xT, i - 1)
                sp.dma_start(xt[:, i % 2], tok_src(i)).then_inc(s_xt[i % 2], 16)
                if i >= 1:
                    if i >= 2:
                        sp.wait_ge(s_posadd, i - 1)
                    sp.dma_start(post, pos[(i - 1) * P:i * P, :]).then_inc(s_pos, 16)

            def win_block(b):
                lo, hi = WIN_BLOCKS[b]
                sp.dma_start(w_in[:, :, lo:hi], ins["w_in"][0, :, lo:hi].rearrange("(k p) n -> p k n", p=P)
                             ).then_inc(s_win[b], 16)

            ada_block(0)
            ada_block(1)
            token_tile(0)
            token_tile(1)
            win_block(0)
            ada_block(2)
            ada_block(3)
            win_block(1)
            ada_block(4)
            ada_block(5)
            for i in range(2, TILES):
                token_tile(i)
            win_block(2)
            for n in range(6, 12):
                ada_block(n)
                if n in (7, 9, 11):
                    win_block(3 + (n - 7) // 2)

        def act_front():
            act, chain = nc.scalar, Chain(nc.scalar, a_self)
            at = 0
            for name, src in [("tshift_mu", "o (a b) -> (o a) b"), ("decay_w0", "o (a b) -> (o a) b"),
                              ("iclr_a0", "o (a b) -> (o a) b"), ("key_k", "o (a b) -> (o a) b"),
                              ("key_a", "o (a b) -> (o a) b"), ("bonus_r_k", None), ("gn_g", 1), ("gn_b", 1),
                              ("conv_dw_b", 1), ("conv_ln_g", 1), ("conv_ln_b", 1), ("norm1_g", 1)]:
                a = ins[name][0]
                if name == "bonus_r_k":
                    a = a.rearrange("o (j h) d -> (o j) (h d)", h=2)
                elif src == 1:
                    a = a.rearrange("(a b) -> a b", b=P)
                else:
                    a = a.rearrange(src, b=P)
                act.dma_start(parrow[at:at + a.shape[0], :], a).then_inc(s_rows, 16)
                at += a.shape[0]
            assert at == NPAR
            act.dma_start(convrow[0:CW * 4, :], ins["conv_dw_w"][0].rearrange("t (j p) -> (t j) p", p=P)
                          ).then_inc(s_rows, 16)
            act.dma_start(lorab[0:64], ins["decay_lora_b"][0].rearrange("o l c -> l o c")).then_inc(s_lora, 16)
            act.dma_start(lorab[64:128], ins["iclr_lora_b"][0].rearrange("o l c -> l o c")).then_inc(s_lora, 16)
            act.dma_start(gateb, ins["gate_lora_b"][0]).then_inc(s_lora, 16)
            act.wait_ge(s_rows, ROWS_ALL)
            nc.scalar.activation(crow[0:16, :], crow[0:16, :], ACT.Silu).then_inc(s_silu, 1)
            for i in range(TILES):
                act.wait_ge(s_xt[i % 2], 16 * (i // 2 + 1))
                if i:
                    act.wait_ge(s_posadd, i)
                chain.announce(nc.scalar.activation(sqr, xt[:, i % 2], ACT.Square, accum_out=small[:, i:i + 1]),
                             s_xstat, i + 1)
                act.wait_ge(s_var, i + 1)
                nc.scalar.activation(small[:, 8 + i:9 + i], small[:, i:i + 1], ACT.Sqrt).then_inc(s_std, 1)
                act.wait_ge(s_xT, i + 1)
                act.wait_ge(s_modcol, 1)
                cond = int(i > 0)
                for k in range(4):
                    last = nc.scalar.activation(hT[:, k, i * P:(i + 1) * P], psum[6][:, k * P:(k + 1) * P],
                                                ACT.Identity, bias=modcol[:, 0, 2 * k + cond:2 * k + cond + 1],
                                                scale=modcol[:, 1, 2 * k + cond:2 * k + cond + 1])
                    if k < 3:
                        last.then_inc(a_self, 1)
                        chain.n += 1
                last.then_inc(s_hTa, 1)
            for n, (kind, tile, _) in enumerate(ZTILES):
                act.wait_ge(s_zmm, n + 1)
                lo = psum[2 * (n % 2)]
                hi = psum[2 * (n % 2) + 1]
                if kind == "gate":
                    chain(nc.scalar.activation(gsig[:, 0:HALF], lo[:, 0:HALF], ACT.Sigmoid))
                    nc.scalar.activation(gsig[:, HALF:T], hi[:, 0:HALF], ACT.Sigmoid).then_inc(s_zeva, 1)
                elif kind == "cb":
                    b = (n // 2) % 2
                    if n >= 18:
                        act.wait_ge(s_ust[b], 16 * ((n - 14) // 4))
                    chain(nc.scalar.activation(convbuf[:, b, 0:HALF], lo[:, 0:HALF], ACT.Sigmoid))
                    nc.scalar.activation(convbuf[:, b, HALF:T], hi[:, 0:HALF], ACT.Sigmoid).then_inc(s_zeva, 1)
                elif kind == "ca":
                    act.wait_ge(s_zevd, n + 1)
                    act.dma_start(uconv[tile - 14], convbuf[:, (n // 2) % 2, :]).then_inc(s_ust[(n // 2) % 2], 16)
                    act.sem_inc(s_zeva, 1)
                else:
                    dst = zlora if kind == "lora" else zrkv[:, tile, :]
                    chain(nc.scalar.activation(dst[:, ZP:ZP + TP], lo[:, 0:TP], ACT.Copy))
                    nc.scalar.activation(dst[:, ZS:ZS + HALF - TP], lo[:, TP:HALF], ACT.Copy).then_inc(s_zeva, 1)
            act.wait_ge(s_zeva, len(ZTILES))
            return chain

        ROWS_ALL = 16 * 15

        def dve_front():
            dve, chain = nc.vector, Chain(nc.vector, d_self)
            dve.wait_ge(s_rowsT, 1)
            chain.announce(nc.vector.tensor_copy(condT, psum[4][:, 0:16]), s_condT, 1)
            chain(nc.vector.tensor_copy(par, psum[2][:, 0:NPAR]))
            chain(nc.vector.tensor_copy(convw, psum[3][:, 0:CW * 4]))
            chain(nc.vector.tensor_scalar(oneminus[:, 0:26], par[:, 0:26], -1.0, 1.0, ALU.mult, ALU.add))
            chain(nc.vector.tensor_scalar(oneminus[:, 26:34], par[:, PAR["ka"]:PAR["ka"] + 8], -1.0, 1.0,
                                          ALU.mult, ALU.add))

            def mod_block(n):
                dve.wait_ge(s_adamm, n + 1)
                dve.wait_ge(s_adab[n % 3], 16 * (n // 3 + 1))
                if n >= 3:
                    dve.wait_ge(s_modst[n % 3], 16 * (n // 3))
                chain.announce(nc.vector.tensor_tensor(modblk[0:2, n % 3], psum[n % 2][0:2, :], adab[0:2, n % 3],
                                                     ALU.add), s_modblk, n + 1)

            for n in range(4):
                mod_block(n)
            dve.wait_ge(s_modT, 4)
            chain(nc.vector.tensor_copy(modcol[:, 0], psum[5][:, 0:16]))
            chain.announce(nc.vector.scalar_tensor_tensor(
                modcol[:, 1].rearrange("p (k c) -> p k c", c=2), psum[5][:, 16:32].rearrange("p (k c) -> p k c", c=2),
                1.0, n1g.unsqueeze(2).broadcast_to([P, 8, 2]), ALU.add, ALU.mult), s_modcol, 1)
            for i in range(TILES):
                x = xt[:, i % 2]
                if i:
                    dve.wait_ge(s_xt[i % 2], 16 * (i // 2 + 1))
                    dve.wait_ge(s_pos, 16 * i)
                    chain.announce(nc.vector.tensor_tensor(x, x, post, ALU.add), s_posadd, i)
                dve.wait_ge(s_xstat, i + 1)
                chain.announce(nc.vector.tensor_scalar(small[:, i:i + 1], small[:, i:i + 1], 1.0 / D, RMS_EPS,
                                                     ALU.mult, ALU.add), s_var, i + 1)
                dve.wait_ge(s_std, i + 1)
                chain(nc.vector.reciprocal(small[:, 16 + i:17 + i], small[:, 8 + i:9 + i]))
                chain.announce(nc.vector.tensor_scalar(x, x, small[:, 16 + i:17 + i], None, ALU.mult), s_xn, i + 1)
                dve.wait_ge(s_xT, i + 1)
                cond = int(i > 0)
                for k in range(4, 8):
                    last = nc.vector.tensor_scalar(hT[:, k, i * P:(i + 1) * P], psum[7][:, (k - 4) * P:(k - 3) * P],
                                                   modcol[:, 1, 2 * k + cond:2 * k + cond + 1],
                                                   modcol[:, 0, 2 * k + cond:2 * k + cond + 1], ALU.mult, ALU.add)
                    if k < 7:
                        chain(last)
                chain.announce(last, s_hTd, i + 1)
            for n in range(4, 12):
                mod_block(n)
            for z in [zrkv[:, j, :] for j in range(12)] + [zlora]:
                for c in (0, TP + 1, ZT - 1):
                    last = nc.vector.memset(z[:, c:c + 1], 0.0)
                    chain(last)
            for n, (kind, tile, _) in enumerate(ZTILES):
                dve.wait_ge(s_zmm, n + 1)
                lo, hi = psum[2 * (n % 2)], psum[2 * (n % 2) + 1]
                if kind in ("gate", "cb"):
                    dve.sem_inc(s_zevd, 1)
                elif kind == "ca":
                    dve.wait_ge(s_zeva, n)
                    u = convbuf[:, (n // 2) % 2]
                    chain(nc.vector.tensor_tensor(u[:, 0:HALF], u[:, 0:HALF], lo[:, 0:HALF], ALU.mult))
                    chain.announce(nc.vector.tensor_tensor(u[:, HALF:T], u[:, HALF:T], hi[:, 0:HALF], ALU.mult),
                                 s_zevd, n + 1)
                else:
                    dst = zlora if kind == "lora" else zrkv[:, tile, :]
                    chain.announce(nc.vector.tensor_copy(dst[:, ZS + HALF - TP:ZS + TS], hi[:, 0:HALF]),
                                 s_zevd, n + 1)
            return chain

        def pool_front():
            for n in range(12):
                nc.gpsimd.wait_ge(s_modblk, n + 1)
                nc.gpsimd.dma_start(modrows[:, n * 512:(n + 1) * 512], modblk[0:2, n % 3]).then_inc(s_modst[n % 3], 16)

        def pe_front():
            pe = nc.tensor
            pe.wait_ge(s_const, 16)
            pe.wait_ge(s_silu, 1)
            nc.tensor.transpose(psum[2][:, 0:NPAR], parrow[0:NPAR, :], ident[0:NPAR, 0:NPAR])
            nc.tensor.transpose(psum[3][:, 0:CW * 4], convrow[0:CW * 4, :], ident[0:CW * 4, 0:CW * 4])
            nc.tensor.transpose(psum[4][:, 0:16], crow[0:16, :], ident[0:16, 0:16]).then_inc(s_rowsT, 1)
            pe.wait_ge(s_condT, 1)

            def ada_block(n):
                pe.wait_ge(s_adaw[n % 2], 16 * (n // 2 + 1))
                if n >= 2:
                    pe.wait_ge(s_modblk, n - 1)
                w = adaw[:, n % 2].rearrange("p (k n) -> p k n", k=KD)
                for k in range(KD):
                    mm = nc.tensor.matmul(psum[n % 2][0:2, :], condT[:, k:16:8], w[:, k, :],
                                          start=(k == 0), stop=(k == KD - 1))
                mm.then_inc(s_adamm, 1)

            def mod_columns(n):
                pe.wait_ge(s_modblk, n + 1)
                for j in range(4):
                    at = 2 * (4 * n + j)
                    mm = nc.tensor.transpose(psum[5][:, at:at + 2], modblk[0:2, n % 3, j * P:(j + 1) * P],
                                             ident[0:2, 0:2])
                mm.then_inc(s_modT, 1)

            def transpose_tile(i):
                pe.wait_ge(s_xn, i + 1)
                if i:
                    pe.wait_ge(s_hTa, i)
                    pe.wait_ge(s_hTd, i)
                for k in range(KD):
                    mm = nc.tensor.transpose(psum[6 + k // 4][:, (k % 4) * P:(k % 4 + 1) * P],
                                             xt[:, i % 2, k * P:(k + 1) * P], ident)
                mm.then_inc(s_xT, 1)

            for n in range(4):
                ada_block(n)
                if n:
                    mod_columns(n - 1)
            mod_columns(3)
            ada_block(4)
            ada_block(5)
            for i in range(TILES):
                transpose_tile(i)
            for n in range(6, 12):
                ada_block(n)
            pe.wait_ge(s_hTa, TILES)
            pe.wait_ge(s_hTd, TILES)
            pe.wait_ge(s_modblk, 12)
            for n, (kind, tile, wb) in enumerate(ZTILES):
                for b in (wb, 4) if kind in ("ca", "cb") else (wb,):
                    pe.wait_ge(s_win[b], 16)
                if n >= 2:
                    pe.wait_ge(s_zeva, n - 1)
                    pe.wait_ge(s_zevd, n - 1)
                for half in range(2):
                    for k in range(KD):
                        mm = nc.tensor.matmul(psum[2 * (n % 2) + half][:, 0:HALF], w_in[:, k, tile * P:(tile + 1) * P],
                                              hT[:, k, half * HALF:(half + 1) * HALF],
                                              start=(k == 0), stop=(k == KD - 1))
                mm.then_inc(s_zmm, 1)

        GC = 16
        COLS = GC * C
        regr = Region(wbase)
        XR, XK, SG, AV, CS, T0 = (regr.take(COLS) for _ in range(6))
        E1 = regr.take(GC, C + 1)
        VP = regr.take(C + COLS)
        BK = regr.take(GC, 2 * C)
        EI = SG
        KN = CS
        UL = XR.rearrange("p (s t) -> p s t", t=32)
        WI = XK[:, 0:512].rearrange("p (s j) -> p s j", j=16)
        WTMP = XK[:, 512:1024].rearrange("p (s j) -> p s j", j=16)
        WB = T0.rearrange("p (n q j) -> p n q j", q=2, j=16)
        TA, Y1 = AV.rearrange("p (n t) -> p n t", t=32), CS.rearrange("p (n t) -> p n t", t=32)
        AR = [regr.take(GC, 2 * C) for _ in range(2)]
        BKT = [regr.take(GC, P) for _ in range(2)]
        SAV = [regr.take(GC, P) for _ in range(2)]
        GM = [regr.take(2 * GC, 2 * C) for _ in range(2)]
        PC = [regr.take(GC) for _ in range(2)]
        ST = regr.take(2, 8, C)
        SP_ = regr.take(8, C)
        S0 = regr.take(8, C)
        XS = regr.take(2 * 8 * C)
        SL = XS.rearrange("p (a b) -> p a b", b=P)
        uin = regr.take(2, UT)
        cacc, cprod = regr.take(CT), regr.take(CT)

        udiag = dram("udiag", [5, 64, 1024])
        winv = dram("winv", [5, 2, 64, 512])
        cout = dram("conv_out", [4, P, CT])

        UNITS = [[(d, j, ZS, TS, (j - j0) * TS) for j in (j0, j0 + 1)] for d in range(2) for j0 in (0, 2)]
        UNITS.append([(d, j, ZP, TP, (4 * d + j) * TP) for d in range(2) for j in range(4)])
        NU = len(UNITS)

        def steps(u):
            return 2 if u == NU - 1 else 8

        def step_at(u, i):
            return 8 * u + i

        def chunks(u, i):
            return list(range(i, GC, steps(u)))

        def pcol(name, d, j):
            c = PAR[name] + 4 * d + j
            return par[:, c:c + 1]

        def current(z, seg):
            d, _, off, n, _ = seg
            return z[:, off:off + n][:, ::-1] if d else z[:, off:off + n]

        def previous(z, seg):
            d, _, off, n, _ = seg
            return z[:, off + 1:off + 1 + n][:, ::-1] if d else z[:, off - 1:off - 1 + n]

        def halves(u):
            return [[s for s in UNITS[u] if s[4] // 512 == h] for h in range(2)]

        PREP = ["shift_r", "shift_k", "shift_v", "lora", "square", "scan", "norm", "exp", "kn", "kp", "ar", "bk",
                "gram0", "gram1", "invload", "bonus", "scale", "turn_bk", "turn_v", "mv",
                "inv0", "inv1", "inv2", "inv3", "inv4", "invstore", "merge"]
        SCHEDULE = [("init", 0, 0)] + [(name, 0, 0) for name in PREP]
        for _u in range(NU):
            todo = [(name, _u + 1, 0) for name in PREP] if _u + 1 < NU else []
            slots = 3 * steps(_u)
            done, slot = 0, 0
            for _i in range(steps(_u)):
                for ev in ("X", "T", "S"):
                    SCHEDULE.append((ev, _u, _i))
                    slot += 1
                    upto_ = len(todo) * slot // slots
                    SCHEDULE += todo[done:upto_]
                    done = upto_
                SCHEDULE.append(("Y", _u, _i))
        SCHEDULE.append(("final", NU - 1, 0))

        USES = [("lw0", 0), ("lw1", 1), ("la0", 2), ("la1", 3), ("n0", 0), ("n1", 1)]
        USES += [(f"g{q}", q % 4) for q in range(8)]
        USES += [("b0", 2), ("b1", 3)]
        USES += [(f"t{q}", q) for q in range(4)] + [(f"v{q}", q) for q in range(4)]
        USES += [(f"m{q}", q) for q in range(4)]
        USES += [("ta0", 0), ("ta1", 1), ("y0", 2), ("y1", 3), ("z0", 0), ("z1", 1)]
        BANK = dict(USES)
        PER_UNIT = [sum(b == x for _, b in USES) for x in range(4)]
        ORDER = {}
        _seen = [0] * 4
        for _n, _b in USES:
            ORDER[_n] = _seen[_b]
            _seen[_b] += 1

        def read_count(u, use):
            return u * PER_UNIT[BANK[use]] + ORDER[use] + 1

        s_read = [sem(f"prep_bank_read{b}") for b in range(4)]

        def wait_read(eng, u, use):
            eng.wait_ge(s_read[BANK[use]], read_count(u, use))

        def wait_free(pe, u, use):
            if read_count(u, use) > 1:
                pe.wait_ge(s_read[BANK[use]], read_count(u, use) - 1)

        s_summed = sem("prep_bank_filled")
        USE_AT = {n: k for k, (n, _) in enumerate(USES)}

        def wait_filled(eng, u, use):
            eng.wait_ge(s_summed, u * len(USES) + USE_AT[use] + 1)
        s_shiftA = sem("shift_scaled")
        s_shiftD = sem("shift_done")
        s_xlA, s_xlD, s_xl = sem("lora_shift_scaled"), sem("lora_shift_done"), sem("lora_input_ready")
        s_sq, s_cs, s_exp, s_rk = sem("squares_ready"), sem("log_decay_summed"), sem("decays_ready"), sem("rk_ready")
        s_ar, s_bk, s_bkh = sem("ar_ready"), sem("bk_ready"), sem("bk_scaled")
        s_ud, s_ul, s_wd, s_wb = sem("udiag_stored"), sem("udiag_loaded"), sem("winv_stored"), sem("winv_loaded")
        s_inv = sem("inverse_done")
        s_wcopy = sem("inverse_blocks_placed")
        s_sl, s_slT, s_s0 = sem("states_loaded"), sem("states_turned"), sem("initial_states_ready")
        s_X, s_XS, s_SA, s_SAS = sem("x_summed"), sem("x_taken"), sem("removals_summed"), sem("removals_taken")
        s_S, s_ST, s_Y, s_YS = sem("state_summed"), sem("state_ready"), sem("y_summed"), sem("y_added")
        s_fin, s_finc, s_finst = sem("final_states_turned"), sem("final_states_taken"), sem("final_states_stored")
        s_uin = [sem(f"conv_tile_loaded{b}") for b in range(2)]
        s_cacc, s_cst = sem("conv_tile_done"), sem("conv_tile_stored")

        NZ = len(ZTILES)

        def sp_mix():
            sp = nc.sync
            sp.wait_ge(s_zmm, NZ)
            sp.wait_ge(s_ust[0], 32)
            sp.wait_ge(s_ust[1], 32)
            for b in range(3):
                sp.wait_ge(s_modst[b], 64)
            for a in range(8):
                sp.dma_start(SL[0:64, a].rearrange("v (h k) -> v h k", h=2),
                             ins["state_rwkv"][0, 0, a // 4, 2 * (a % 4):2 * (a % 4) + 2].rearrange("h v k -> v h k")
                             ).then_inc(s_sl, 16)
            for ev, u, i in SCHEDULE:
                if ev == "gram1":
                    wait_read(sp, u, "g7")
                    for r in range(3):
                        wait_read(sp, u, f"g{4 + r}")
                    for b in range(2):
                        sp.dma_start(udiag[u, 32 * b:32 * b + 32].rearrange("n (s t) -> s n t", t=32),
                                     GM[u % 2][32 * b:32 * b + 32, :, 32 * b:32 * b + 32]).then_inc(s_ud, 16)
                elif ev == "bonus":
                    sp.wait_ge(s_ud, 32 * (u + 1))
                    sp.wait_ge(s_rk, u + 1)
                    sp.wait_ge(s_ar, u + 1)
                    for q in range(2):
                        sp.dma_start(UL[64 * q:64 * q + 64].rearrange("p s t -> p (s t)"), udiag[u]
                                     ).then_inc(s_ul, 16)
                elif ev == "invstore":
                    sp.wait_ge(s_inv, u + 1)
                    sp.dma_start(winv[u].rearrange("q n f -> (q n) f"), WI.rearrange("p s j -> p (s j)")
                                 ).then_inc(s_wd, 16)
                    sp.wait_ge(s_wd, 16 * (u + 1))
                    for r in (0, 1):
                        wait_read(sp, u, f"b{r}")
                    for b in range(2):
                        for q in range(2):
                            sp.dma_start(WB[32 * b:32 * b + 32, :, q, :],
                                         winv[u, q, 32 * b:32 * b + 32].rearrange("n (s j) -> s n j", j=16)
                                         ).then_inc(s_wb, 16)
                elif ev == "final":
                    sp.wait_ge(s_finc, 1)
                    for a in range(8):
                        sp.dma_start(outs["new_state"][0, 0, a // 4, 2 * (a % 4):2 * (a % 4) + 2]
                                     .rearrange("h v k -> v h k"),
                                     SL[0:64, a].rearrange("v (h k) -> v h k", h=2)).then_inc(s_finst, 16)

        def act_mix(chain):
            act = nc.scalar
            act.wait_ge(s_zevd, NZ)
            for d in range(2):
                for n, (off, ln, at) in enumerate([(ZP, TP, 0), (ZS, TS, TP)]):
                    seg = (d, 0, off, ln, 0)
                    c = PAR["mu"] + 13 * d + 12
                    chain.announce(nc.scalar.activation(xlora[:, d, at:at + ln], previous(zlora, seg), ACT.Copy,
                                                      scale=par[:, c:c + 1]), s_xlA, 2 * d + n + 1)
            act.wait_ge(s_xlD, 4)
            for d in range(2):
                chain.announce(nc.scalar.activation(xlora[0:64, d], xlora[0:64, d], ACT.Tanh), s_xl, d + 1)
            act.wait_ge(s_zmm, NZ)
            for ev, u, i in SCHEDULE:
                b = u % 2
                segs = UNITS[u]
                if ev in ("shift_r", "shift_k", "shift_v"):
                    m = ("shift_r", "shift_k", "shift_v").index(ev)
                    if m == 0 and u:
                        wait_read(act, u - 1, "z0")
                        wait_read(act, u - 1, "z1")
                    X = (XR, XK, VP[:, C:])[m]
                    for n, s in enumerate(segs):
                        c = PAR["mu"] + 13 * s[0] + 4 * m + s[1]
                        ins_ = nc.scalar.activation(X[:, s[4]:s[4] + s[3]], previous(zrkv[:, 4 * m + s[1], :], s),
                                                    ACT.Copy, scale=par[:, c:c + 1])
                        if n < len(segs) - 1:
                            chain(ins_)
                    chain.announce(ins_, s_shiftA, 3 * u + m + 1)
                elif ev == "lora":
                    for name, dst, bias in (("lw", SG, "w0"), ("la", AV, "a0")):
                        for h, part in enumerate(halves(u)):
                            wait_filled(act, u, f"{name}{h}")
                            for s in part:
                                ins_ = nc.scalar.activation(
                                    dst[:, s[4]:s[4] + s[3]], psum[BANK[f"{name}{h}"]][:, s[4] % 512:s[4] % 512 + s[3]],
                                    ACT.Sigmoid, bias=pcol(bias, s[0], s[1]))
                                if s is not part[-1]:
                                    chain(ins_)
                            chain.announce(ins_, s_read[BANK[f"{name}{h}"]], read_count(u, f"{name}{h}"))
                elif ev == "square":
                    act.wait_ge(s_shiftD, 3 * u + 2)
                    if u:
                        act.wait_ge(s_wcopy, 2 * u)
                    for n, s in enumerate(segs):
                        ins_ = nc.scalar.activation(T0[:, s[4]:s[4] + s[3]], XK[:, s[4]:s[4] + s[3]], ACT.Square,
                                                    scale=pcol("kk", s[0], s[1]))
                        if n < len(segs) - 1:
                            chain(ins_)
                    chain.announce(ins_, s_sq, u + 1)
                elif ev == "norm":
                    for h in range(2):
                        wait_filled(act, u, f"n{h}")
                        chain.announce(nc.scalar.activation(T0[:, 512 * h:512 * h + 512], psum[BANK[f"n{h}"]][:, :],
                                                          ACT.Sqrt), s_read[BANK[f"n{h}"]], read_count(u, f"n{h}"))
                elif ev == "exp":
                    act.wait_ge(s_cs, u + 1)
                    cs = CS.rearrange("p (g c) -> p g c", c=C)
                    if u == 0:
                        act.wait_ge(s_pads, 1)
                    chain.announce(nc.scalar.activation(E1[:, :, 1:C + 1], cs, ACT.Exp, scale=-KAPPA), s_exp, 2 * u + 1)
                    chain.announce(nc.scalar.activation(EI, CS, ACT.Exp, scale=KAPPA), s_exp, 2 * u + 2)
                elif ev in ("turn_bk", "turn_v"):
                    name = "t" if ev == "turn_bk" else "v"
                    for q in range(4):
                        wait_filled(act, u, f"{name}{q}")
                        src = psum[BANK[f"{name}{q}"]][:, :].rearrange("p (g c) -> p g c", c=P)
                        if name == "t":
                            ins_ = nc.scalar.activation(BKT[b][:, 4 * q:4 * q + 4, :], src, ACT.Copy)
                        else:
                            ins_ = nc.scalar.activation(SAV[b][64:128, 4 * q:4 * q + 4, :], src[64:128], ACT.Copy)
                        chain.announce(ins_, s_read[BANK[f"{name}{q}"]], read_count(u, f"{name}{q}"))
                elif ev == "merge":
                    act.wait_ge(s_wb, 64 * (u + 1))
                    for k in range(2):
                        r = slice(32 * k, 32 * k + 32)
                        chain.announce(nc.scalar.activation(
                            GM[b][r, :, 32 * k:32 * k + 32].rearrange("p n (j q) -> p n j q", q=2),
                            WB[r].rearrange("p n q j -> p n j q"), ACT.Copy), s_wcopy, 2 * u + k + 1)
                    for h in range(2):
                        wait_filled(act, u, f"ta{h}")
                        chain.announce(nc.scalar.activation(
                            TA[0:32, 16 * h:16 * h + 16, :],
                            psum[BANK[f"ta{h}"]][0:32, :].rearrange("p (n t) -> p n t", t=32), ACT.Copy),
                            s_read[BANK[f"ta{h}"]], read_count(u, f"ta{h}"))
                elif ev == "mv":
                    for q in range(4):
                        wait_filled(act, u, f"m{q}")
                        h, g0 = q // 2, 8 * (q % 2)
                        chain.announce(nc.scalar.activation(
                            SAV[b][0:64, g0:g0 + 8, C * h:C * h + C],
                            psum[BANK[f"m{q}"]][0:64, :].rearrange("p (n c) -> p n c", c=C), ACT.Copy),
                            s_read[BANK[f"m{q}"]], read_count(u, f"m{q}"))
                elif ev == "T":
                    g, n = step_at(u, i), len(chunks(u, i))
                    act.wait_ge(s_SA, g + 1)
                    for h in range(2):
                        ins_ = nc.scalar.activation(SAV[b][0:64, i::steps(u), C * h:C * h + C],
                                                    psum[6 + h][0:64, 0:n * C].rearrange("p (n c) -> p n c", c=C),
                                                    ACT.Copy)
                        if h == 0:
                            chain(ins_)
                    chain.announce(ins_, s_SAS, g + 1)
                elif ev == "final":
                    act.wait_ge(s_fin, 1)
                    chain(nc.scalar.activation(SL[0:64, 0:4], psum[6][0:64, :].rearrange("p (a b) -> p a b", b=P),
                                               ACT.Copy))
                    chain.announce(nc.scalar.activation(SL[0:64, 4:8], psum[7][0:64, :].rearrange("p (a b) -> p a b", b=P),
                                                      ACT.Copy), s_finc, 1)

        def dve_mix(chain):
            dve = nc.vector
            for k, (d, off, ln, at) in enumerate([(d, *x) for d in range(2) for x in ((ZP, TP, 0), (ZS, TS, TP))]):
                dve.wait_ge(s_zeva, 1)
                dve.wait_ge(s_xlA, k + 1)
                x = xlora[:, d, at:at + ln]
                c = 13 * d + 12
                chain.announce(nc.vector.scalar_tensor_tensor(x, current(zlora, (d, 0, off, ln, 0)), oneminus[:, c:c + 1],
                                                            x, ALU.mult, ALU.add), s_xlD, k + 1)
            dve.wait_ge(s_zmm, NZ)
            dve.wait_ge(s_ust[0], 32)
            dve.wait_ge(s_ust[1], 32)
            chain(nc.vector.memset(VP[:, 0:C], 0.0))
            chain.announce(nc.vector.memset(E1[:, :, 0:1], 1.0), s_pads, 1)
            for ev, u, i in SCHEDULE:
                b = u % 2
                segs = UNITS[u]
                if ev == "init":
                    dve.wait_ge(s_slT, 1)
                    chain.announce(nc.vector.tensor_copy(S0, psum[5][:, :].rearrange("p (a b) -> p a b", b=C)), s_s0, 1)
                elif ev in ("shift_r", "shift_k", "shift_v"):
                    m = ("shift_r", "shift_k", "shift_v").index(ev)
                    X = (XR, XK, VP[:, C:])[m]
                    dve.wait_ge(s_shiftA, 3 * u + m + 1)
                    for n, s in enumerate(segs):
                        c = 13 * s[0] + 4 * m + s[1]
                        x = X[:, s[4]:s[4] + s[3]]
                        ins_ = nc.vector.scalar_tensor_tensor(x, current(zrkv[:, 4 * m + s[1], :], s),
                                                              oneminus[:, c:c + 1], x, ALU.mult, ALU.add)
                        if n < len(segs) - 1:
                            chain(ins_)
                    chain.announce(ins_, s_shiftD, 3 * u + m + 1)
                elif ev == "scan":
                    for h in range(2):
                        wait_read(dve, u, f"lw{h}")
                        ins_ = nc.vector.tensor_tensor_scan(CS[:, 512 * h:512 * h + 512], const("scanmask"),
                                                            SG[:, 512 * h:512 * h + 512], 0.0, ALU.mult, ALU.add)
                        if h == 0:
                            chain(ins_)
                    chain.announce(ins_, s_cs, u + 1)
                elif ev == "kn":
                    for h in range(2):
                        wait_read(dve, u, f"n{h}")
                    chain(nc.vector.tensor_scalar(T0, T0, 1e-12, None, ALU.max))
                    chain(nc.vector.reciprocal(T0, T0))
                    dve.wait_ge(s_exp, 2 * u + 2)
                    for s in segs:
                        c = slice(s[4], s[4] + s[3])
                        chain(nc.vector.scalar_tensor_tensor(KN[:, c], XK[:, c], pcol("kk", s[0], s[1]), T0[:, c],
                                                             ALU.mult, ALU.mult))
                elif ev == "kp":
                    for h in range(2):
                        wait_read(dve, u, f"la{h}")
                    for s in segs:
                        c = slice(s[4], s[4] + s[3])
                        o = 26 + 4 * s[0] + s[1]
                        chain(nc.vector.tensor_scalar(T0[:, c], AV[:, c], pcol("ka", s[0], s[1]),
                                                      oneminus[:, o:o + 1], ALU.mult, ALU.add))
                    chain(nc.vector.tensor_tensor(XK, XK, T0, ALU.mult))
                    chain(nc.vector.tensor_tensor(AV, AV, KN, ALU.mult))
                elif ev == "ar":
                    def gc(x):
                        return x.rearrange("p (g c) -> p g c", c=C)
                    chain(nc.vector.scalar_tensor_tensor(AR[b][:, :, 0:C], gc(KN), -1.0, E1[:, :, 0:C],
                                                         ALU.mult, ALU.mult))
                    chain(nc.vector.tensor_copy(PC[b].unsqueeze(2), E1[:, :, C:C + 1]))
                    chain.announce(nc.vector.tensor_tensor(AR[b][:, :, C:2 * C], gc(XR), E1[:, :, 1:C + 1], ALU.mult),
                                 s_ar, u + 1)
                elif ev == "bk":
                    chain(nc.vector.tensor_tensor(BK[:, :, 0:C], gc(AV), gc(EI), ALU.mult))
                    chain.announce(nc.vector.tensor_tensor(BK[:, :, C:2 * C], gc(XK), gc(EI), ALU.mult), s_bk, u + 1)
                    for n, s in enumerate(segs):
                        c = slice(s[4], s[4] + s[3])
                        ins_ = nc.vector.scalar_tensor_tensor(T0[:, c], XR[:, c], pcol("rk", s[0], s[1]), XK[:, c],
                                                              ALU.mult, ALU.mult)
                        if n < len(segs) - 1:
                            chain(ins_)
                    chain.announce(ins_, s_rk, u + 1)
                elif ev in ("gram0", "gram1"):
                    for q in range(4 * (ev == "gram1"), 4 * (ev == "gram1") + 4):
                        wait_filled(dve, u, f"g{q}")
                        chain.announce(nc.vector.tensor_tensor(
                            GM[b][:, GC * (q % 2) + 4 * (q // 2):GC * (q % 2) + 4 * (q // 2) + 4, :], psum[BANK[f"g{q}"]][:, :].rearrange("p (n c) -> p n c", c=P),
                            const("gmask").unsqueeze(1).broadcast_to([P, 4, P]), ALU.mult),
                            s_read[BANK[f"g{q}"]], read_count(u, f"g{q}"))
                elif ev == "bonus":
                    for h, part in enumerate(halves(u)):
                        wait_filled(dve, u, f"b{h}")
                        todo_ = []
                        for s in part:
                            d, j, off, n, c0 = s
                            v = VP[:, C + c0:C + c0 + n]
                            sums = psum[BANK[f"b{h}"]][:, c0 % 512:c0 % 512 + n]
                            t0 = 0 if off == ZP else TP
                            y = ysum[:, j, t0:t0 + n]
                            if d == 0:
                                ins_ = nc.vector.tensor_tensor(y, sums, v, ALU.mult)
                            else:
                                ins_ = nc.vector.tensor_tensor(T0[:, c0:c0 + n], sums, v, ALU.mult)
                                todo_.append((y[:, ::-1], T0[:, c0:c0 + n]))
                            if s is not part[-1]:
                                chain(ins_)
                            elif not todo_:
                                chain.announce(ins_, s_read[BANK[f"b{h}"]], read_count(u, f"b{h}"))
                            else:
                                chain(ins_)
                        for n, (y, t) in enumerate(todo_):
                            ins_ = nc.vector.tensor_tensor(y, y, t, ALU.add)
                            if n < len(todo_) - 1:
                                chain(ins_)
                            else:
                                chain.announce(ins_, s_read[BANK[f"b{h}"]], read_count(u, f"b{h}"))
                elif ev.startswith("inv") and ev[3:].isdigit():
                    part = int(ev[3:])
                    if part == 0:
                        dve.wait_ge(s_ul, 32 * (u + 1))
                        chain(nc.vector.tensor_copy(WI, const("eye16").rearrange("p (s j) -> p s j", j=16)))
                    cuts = [31, 26, 20, 14, 7, 0]
                    for t in range(cuts[part], cuts[part + 1], -1):
                        j0 = t // 2
                        w = [P, t, 16 - j0]
                        tmp = WTMP[:, 0:t, j0:16]
                        chain(nc.vector.tensor_tensor(tmp, UL[:, 0:t, t:t + 1].broadcast_to(w),
                                                      WI[:, t:t + 1, j0:16].broadcast_to(w), ALU.mult))
                        ins_ = nc.vector.tensor_tensor(WI[:, 0:t, j0:16], WI[:, 0:t, j0:16], tmp, ALU.add)
                        if t > 1:
                            chain(ins_)
                        else:
                            chain.announce(ins_, s_inv, u + 1)
                elif ev == "merge":
                    for h in range(2):
                        wait_filled(dve, u, f"y{h}")
                        chain.announce(nc.vector.tensor_copy(
                            Y1[32:64, 16 * h:16 * h + 16, :],
                            psum[BANK[f"y{h}"]][32:64, :].rearrange("p (n t) -> p n t", t=32)),
                            s_read[BANK[f"y{h}"]], read_count(u, f"y{h}"))
                    for h in range(2):
                        wait_filled(dve, u, f"z{h}")
                        chain.announce(nc.vector.tensor_copy(
                            GM[b][0:32, 16 * h:16 * h + 16, 32:64],
                            psum[BANK[f"z{h}"]][0:32, :].rearrange("p (n t) -> p n t", t=32)),
                            s_read[BANK[f"z{h}"]], read_count(u, f"z{h}"))
                elif ev == "X":
                    g, n = step_at(u, i), len(chunks(u, i))
                    if i == 0:
                        if u == NU - 1:
                            ins_ = nc.vector.memset(ST[:, 0, 0:n], 0.0)
                        else:
                            ins_ = nc.vector.tensor_copy(ST[:, 0, 0:n], S0[:, 2 * u:2 * u + 2])
                        chain.announce(ins_, s_ST, g + u + 1)
                    dve.wait_ge(s_X, g + 1)
                    for h in range(2):
                        ins_ = nc.vector.tensor_tensor(
                            XS[0:64, 8 * C * h:8 * C * h + n * C].rearrange("p (n c) -> p n c", c=C),
                            psum[6 + h][0:64, 0:n * C].rearrange("p (n c) -> p n c", c=C),
                            SAV[b][0:64, i::steps(u), C * h:C * h + C], ALU.add)
                        if h == 0:
                            chain(ins_)
                    chain.announce(ins_, s_XS, g + 1)
                elif ev == "T":
                    n = len(chunks(u, i))
                    pc = PC[b][:, i::steps(u)].unsqueeze(2).broadcast_to([P, n, C])
                    chain(nc.vector.tensor_tensor(SP_[:, 0:n], ST[:, i % 2, 0:n], pc, ALU.mult))
                elif ev == "S":
                    g, n = step_at(u, i), len(chunks(u, i))
                    dve.wait_ge(s_S, g + 1)
                    if g:
                        dve.wait_ge(s_Y, g)
                    chain.announce(nc.vector.tensor_tensor(
                        ST[:, (i + 1) % 2, 0:n], psum[5][:, 0:n * C].rearrange("p (n c) -> p n c", c=C), SP_[:, 0:n],
                        ALU.add), s_ST, g + u + 2)
                elif ev == "Y":
                    g, n = step_at(u, i), len(chunks(u, i))
                    dve.wait_ge(s_Y, g + 1)
                    y = psum[4][:, 0:n * C].rearrange("p (n c) -> p n c", c=C)
                    if u == NU - 1:
                        a = ysum[:, :, i * C:(i + 1) * C]
                        chain(nc.vector.tensor_tensor(a, a, y[:, 0:4], ALU.add))
                        a = ysum[:, :, TP - (i + 1) * C:TP - i * C][:, :, ::-1]
                        ins_ = nc.vector.tensor_tensor(a, a, y[:, 4:8], ALU.add)
                    else:
                        d, j = segs[0][0], segs[0][1]
                        a = ysum[:, j:j + 2, TP + i * C:TP + (i + 1) * C]
                        if d:
                            a = ysum[:, j:j + 2, T - (i + 1) * C:T - i * C][:, :, ::-1]
                        ins_ = nc.vector.tensor_tensor(a, a, y, ALU.add)
                    chain.announce(ins_, s_YS, g + 1)

        def pool_mix(chain):
            pool = nc.gpsimd
            pool.wait_ge(s_zmm, NZ)
            for s in s_ust:
                pool.wait_ge(s, 32)
            for x in range(2):
                for lo in (0, UP + TP, US + TS):
                    chain(nc.gpsimd.memset(uin[:, x, lo:lo + 15], 0.0))

            def load_tile(j):
                pool.dma_start(uin[:, j % 2, UP:UP + TP], uconv[j][:, 0:TP]).then_inc(s_uin[j % 2], 16)
                pool.dma_start(uin[:, j % 2, US:US + TS], uconv[j][:, TP:T]).then_inc(s_uin[j % 2], 16)

            load_tile(0)
            load_tile(1)

            def tap(j, k):
                if k == 0:
                    pool.wait_ge(s_uin[j % 2], 32 * (j // 2 + 1))
                    if j:
                        pool.wait_ge(s_cst, 16 * j)
                u_, w = uin[:, j % 2, k:k + CT], convw[:, 4 * k + j:4 * k + j + 1]
                if k == 0:
                    chain(nc.gpsimd.tensor_scalar(cacc, u_, w, par[:, PAR["cb"] + j:PAR["cb"] + j + 1],
                                                  ALU.mult, ALU.add))
                    return
                chain(nc.gpsimd.tensor_scalar(cprod, u_, w, None, ALU.mult))
                ins_ = nc.gpsimd.tensor_tensor(cacc, cacc, cprod, ALU.add)
                if k < CW - 1:
                    chain(ins_)
                    return
                chain.announce(ins_, s_cacc, j + 1)
                pool.dma_start(cout[j], cacc).then_inc(s_cst, 16)
                if j + 2 < 4:
                    load_tile(j + 2)

            total, taps = len(SCHEDULE), [(j, k) for j in range(4) for k in range(CW)]
            done = 0
            for n, (ev, u, i) in enumerate(SCHEDULE):
                if ev == "scale":
                    b = u % 2
                    wait_filled(pool, u, "g7")
                    pool.wait_ge(s_bk, u + 1)
                    chain.announce(nc.gpsimd.tensor_tensor(BK, BK, PC[b].unsqueeze(2).broadcast_to([P, GC, 2 * C]),
                                                         ALU.mult), s_bkh, u + 1)
                want = len(taps) * (n + 1) // total
                for j, k in taps[done:want]:
                    tap(j, k)
                done = want

        def pe_mix():
            pe = nc.tensor
            for ev, u, i in SCHEDULE:
                b = u % 2
                segs = UNITS[u]
                if ev == "init":
                    pe.wait_ge(s_sl, 16 * 8)
                    for a in range(8):
                        mm = nc.tensor.transpose(psum[5][:, a * C:(a + 1) * C], SL[0:64, a], ident[0:64, 0:64])
                    mm.then_inc(s_slT, 1)
                elif ev == "lora":
                    pe.wait_ge(s_xl, 2)
                    pe.wait_ge(s_lora, 48)
                    if u == 0:
                        pe.wait_ge(s_zeva, NZ)
                        pe.wait_ge(s_zevd, NZ)
                    for name, r in (("lw", slice(0, 64)), ("la", slice(64, 128))):
                        for h, part in enumerate(halves(u)):
                            wait_free(pe, u, f"{name}{h}")
                            for d, j, off, n, c0 in part:
                                t0 = 0 if off == ZP else TP
                                mm = nc.tensor.matmul(psum[BANK[f"{name}{h}"]][:, c0 % 512:c0 % 512 + n],
                                                      lorab[r, d, j * P:(j + 1) * P], xlora[r, d, t0:t0 + n],
                                                      start=True, stop=True)
                            mm.then_inc(s_summed, 1)
                elif ev in ("norm", "bonus"):
                    name = ev[0]
                    pe.wait_ge(s_sq if name == "n" else s_rk, u + 1)
                    for h in range(2):
                        wait_free(pe, u, f"{name}{h}")
                        nc.tensor.matmul(psum[BANK[f"{name}{h}"]][:, :], headones, T0[:, 512 * h:512 * h + 512],
                                         start=True, stop=True).then_inc(s_summed, 1)
                elif ev in ("gram0", "gram1"):
                    pe.wait_ge(s_ar, u + 1)
                    pe.wait_ge(s_bk, u + 1)
                    for q in range(4 * (ev == "gram1"), 4 * (ev == "gram1") + 4, 2):
                        wait_free(pe, u, f"g{q}")
                        wait_free(pe, u, f"g{q + 1}")
                        for n in range(4):
                            gc_ = 2 * q + n
                            for h in range(2):
                                r = slice(64 * h, 64 * h + 64)
                                mm = nc.tensor.matmul(psum[BANK[f"g{q + h}"]][:, n * P:(n + 1) * P], BK[r, gc_, :],
                                                      AR[b][r, gc_, :], start=True, stop=True)
                                if n == 3:
                                    mm.then_inc(s_summed, 1)
                elif ev in ("turn_bk", "turn_v"):
                    name = "t" if ev == "turn_bk" else "v"
                    pe.wait_ge(s_bkh if name == "t" else s_shiftD, (u + 1) * (1 if name == "t" else 3))
                    for q in range(4):
                        wait_free(pe, u, f"{name}{q}")
                        for n in range(4):
                            g_ = 4 * q + n
                            src = BK[:, g_, :] if name == "t" else VP[:, g_ * C:g_ * C + P]
                            mm = nc.tensor.transpose(psum[BANK[f"{name}{q}"]][:, n * P:(n + 1) * P], src, ident)
                        mm.then_inc(s_summed, 1)
                elif ev == "mv":
                    for q in range(4):
                        wait_read(pe, u, f"v{q}")
                    for q in range(4):
                        wait_free(pe, u, f"m{q}")
                        for n in range(8):
                            gc_, h = 8 * (q % 2) + n, q // 2
                            mm = nc.tensor.matmul(psum[BANK[f"m{q}"]][0:64, n * C:(n + 1) * C],
                                                  GM[b][64:128, GC * h + gc_, 0:C],
                                                  SAV[b][64:128, gc_, C * h:C * h + C], start=True, stop=True)
                        mm.then_inc(s_summed, 1)
                elif ev == "merge":
                    pe.wait_ge(s_wcopy, 2 * (u + 1))
                    lo, hi = slice(0, 32), slice(32, 64)
                    for name in ("ta", "y", "z"):
                        for h in range(2):
                            wait_free(pe, u, f"{name}{h}")
                            if name == "y":
                                wait_read(pe, u, f"ta{h}")
                            if name == "z":
                                wait_read(pe, u, f"y{h}")
                            for n in range(16):
                                p_ = 16 * h + n
                                c = slice(32 * n, 32 * n + 32)
                                bank = psum[BANK[f"{name}{h}"]]
                                if name == "ta":
                                    mm = nc.tensor.matmul(bank[lo, c], GM[b][lo, p_, 0:32], ident[lo, 0:32],
                                                          start=True, stop=True)
                                elif name == "y":
                                    mm = nc.tensor.matmul(bank[hi, c], GM[b][lo, p_, 32:64], TA[lo, p_, :],
                                                          start=True, stop=True)
                                else:
                                    mm = nc.tensor.matmul(bank[lo, c], Y1[hi, p_, :], GM[b][hi, p_, 32:64],
                                                          start=True, stop=True)
                            mm.then_inc(s_summed, 1)
                elif ev == "X":
                    g = step_at(u, i)
                    pe.wait_ge(s_ST, g + u + 1)
                    if i == 0:
                        for use in ("z0", "z1", "m2", "m3"):
                            wait_read(pe, u, use)
                    if g:
                        pe.wait_ge(s_SAS, g)
                    for k, gc_ in enumerate(chunks(u, i)):
                        for h in range(2):
                            r = slice(64 * h, 64 * h + 64)
                            mm = nc.tensor.matmul(psum[6 + h][0:64, k * C:(k + 1) * C], AR[b][r, gc_, 0:C],
                                                  ST[r, i % 2, k, :], start=True, stop=True)
                    mm.then_inc(s_X, 1)
                elif ev == "T":
                    g = step_at(u, i)
                    pe.wait_ge(s_XS, g + 1)
                    for k, gc_ in enumerate(chunks(u, i)):
                        for h in range(2):
                            at = 8 * C * h + C * k
                            mm = nc.tensor.matmul(psum[6 + h][0:64, k * C:(k + 1) * C], GM[b][0:64, GC * h + gc_, 0:C],
                                                  XS[0:64, at:at + C], start=True, stop=True)
                    mm.then_inc(s_SA, 1)
                elif ev == "S":
                    g = step_at(u, i)
                    pe.wait_ge(s_SAS, g + 1)
                    for k, gc_ in enumerate(chunks(u, i)):
                        for h in range(2):
                            hc = slice(C * h, C * h + C)
                            mm = nc.tensor.matmul(psum[5][64 * h:64 * h + 64, k * C:(k + 1) * C],
                                                  BKT[b][:, gc_, hc], SAV[b][:, gc_, hc], start=True, stop=True)
                    mm.then_inc(s_S, 1)
                elif ev == "Y":
                    g = step_at(u, i)
                    if g:
                        pe.wait_ge(s_YS, g)
                    for part in range(2):
                        for k, gc_ in enumerate(chunks(u, i)):
                            for h in range(2):
                                r = slice(64 * h, 64 * h + 64)
                                out = psum[4][r, k * C:(k + 1) * C]
                                if part == 0:
                                    nc.tensor.matmul(out, SAV[b][:, gc_, C * h:C * h + C],
                                                     GM[b][:, GC * h + gc_, C:2 * C],
                                                     start=(k == 0), stop=False, skip_group_check=True)
                                else:
                                    mm = nc.tensor.matmul(out, ST[r, i % 2, k, :], AR[b][r, gc_, C:2 * C],
                                                          start=False, stop=True, skip_group_check=True)
                    mm.then_inc(s_Y, 1)
                elif ev == "final":
                    pe.wait_ge(s_ST, step_at(u, 1) + u + 2)
                    for a in range(8):
                        mm = nc.tensor.transpose(psum[6 + a // 4][0:64, (a % 4) * P:(a % 4 + 1) * P],
                                                 ST[:, 0, a, :], ident)
                    mm.then_inc(s_fin, 1)
        EXPERT = 3 * 2048
        NB = 5
        ebuf = [ARENA - (n + 1) * EXPERT for n in range(NB)]
        regp = Region(wbase, ebuf[NB - 1])
        x2 = regp.take(TILES, D)
        NOV = 9
        NSLOT = NEXP + NOV
        tab = regp.take(NSLOT, 4)
        ovid = regp.take(16)
        regs = Region(ebuf[NB - 1], ebuf[1])
        conv = regs.take(4, CT)
        sq2 = regs.take(2, CT)
        rstd = regs.take(CT)
        g1b, gain2, sh2b = regs.take(2, D), regs.take(2, D), regs.take(2, D)
        h2 = regs.take(D)
        xtmp, xsq, sq_pos = regs.take(D), regs.take(D), regs.take(D)
        rw_, rw_e, rb = regs.take(KD, 4), regs.take(KD, 32), regs.take(36)
        regw2 = Region(zbase, zbase + 3 * PAIRS * ZT + ZT)
        wout = regw2.take(KD, D)
        h2T = view(zbase + 3 * PAIRS * ZT + ZT, KD, P)
        routing = Region(ebuf[NB - 1], ebuf[NB - 1] + 4 * CT + 3 * CT)
        h2d = dram("tokens_for_experts", [T, D])
        slots = dram("slots", [NSLOT * P, 4], I32)
        yexp = dram("expert_rows", [2 * T, D])

        s_wout, s_modb, s_conv_in = sem("w_out_landed"), sem("mod_rows_landed"), sem("conv_landed")
        s_rw = sem("router_landed")
        s_gmean, s_gvar, s_gate = sem("head_means"), sem("head_variances"), sem("gates_summed")
        s_gd, s_gsq, s_gstd, s_gv, s_mixa = (sem(n) for n in (
            "head_centred", "head_squares", "head_deviation", "head_variance_taken", "rwkv_mixed"))
        s_cn, s_mixc = sem("conv_normed"), sem("conv_mixed")
        s_x2in, s_pos2 = sem("residual_landed"), sem("positions_landed_again")
        s_wo, s_x2, s_h2, s_h2st = (sem(n) for n in (
            "w_out_summed", "residual_ready", "expert_input_ready", "expert_input_stored"))
        s_h2t, s_h2Ta, s_h2Td, s_lg = (sem(n) for n in (
            "expert_input_turned", "h2T_low_ready", "h2T_high_ready", "logits_summed"))
        HC = [(0, 328), (328, CT)]

        def conv_tokens(i):
            at = 0 if i == 0 else P + 15 + (i - 1) * P
            return slice(at, at + P)

        def sp_out():
            sp = nc.sync
            sp.wait_ge(s_shiftD, 3 * NU)
            sp.wait_ge(s_shiftA, 3 * NU)
            sp.dma_start(wout, ins["w_out"][0].rearrange("(k p) n -> p k n", p=P)).then_inc(s_wout, 16)
            sp.wait_ge(s_finst, 128)
            sp.wait_ge(s_Y, step_at(NU - 1, 2))
            sp.wait_ge(s_YS, step_at(NU - 1, 2))
            sp.wait_ge(s_cst, 64)
            for j in range(4):
                sp.dma_start(conv[:, j], cout[j]).then_inc(s_conv_in, 16)
            sp.dma_start(rw_, ins["router_group_w"][0].rearrange("(k p) n -> p k n", p=P)).then_inc(s_rw, 16)
            sp.dma_start(rw_e, ins["router_expert_w"][0].rearrange("(k p) n -> p k n", p=P)).then_inc(s_rw, 16)
            sp.dma_start(rb[:, 0:4], ins["router_group_b"].broadcast_to([P, 4])).then_inc(s_rw, 16)
            sp.dma_start(rb[:, 4:36], ins["router_expert_b"].broadcast_to([P, 32])).then_inc(s_rw, 16)
            for i in range(TILES):
                sp.dma_start(x2[:, i], tok_src(i)).then_inc(s_x2in, 16)
            for c in range(2):
                for dst, m in ((g1b, 2), (sh2b, 3), (gain2, 4)):
                    sp.dma_start(dst[:, c], modrows[c:c + 1, m * D:(m + 1) * D].broadcast_to([P, D])
                                 ).then_inc(s_modb, 16)
            sp.dma_start(h2, ins["norm2_g"].broadcast_to([P, D])).then_inc(s_modb, 16)

        def experts_load(n):
            sp = nc.sync
            b = ebuf[n % NB]
            if n >= NB:
                sp.wait_ge(s_edown, n - NB + 1)
            for m, name in enumerate(("expert_w_gate", "expert_w_up", "expert_w_down")):
                sp.dma_start(view(b + 2048 * m, 2048), ins[name][0, n].rearrange("(p c) f -> p (c f)", p=P)
                             ).then_inc(s_ew[n % NB], 16)

        def pe_out():
            pe = nc.tensor
            pe.wait_ge(s_YS, step_at(NU - 1, 2))
            pe.wait_ge(s_finc, 1)
            for j in range(PAIRS):
                if j:
                    pe.wait_ge(s_gd, j)
                for h in range(2):
                    mm = nc.tensor.matmul(psum[h][:, 0:HALF], headones, ysum[:, j, h * HALF:(h + 1) * HALF],
                                          start=True, stop=True)
                mm.then_inc(s_gmean, 1)
                if j:
                    pe.wait_ge(s_mixa, j)
                for h in range(2):
                    mm = nc.tensor.matmul(psum[4 + h][:, 0:HALF], gateb[:, j * P:(j + 1) * P],
                                          gsig[:, h * HALF:(h + 1) * HALF], start=True, stop=True)
                mm.then_inc(s_gate, 1)
                pe.wait_ge(s_gsq, j + 1)
                if j:
                    pe.wait_ge(s_gv, j)
                for h in range(2):
                    mm = nc.tensor.matmul(psum[2 + h][:, 0:HALF], headones, sq2[:, j % 2, h * HALF:(h + 1) * HALF],
                                          start=True, stop=True)
                mm.then_inc(s_gvar, 1)
            pe.wait_ge(s_conv_in, 64)
            for h, (lo, hi) in enumerate(HC):
                for j in range(4):
                    mm = nc.tensor.matmul(psum[6 + h][:, 0:hi - lo], ones, conv[:, j, lo:hi],
                                          start=(j == 0), stop=(j == 3))
            mm.then_inc(s_gmean, 1)
            pe.wait_ge(s_gd, PAIRS + 4)
            for j in range(4):
                pe.wait_ge(s_gsq, PAIRS + j + 1)
                for h, (lo, hi) in enumerate(HC):
                    mm = nc.tensor.matmul(psum[6 + h][:, 0:hi - lo], ones, sq2[:, j % 2, lo:hi],
                                          start=(j == 0), stop=(j == 3))
                mm.then_inc(s_gvar, 1)
            pe.wait_ge(s_mixa, 4)
            pe.wait_ge(s_mixc, 4)
            pe.wait_ge(s_wout, 16)

            def turn(i):
                pe.wait_ge(s_h2, i + 1)
                if i:
                    pe.wait_ge(s_h2Ta, i)
                    pe.wait_ge(s_h2Td, i)
                for k in range(KD):
                    mm = nc.tensor.transpose(psum[4 + k // 4][:, (k % 4) * P:(k % 4 + 1) * P],
                                             h2[:, k * P:(k + 1) * P], ident)
                mm.then_inc(s_h2t, 1)
                pe.wait_ge(s_h2Ta, i + 1)
                pe.wait_ge(s_h2Td, i + 1)
                if i == 0:
                    pe.wait_ge(s_rw, 64)
                for lo, hi, w in ((0, 4, rw_), (4, 36, rw_e)):
                    for k in range(KD):
                        mm = nc.tensor.matmul(psum[6][:, 36 * i + lo:36 * i + hi], h2T[:, k], w[:, k],
                                              start=(k == 0), stop=(k == KD - 1))
                mm.then_inc(s_lg, 1)

            for i in range(TILES):
                for n in range(2):
                    if i >= 2:
                        pe.wait_ge(s_x2, i - 1)
                    for c in range(8):
                        lhs = ysum[:, c, i * P:(i + 1) * P] if c < 4 else conv[:, c - 4, conv_tokens(i)]
                        mm = nc.tensor.matmul(psum[2 * (i % 2) + n][:, :], lhs, wout[:, c, n * 512:(n + 1) * 512],
                                              start=(c == 0), stop=(c == 7))
                mm.then_inc(s_wo, 1)
                if i:
                    turn(i - 1)
            turn(TILES - 1)

        def dve_out(chain):
            dve = nc.vector
            for j in range(PAIRS):
                y = ysum[:, j]
                dve.wait_ge(s_gmean, j + 1)
                for h in range(2):
                    c = slice(h * HALF, (h + 1) * HALF)
                    ins_ = nc.vector.scalar_tensor_tensor(y[:, c], psum[h][:, 0:HALF], -1.0 / 64, y[:, c],
                                                          ALU.mult, ALU.add)
                    if h == 0:
                        chain(ins_)
                chain.announce(ins_, s_gd, j + 1)
                dve.wait_ge(s_gvar, j + 1)
                chain(nc.vector.tensor_scalar(rstd[:, 0:HALF], psum[2][:, 0:HALF], 1.0 / 64, GN_EPS, ALU.mult, ALU.add))
                chain.announce(nc.vector.tensor_scalar(rstd[:, HALF:T], psum[3][:, 0:HALF], 1.0 / 64, GN_EPS,
                                                     ALU.mult, ALU.add), s_gv, j + 1)
                dve.wait_ge(s_gstd, j + 1)
                chain(nc.vector.reciprocal(rstd[:, 0:T], rstd[:, 0:T]))
                g, b_ = PAR["gng"] + j, PAR["gnb"] + j
                chain(nc.vector.scalar_tensor_tensor(y, y, par[:, g:g + 1], rstd[:, 0:T], ALU.mult, ALU.mult))
                dve.wait_ge(s_gate, j + 1)
                for h in range(2):
                    c = slice(h * HALF, (h + 1) * HALF)
                    ins_ = nc.vector.scalar_tensor_tensor(y[:, c], y[:, c], par[:, b_:b_ + 1], psum[4 + h][:, 0:HALF],
                                                          ALU.add, ALU.mult)
                    if h == 0:
                        chain(ins_)
                chain.announce(ins_, s_mixa, j + 1)
            dve.wait_ge(s_gmean, PAIRS + 1)
            for j in range(4):
                for h, (lo, hi) in enumerate(HC):
                    ins_ = nc.vector.scalar_tensor_tensor(conv[:, j, lo:hi], psum[6 + h][:, 0:hi - lo], -1.0 / 512,
                                                          conv[:, j, lo:hi], ALU.mult, ALU.add)
                    if h == 0:
                        chain(ins_)
                chain.announce(ins_, s_gd, PAIRS + j + 1)
            dve.wait_ge(s_gvar, PAIRS + 4)
            for h, (lo, hi) in enumerate(HC):
                ins_ = nc.vector.tensor_scalar(rstd[:, lo:hi], psum[6 + h][:, 0:hi - lo], 1.0 / 512, LN_EPS,
                                               ALU.mult, ALU.add)
                if h == 0:
                    chain(ins_)
            chain.announce(ins_, s_gv, PAIRS + 1)
            dve.wait_ge(s_gstd, PAIRS + 1)
            chain(nc.vector.reciprocal(rstd, rstd))
            for j in range(4):
                chain.announce(nc.vector.tensor_tensor(conv[:, j], conv[:, j], rstd, ALU.mult), s_cn, j + 1)
            dve.wait_ge(s_modb, 16 * 7)
            for c in range(2):
                chain(nc.vector.scalar_tensor_tensor(gain2[:, c], gain2[:, c], 1.0, h2, ALU.add, ALU.mult))
            dve.wait_ge(s_x2in, 16 * TILES)

            def taken(i):
                dve.wait_ge(s_h2t, i + 1)
                chain.announce(nc.vector.tensor_copy(h2T[:, 4:8], psum[5][:, :].rearrange("p (k t) -> p k t", t=P)),
                             s_h2Td, i + 1)

            for i in range(TILES):
                c = int(i > 0)
                dve.wait_ge(s_wo, i + 1)
                if i:
                    dve.wait_ge(s_pos2, 16 * i)
                    chain(nc.vector.tensor_tensor(x2[:, i], x2[:, i], sq_pos, ALU.add))
                for n in range(2):
                    o = slice(n * 512, n * 512 + 512)
                    chain(nc.vector.tensor_tensor(xtmp[:, o], psum[2 * (i % 2) + n][:, :], g1b[:, c, o], ALU.mult))
                chain.announce(nc.vector.tensor_tensor(x2[:, i], x2[:, i], xtmp, ALU.add), s_x2, i + 1)
                dve.wait_ge(s_xstat, TILES + i + 1)
                chain.announce(nc.vector.tensor_scalar(small[:, i:i + 1], small[:, i:i + 1], 1.0 / D, RMS_EPS,
                                                     ALU.mult, ALU.add), s_var, TILES + i + 1)
                dve.wait_ge(s_std, TILES + i + 1)
                chain(nc.vector.reciprocal(small[:, 16 + i:17 + i], small[:, 8 + i:9 + i]))
                if i:
                    dve.wait_ge(s_h2t, i)
                    dve.wait_ge(s_h2st, 16 * i)
                chain(nc.vector.scalar_tensor_tensor(h2, x2[:, i], small[:, 16 + i:17 + i], gain2[:, c],
                                                     ALU.mult, ALU.mult))
                chain.announce(nc.vector.tensor_tensor(h2, h2, sh2b[:, c], ALU.add), s_h2, i + 1)
                taken(i)

        def act_out(chain):
            act = nc.scalar
            for j in range(PAIRS):
                act.wait_ge(s_gd, j + 1)
                if j >= 2:
                    act.wait_ge(s_gvar, j - 1)
                chain.announce(nc.scalar.activation(sq2[:, j % 2, 0:T], ysum[:, j], ACT.Square), s_gsq, j + 1)
                act.wait_ge(s_gv, j + 1)
                chain.announce(nc.scalar.activation(rstd[:, 0:T], rstd[:, 0:T], ACT.Sqrt), s_gstd, j + 1)
            for j in range(4):
                act.wait_ge(s_gd, PAIRS + j + 1)
                if j >= 2:
                    act.wait_ge(s_gvar, PAIRS + j - 1)
                else:
                    act.wait_ge(s_gvar, 4)
                chain.announce(nc.scalar.activation(sq2[:, j % 2], conv[:, j], ACT.Square), s_gsq, PAIRS + j + 1)
            act.wait_ge(s_gv, PAIRS + 1)
            chain.announce(nc.scalar.activation(rstd, rstd, ACT.Sqrt), s_gstd, PAIRS + 1)
            for j in range(4):
                act.wait_ge(s_cn, j + 1)
                g, b_ = PAR["clg"] + j, PAR["clb"] + j
                chain.announce(nc.scalar.activation(conv[:, j], conv[:, j], ACT.Silu, bias=par[:, b_:b_ + 1],
                                                  scale=par[:, g:g + 1]), s_mixc, j + 1)
            for i in range(TILES):
                if i:
                    if i >= 2:
                        act.wait_ge(s_x2, i)
                    act.dma_start(sq_pos, pos[(i - 1) * P:i * P, :]).then_inc(s_pos2, 16)
                act.wait_ge(s_x2, i + 1)
                chain.announce(nc.scalar.activation(xsq, x2[:, i], ACT.Square, accum_out=small[:, i:i + 1]),
                             s_xstat, TILES + i + 1)
                act.wait_ge(s_var, TILES + i + 1)
                chain.announce(nc.scalar.activation(small[:, 8 + i:9 + i], small[:, i:i + 1], ACT.Sqrt), s_std, TILES + i + 1)
                act.wait_ge(s_h2, i + 1)
                act.dma_start(h2d[i * P:(i + 1) * P, :], h2).then_inc(s_h2st, 16)
                act.wait_ge(s_h2t, i + 1)
                chain.announce(nc.scalar.activation(h2T[:, 0:4], psum[4][:, :].rearrange("p (k t) -> p k t", t=P),
                                                  ACT.Copy), s_h2Ta, i + 1)

        NLANE = 2 * TILES
        lg = routing.take(TILES, 36)
        oh = routing.take(2, TILES, 32)
        ohg = routing.take(TILES, 4)
        sel, seq_ = routing.take(TILES, 32), routing.take(TILES, 32)
        both, base = routing.take(TILES, 32), routing.take(TILES + 1, 32)
        pick = routing.take(2, TILES, 32)
        iot = routing.take(32)
        mx, mn = routing.take(2, TILES), routing.take(2, TILES)
        gexp = routing.take(TILES, 4)
        t1, t2, t3, t4 = (routing.take(TILES) for _ in range(4))
        r_, ob, kk_, big, tl = (routing.take(2, TILES) for _ in range(5))
        nt, inc, ovb = routing.take(32), routing.take(32), routing.take(32)
        ova, ovc = routing.take(NOV, 32), routing.take(NOV, 32)
        oint = routing.take(16)
        ent = routing.take(NLANE, 4)
        sloti = routing.take(NLANE)
        initt = routing.take(NSLOT, 4)
        MISS = 1 << 20

        regm = Region(zbase, wbase)
        xe, xeT = regm.take(2, D), regm.take(2, KD, P)
        hid, hidT = regm.take(2, 256), regm.take(2, 2, P)
        eo = regm.take(2, D)
        ovtab = regm.take(4)
        OVB = NEXP % NB
        OVFILLS = NEXP // NB
        rege = Region(zbase, wbase)
        ya, yb = rege.take(2, D), rege.take(2, D)
        g2b, fgain, fsq = rege.take(2, D), rege.take(D), rege.take(D)

        s_ew = [sem(f"expert_landed{b}") for b in range(NB)]
        s_mx, s_ge, s_oh, s_rank, s_ent = (sem(n) for n in (
            "gate_logits_centred", "gate_exponentials", "experts_picked", "ranks_summed", "slot_entries_ready"))
        s_tinit0, s_tinit, s_scat, s_tab, s_ovst = (sem(n) for n in (
            "slot_blank_ready", "slots_blank", "slots_filled", "slots_read", "overflow_list_ready"))
        s_gat = [sem(f"expert_rows_gathered{b}") for b in range(2)]
        s_escat = [sem(f"expert_out_scattered{b}") for b in range(2)]
        s_fst = [sem(f"final_stored{b}") for b in range(2)]
        s_xez, s_et, s_eTa, s_eTd = (sem(n) for n in (
            "expert_rows_zeroed", "expert_rows_turned", "xeT_low_ready", "xeT_high_ready"))
        s_gu, s_silu2, s_hid, s_ht, s_hT, s_edown, s_eoa, s_eod = (sem(n) for n in (
            "gate_up_summed", "gate_silu_done", "hidden_ready", "hidden_turned", "hiddenT_ready", "down_summed",
            "expert_out_low", "expert_out_high"))
        s_fin_in = [sem(f"rows_back{b}") for b in range(2)]
        s_ovgo = sem("overflow_dma_may_start")
        s_fg, s_xf, s_fout = sem("final_gains_landed"), sem("final_sum_ready"), sem("final_ready")
        from concourse.bass import IndirectOffsetOnAxis as At

        def dve_route(chain):
            dve = nc.vector
            B5 = [P, TILES, 32]
            iotam = const("expiota")
            dve.wait_ge(s_lg, TILES)
            dve.wait_ge(s_h2st, 16 * TILES)
            chain(nc.vector.memset(initt[:, :, 2:4], 0.0))
            chain.announce(nc.vector.memset(initt[:, :, 0:2].bitcast(I32), MISS), s_tinit0, 1)
            chain(nc.vector.tensor_tensor(lg, psum[6][:, 0:36 * TILES].rearrange("p (i e) -> p i e", e=36),
                                          rb.unsqueeze(1).broadcast_to([P, TILES, 36]), ALU.add))
            chain(nc.vector.tensor_scalar(iot, iotam, 64.0, None, ALU.add))
            lgg, lge = lg[:, :, 0:4], lg[:, :, 4:36]

            def first_max(vals, n, out, top, low):
                sh = [P, TILES, n]
                im = iotam[:, 0:n].unsqueeze(1).broadcast_to(sh)
                cand = seq_[:, :, 0:n]
                chain(nc.vector.tensor_reduce(top, vals, AX_X, ALU.max))
                chain(nc.vector.tensor_tensor(cand, vals, top.unsqueeze(2).broadcast_to(sh), ALU.is_ge))
                chain(nc.vector.tensor_tensor(cand, cand, im, ALU.mult))
                chain(nc.vector.tensor_reduce(low, cand, AX_X, ALU.min))
                chain(nc.vector.tensor_tensor(out, im, low.unsqueeze(2).broadcast_to(sh), ALU.is_equal))

            first_max(lgg, 4, ohg, t1, t2)
            chain.announce(nc.vector.tensor_tensor(gexp, lgg, t1.unsqueeze(2).broadcast_to([P, TILES, 4]),
                                                 ALU.subtract), s_mx, 1)
            g4 = ohg.unsqueeze(3).broadcast_to([P, TILES, 4, 8])
            s4 = sel.rearrange("p i (g e) -> p i g e", g=4)
            chain(nc.vector.tensor_tensor(s4, lge.rearrange("p i (g e) -> p i g e", g=4), g4, ALU.mult))
            chain(nc.vector.tensor_scalar(ohg, ohg, 1.0, 1e30, ALU.subtract, ALU.mult))
            chain(nc.vector.tensor_tensor(s4, s4, g4, ALU.add))
            first_max(sel, 32, oh[:, 0], mx[:, 0], mn[:, 0])
            chain(nc.vector.scalar_tensor_tensor(sel, oh[:, 0], -1e30, sel, ALU.mult, ALU.add))
            first_max(sel, 32, oh[:, 1], mx[:, 1], mn[:, 1])
            chain.announce(nc.vector.tensor_tensor(both, oh[:, 0], oh[:, 1], ALU.add), s_oh, 1)
            chain.announce(nc.vector.tensor_tensor(t3, mx[:, 1], mx[:, 0], ALU.subtract), s_mx, 2)
            dve.wait_ge(s_ge, 2)
            chain(nc.vector.tensor_reduce(t1, gexp, AX_X, ALU.add))
            chain(nc.vector.scalar_tensor_tensor(t2, t3, 1.0, t1, ALU.add, ALU.mult))
            chain(nc.vector.reciprocal(t2, t2))
            chain(nc.vector.tensor_copy(ent[:, 0:TILES, 2], t2))
            chain(nc.vector.tensor_tensor(ent[:, TILES:NLANE, 2], t2, t3, ALU.mult))
            chain(nc.vector.memset(ent[:, :, 3], 0.0))
            dve.wait_ge(s_rank, 1)
            chain(nc.vector.memset(base[:, 0], 0.0))
            tot = psum[3][:, 0:160].rearrange("p (i e) -> p i e", e=32)
            for i in range(TILES):
                chain(nc.vector.tensor_tensor(base[:, i + 1], base[:, i], tot[:, i], ALU.add))
            chain(nc.vector.tensor_tensor(both, psum[2][:, 0:160].rearrange("p (i e) -> p i e", e=32),
                                          base[:, 0:TILES], ALU.add))
            n_e = base[:, TILES]
            chain(nc.vector.tensor_scalar(nt, n_e, float(P), None, ALU.is_gt))
            for c in range(2, 5):
                chain(nc.vector.scalar_tensor_tensor(nt, n_e, float(P * c), nt, ALU.is_gt, ALU.add))
            chain(nc.vector.tensor_tensor_scan(inc, const("ones")[:, 0:32], nt, 0.0, ALU.mult, ALU.add))
            chain(nc.vector.tensor_tensor(ovb, inc, nt, ALU.subtract))
            four = [P, 2, TILES, 32]
            chain(nc.vector.tensor_tensor(pick, oh, both.unsqueeze(1).broadcast_to(four), ALU.mult))
            chain(nc.vector.tensor_reduce(r_, pick, AX_X, ALU.add))
            chain(nc.vector.tensor_tensor(pick, oh, ovb.unsqueeze(1).unsqueeze(1).broadcast_to(four), ALU.mult))
            chain(nc.vector.tensor_reduce(ob, pick, AX_X, ALU.add))
            chain(nc.vector.tensor_scalar(kk_, r_, float(P), None, ALU.is_ge))
            for c in range(2, 5):
                chain(nc.vector.scalar_tensor_tensor(kk_, r_, float(P * c), kk_, ALU.is_ge, ALU.add))
            chain(nc.vector.tensor_scalar(big, kk_, 1.0, None, ALU.min))
            chain(nc.vector.tensor_scalar(mn, mn, 64.0, None, ALU.add))
            chain(nc.vector.tensor_tensor(tl, ob, kk_, ALU.add))
            chain(nc.vector.scalar_tensor_tensor(tl, tl, float(NEXP - 1), mn, ALU.add, ALU.subtract))
            chain(nc.vector.tensor_tensor(tl, tl, big, ALU.mult))
            chain(nc.vector.tensor_tensor(tl, tl, mn, ALU.add))
            chain(nc.vector.tensor_tensor(tl, tl, kk_, ALU.subtract))
            chain(nc.vector.scalar_tensor_tensor(tl, tl, float(P), r_, ALU.mult, ALU.add))
            chain(nc.vector.tensor_copy(sloti.bitcast(I32), tl.rearrange("p a b -> p (a b)")))
            tok = const("lanes")[:, 0:TILES]
            e2 = ent.bitcast(I32)
            for k in range(2):
                chain(nc.vector.tensor_copy(e2[:, k * TILES:(k + 1) * TILES, 0], tok))
                ins_ = nc.vector.tensor_scalar(e2[:, k * TILES:(k + 1) * TILES, 1], tok, float(k * T), None, ALU.add)
                if k == 0:
                    chain(ins_)
            chain.announce(ins_, s_ent, 1)
            so = [P, NOV, 32]
            m_ = const("ovi")[:, 0:NOV].unsqueeze(2).broadcast_to(so)
            chain(nc.vector.tensor_tensor(ova, ovb.unsqueeze(1).broadcast_to(so), m_, ALU.is_le))
            chain(nc.vector.tensor_tensor(ovc, inc.unsqueeze(1).broadcast_to(so), m_, ALU.is_gt))
            chain(nc.vector.tensor_tensor(ova, ova, ovc, ALU.mult))
            chain(nc.vector.tensor_tensor(ova, ova, iot.unsqueeze(1).broadcast_to(so), ALU.mult))
            chain(nc.vector.tensor_reduce(oint[:, 0:NOV], ova, AX_X, ALU.add))
            chain(nc.vector.tensor_copy(ovid[:, 0:NOV].bitcast(I32), oint[:, 0:NOV]))
            chain.announce(nc.vector.tensor_copy(ovid[:, 15:16].bitcast(I32), inc[:, 31:32]), s_ovst, 1)

        def act_route(chain):
            act = nc.scalar
            act.wait_ge(s_mx, 1)
            chain.announce(nc.scalar.activation(gexp, gexp, ACT.Exp), s_ge, 1)
            act.wait_ge(s_mx, 2)
            chain.announce(nc.scalar.activation(t3, t3, ACT.Exp), s_ge, 2)

        def pe_route():
            pe = nc.tensor
            pe.wait_ge(s_oh, 1)
            flat = both.rearrange("p i e -> p (i e)")
            nc.tensor.matmul(psum[2][:, 0:160], const("before"), flat, start=True, stop=True)
            nc.tensor.matmul(psum[3][:, 0:160], ones, flat, start=True, stop=True).then_inc(s_rank, 1)

        def pool_route():
            pool = nc.gpsimd
            pool.wait_ge(s_tinit0, 1)
            pool.dma_start(slots.rearrange("(p a) b -> p a b", p=P), initt.bitcast(I32)).then_inc(s_tinit, 16)
            pool.wait_ge(s_tinit, 16)
            pool.wait_ge(s_ent, 1)
            for n in range(NLANE):
                pool.indirect_dma_start(out=slots, out_offset=At(ap=sloti[:, n:n + 1].bitcast(U32), axis=0),
                                        in_=ent[:, n, :].bitcast(I32), in_offset=None).then_inc(s_scat, 16)

        def sp_table():
            sp = nc.sync
            sp.wait_ge(s_scat, 16 * NLANE)
            sp.dma_start(tab.bitcast(I32), slots.rearrange("(a p) b -> p a b", p=P)).then_inc(s_tab, 16)

        def gather(pool, n):
            if n >= 2:
                pool.wait_ge(s_et, n - 1)
            pool.indirect_dma_start(out=xe[:, n % 2], out_offset=None, in_=h2d,
                                    in_offset=At(ap=tab[:, n, 0:1].bitcast(U32), axis=0),
                                    bounds_check=T - 1, oob_is_err=False).then_inc(s_gat[n % 2], 16)

        def pool_experts(chain):
            pool = nc.gpsimd
            pool.wait_ge(s_wo, TILES)
            pool.wait_ge(s_lg, TILES)
            chain.announce(nc.gpsimd.memset(xe, 0.0), s_xez, 1)
            pool.wait_ge(s_tab, 16)
            pool.wait_ge(s_h2st, 16 * TILES)
            gather(pool, 0)
            gather(pool, 1)
            for n in range(NEXP):
                if n + 2 < NEXP:
                    gather(pool, n + 2)
                pool.wait_ge(s_eoa, n + 1)
                pool.wait_ge(s_eod, n + 1)
                pool.indirect_dma_start(out=yexp, out_offset=At(ap=tab[:, n, 1:2].bitcast(U32), axis=0),
                                        in_=eo[:, n % 2], in_offset=None,
                                        bounds_check=2 * T - 1, oob_is_err=False).then_inc(s_escat[n % 2], 16)

        def overflow_count(engine):
            engine.wait_ge(s_ovst, 1)
            return engine.value_load(ovid[0:1, 15:16].bitcast(I32), min_val=0, max_val=NOV)

        def sp_overflow():
            sp = nc.sync
            count = overflow_count(sp)
            w = ebuf[OVB]
            with sp.Fori(0, count) as m:
                sp.wait_ge(s_edown, m + NEXP)
                sp.wait_ge(s_escat[0], m * 16 + 8 * NEXP)
                sp.dma_start(ovtab.bitcast(I32), slots[bass.ds((m + NEXP) * P, P), :]).then_inc(s_tab, 16)
                e = sp.value_load(ovid[0:1, bass.ds(m, 1)].bitcast(I32), min_val=0, max_val=NEXP - 1)
                for j, name in enumerate(("expert_w_gate", "expert_w_up", "expert_w_down")):
                    sp.dma_start(view(w + 2048 * j, 2048), ins[name][0, bass.ds(e, 1)].rearrange(
                        "o (p c) f -> p (o c f)", p=P)).then_inc(s_ew[OVB], 16)
            sp.wait_ge(s_escat[0], count * 16 + 8 * NEXP)
            sp.wait_ge(s_escat[0], 8 * NEXP + 16)
            sp.wait_ge(s_escat[1], 8 * NEXP)

        def pool_overflow():
            pool = nc.gpsimd
            count = overflow_count(pool)
            last_token, last_row = pool.to_reg(T - 1), pool.to_reg(2 * T - 1)
            with pool.Fori(0, count) as m:
                pool.wait_ge(s_tab, m * 16 + 32)
                pool.wait_ge(s_et, m + NEXP)
                pool.sem_inc(s_ovgo, 1)
                pool.indirect_dma_start(out=xe[:, 0], out_offset=None, in_=h2d,
                                        in_offset=At(ap=ovtab[:, 0:1].bitcast(U32), axis=0),
                                        bounds_check=last_token, oob_is_err=False).then_inc(s_gat[0], 16)
                pool.wait_ge(s_eoa, m + NEXP + 1)
                pool.wait_ge(s_eod, m + NEXP + 1)
                pool.sem_inc(s_ovgo, 1)
                pool.indirect_dma_start(out=yexp, out_offset=At(ap=ovtab[:, 1:2].bitcast(U32), axis=0),
                                        in_=eo[:, 0], in_offset=None,
                                        bounds_check=last_row, oob_is_err=False).then_inc(s_escat[0], 16)

        def pe_overflow():
            pe = nc.tensor
            gu, wd = wview(OVB)
            with pe.Fori(0, overflow_count(pe)) as m:
                pe.wait_ge(s_gat[0], m * 16 + 8 * NEXP + 16)
                pe.wait_ge(s_eTa, m + NEXP)
                pe.wait_ge(s_eTd, m + NEXP)
                for c in range(KD):
                    mm = nc.tensor.transpose(psum[c // 4][:, (c % 4) * P:(c % 4 + 1) * P], xe[:, 0, c::KD], ident)
                mm.then_inc(s_et, 1)
                pe.wait_ge(s_eTa, m + NEXP + 1)
                pe.wait_ge(s_eTd, m + NEXP + 1)
                pe.wait_ge(s_ew[OVB], (m + OVFILLS + 1) * 48)
                pe.wait_ge(s_hid, m + NEXP)
                for c in range(KD):
                    mm = nc.tensor.matmul(psum[2][:, :], xeT[:, 0, c], gu[:, :, c, :], start=(c == 0), stop=(c == KD - 1))
                mm.then_inc(s_gu, 1)
                pe.wait_ge(s_hid, m + NEXP + 1)
                for c in range(2):
                    mm = nc.tensor.transpose(psum[4][:, c * P:(c + 1) * P], hid[:, 0, c::2], ident)
                mm.then_inc(s_ht, 1)
                pe.wait_ge(s_hT, m + NEXP + 1)
                pe.wait_ge(s_eoa, m + NEXP)
                pe.wait_ge(s_eod, m + NEXP)
                for h in range(2):
                    for c in range(2):
                        mm = nc.tensor.matmul(psum[5 + h][:, :], hidT[:, 0, c], wd[:, c, h * 512:(h + 1) * 512],
                                              start=(c == 0), stop=(c == 1))
                mm.then_inc(s_edown, 1)

        def act_overflow():
            act = nc.scalar
            with act.Fori(0, overflow_count(act)) as m:
                act.wait_ge(s_et, m + NEXP + 1)
                nc.scalar.activation(xeT[:, 0, 0:4], psum[0][:, :].rearrange("p (k t) -> p k t", t=P),
                                     ACT.Copy).then_inc(s_eTa, 1)
                act.wait_ge(s_gu, m + NEXP + 1)
                nc.scalar.activation(hid[:, 0], psum[2][:, 0:256], ACT.Silu).then_inc(s_silu2, 1)
                act.wait_ge(s_edown, m + NEXP + 1)
                act.wait_ge(s_escat[0], m * 16 + 8 * NEXP)
                nc.scalar.activation(eo[:, 0, 0:512], psum[5][:, :], ACT.Copy, scale=ovtab[:, 2:3]).then_inc(s_eoa, 1)

        def dve_overflow():
            dve = nc.vector
            with dve.Fori(0, overflow_count(dve)) as m:
                dve.wait_ge(s_et, m + NEXP + 1)
                nc.vector.tensor_copy(xeT[:, 0, 4:8], psum[1][:, :].rearrange("p (k t) -> p k t", t=P)
                                      ).then_inc(s_eTd, 1)
                dve.wait_ge(s_silu2, m + NEXP + 1)
                nc.vector.tensor_tensor(hid[:, 0], hid[:, 0], psum[2][:, 256:512], ALU.mult).then_inc(s_hid, 1)
                dve.wait_ge(s_ht, m + NEXP + 1)
                nc.vector.tensor_copy(hidT[:, 0], psum[4][:, 0:256].rearrange("p (k t) -> p k t", t=P)
                                      ).then_inc(s_hT, 1)
                dve.wait_ge(s_edown, m + NEXP + 1)
                dve.wait_ge(s_escat[0], m * 16 + 8 * NEXP)
                nc.vector.tensor_scalar(eo[:, 0, 512:1024], psum[6][:, :], ovtab[:, 2:3], None, ALU.mult
                                        ).then_inc(s_eod, 1)

        def wview(n):
            b = ebuf[n % NB]
            gu = view(b, 4096).rearrange("p (m c f) -> p m c f", m=2, c=KD)
            return gu, view(b + 4096, 2, D)

        def pe_experts():
            pe = nc.tensor

            def turn(n):
                pe.wait_ge(s_gat[n % 2], 16 * (n // 2 + 1))
                if n:
                    pe.wait_ge(s_eTa, n)
                    pe.wait_ge(s_eTd, n)
                for c in range(KD):
                    mm = nc.tensor.transpose(psum[c // 4][:, (c % 4) * P:(c % 4 + 1) * P], xe[:, n % 2, c::KD], ident)
                mm.then_inc(s_et, 1)

            def gate_up(n):
                pe.wait_ge(s_eTa, n + 1)
                pe.wait_ge(s_eTd, n + 1)
                pe.wait_ge(s_ew[n % NB], 48 * (n // NB + 1))
                if n >= 2:
                    pe.wait_ge(s_hid, n - 1)
                gu, _ = wview(n)
                for c in range(KD):
                    mm = nc.tensor.matmul(psum[2 + n % 2][:, :], xeT[:, n % 2, c], gu[:, :, c, :],
                                          start=(c == 0), stop=(c == KD - 1))
                mm.then_inc(s_gu, 1)

            def down(n):
                pe.wait_ge(s_hid, n + 1)
                if n:
                    pe.wait_ge(s_hT, n)
                for c in range(2):
                    mm = nc.tensor.transpose(psum[4][:, c * P:(c + 1) * P], hid[:, n % 2, c::2], ident)
                mm.then_inc(s_ht, 1)
                pe.wait_ge(s_hT, n + 1)
                if n:
                    pe.wait_ge(s_eoa, n)
                    pe.wait_ge(s_eod, n)
                _, wd = wview(n)
                for h in range(2):
                    for c in range(2):
                        mm = nc.tensor.matmul(psum[5 + h][:, :], hidT[:, n % 2, c], wd[:, c, h * 512:(h + 1) * 512],
                                              start=(c == 0), stop=(c == 1))
                mm.then_inc(s_edown, 1)

            pe.wait_ge(s_ent, 1)
            turn(0)
            for n in range(NEXP):
                gate_up(n)
                if n + 1 < NEXP:
                    turn(n + 1)
                if n:
                    down(n - 1)
            down(NEXP - 1)

        def act_experts(chain):
            act = nc.scalar

            def turned(n):
                act.wait_ge(s_et, n + 1)
                if n >= 2:
                    act.wait_ge(s_gu, n - 1)
                chain.announce(nc.scalar.activation(xeT[:, n % 2, 0:4], psum[0][:, :].rearrange("p (k t) -> p k t", t=P),
                                                  ACT.Copy), s_eTa, n + 1)

            def out(n):
                act.wait_ge(s_edown, n + 1)
                if n >= 2:
                    act.wait_ge(s_escat[n % 2], 16 * (n // 2))
                chain.announce(nc.scalar.activation(eo[:, n % 2, 0:512], psum[5][:, :], ACT.Copy,
                                                  scale=tab[:, n, 2:3]), s_eoa, n + 1)

            turned(0)
            for n in range(NEXP):
                if n + 1 < NEXP:
                    turned(n + 1)
                act.wait_ge(s_gu, n + 1)
                chain.announce(nc.scalar.activation(hid[:, n % 2], psum[2 + n % 2][:, 0:256], ACT.Silu), s_silu2, n + 1)
                if n:
                    out(n - 1)
            out(NEXP - 1)

        def dve_experts(chain):
            dve = nc.vector

            def turned(n):
                dve.wait_ge(s_et, n + 1)
                if n >= 2:
                    dve.wait_ge(s_gu, n - 1)
                chain.announce(nc.vector.tensor_copy(xeT[:, n % 2, 4:8], psum[1][:, :].rearrange("p (k t) -> p k t", t=P)),
                             s_eTd, n + 1)

            def out(n):
                dve.wait_ge(s_ht, n + 1)
                chain.announce(nc.vector.tensor_copy(hidT[:, n % 2], psum[4][:, 0:256].rearrange("p (k t) -> p k t", t=P)),
                             s_hT, n + 1)
                dve.wait_ge(s_edown, n + 1)
                if n >= 2:
                    dve.wait_ge(s_escat[n % 2], 16 * (n // 2))
                chain.announce(nc.vector.tensor_scalar(eo[:, n % 2, 512:1024], psum[6][:, :], tab[:, n, 2:3], None,
                                                     ALU.mult), s_eod, n + 1)

            dve.wait_ge(s_tab, 16)
            turned(0)
            for n in range(NEXP):
                if n + 1 < NEXP:
                    turned(n + 1)
                dve.wait_ge(s_silu2, n + 1)
                chain.announce(nc.vector.tensor_tensor(hid[:, n % 2], hid[:, n % 2], psum[2 + n % 2][:, 256:512],
                                                     ALU.mult), s_hid, n + 1)
                if n:
                    out(n - 1)
            out(NEXP - 1)

        def tok_dst(i):
            return outs["y_prompt"][0] if i == 0 else outs["y_sample"][0, (i - 1) * P:i * P, :]

        def sp_end():
            sp = nc.sync
            for c in range(2):
                sp.dma_start(g2b[:, c], modrows[c:c + 1, 5 * D:6 * D].broadcast_to([P, D])).then_inc(s_fg, 16)
            sp.dma_start(fgain, ins["final_norm_g"].rearrange("(o n) -> o n", o=1).broadcast_to([P, D])
                         ).then_inc(s_fg, 16)
            for i in range(TILES):
                if i >= 2:
                    sp.wait_ge(s_fst[i % 2], 16 * (i // 2))
                for k, dst in enumerate((ya, yb)):
                    sp.dma_start(dst[:, i % 2], yexp[k * T + i * P:k * T + (i + 1) * P, :]).then_inc(s_fin_in[i % 2], 16)

        def dve_end(chain):
            dve = nc.vector
            dve.wait_ge(s_fg, 48)
            for i in range(TILES):
                y = ya[:, i % 2]
                dve.wait_ge(s_fin_in[i % 2], 32 * (i // 2 + 1))
                chain(nc.vector.tensor_tensor(y, y, yb[:, i % 2], ALU.add))
                chain(nc.vector.tensor_tensor(y, y, g2b[:, int(i > 0)], ALU.mult))
                chain.announce(nc.vector.tensor_tensor(x2[:, i], x2[:, i], y, ALU.add), s_xf, i + 1)
                dve.wait_ge(s_xstat, 2 * TILES + i + 1)
                chain.announce(nc.vector.tensor_scalar(small[:, i:i + 1], small[:, i:i + 1], 1.0 / D, RMS_EPS,
                                                     ALU.mult, ALU.add), s_var, 2 * TILES + i + 1)
                dve.wait_ge(s_std, 2 * TILES + i + 1)
                chain(nc.vector.reciprocal(small[:, 16 + i:17 + i], small[:, 8 + i:9 + i]))
                chain.announce(nc.vector.scalar_tensor_tensor(y, x2[:, i], small[:, 16 + i:17 + i], fgain,
                                                            ALU.mult, ALU.mult), s_fout, i + 1)

        def act_end(chain):
            act = nc.scalar
            for i in range(TILES):
                act.wait_ge(s_xf, i + 1)
                chain.announce(nc.scalar.activation(fsq, x2[:, i], ACT.Square, accum_out=small[:, i:i + 1]),
                             s_xstat, 2 * TILES + i + 1)
                act.wait_ge(s_var, 2 * TILES + i + 1)
                chain.announce(nc.scalar.activation(small[:, 8 + i:9 + i], small[:, i:i + 1], ACT.Sqrt), s_std, 2 * TILES + i + 1)
                act.wait_ge(s_fout, i + 1)
                act.dma_start(tok_dst(i), ya[:, i % 2]).then_inc(s_fst[i % 2], 16)
            act.wait_ge(s_fst[0], 48)
            act.wait_ge(s_fst[1], 32)

        @block.sync
        def _(sp):
            sp_front()
            sp_mix()
            sp_out()
            for n in range(2):
                experts_load(n)
            sp_table()
            sp.wait_ge(s_ovst, 1)
            for n in range(2, NEXP):
                experts_load(n)
            sp_overflow()
            sp_end()

        @block.scalar
        def _(act):
            chain = act_front()
            act_mix(chain)
            act_out(chain)
            act_route(chain)
            act_experts(chain)
            act_overflow()
            act_end(chain)

        @block.vector
        def _(dve):
            chain = dve_front()
            dve_mix(chain)
            dve_out(chain)
            dve_route(chain)
            dve_experts(chain)
            dve_overflow()
            dve_end(chain)

        @block.gpsimd
        def _(pool):
            chain = Chain(nc.gpsimd, g_self)
            pool_front()
            pool_mix(chain)
            pool_route()
            pool_experts(chain)
            pool_overflow()

        @block.tensor
        def _(pe):
            pe_front()
            pe_mix()
            pe_out()
            pe_route()
            pe_experts()
            pe_overflow()


def _constants():
    import numpy as np

    c = {}
    i = np.arange(P)
    c["ident"] = np.eye(P)
    c["headones"] = (i[:, None] // 64 == i[None] // 64) * 1.0
    c["ones"] = np.ones((P, P))
    s, t = i[:, None] % C, np.arange(C)[None]
    c["gmask"] = np.concatenate([s < t, s <= t], 1) * 1.0
    c["scanmask"] = np.tile((np.arange(512) % C != 0) * 1.0, (P, 1))
    r, j = np.arange(32)[:, None], np.arange(16)[None]
    c["eye16"] = np.stack([(r == 2 * j + q // 64).reshape(-1) for q in range(P)]) * 1.0
    c["before"] = (i[:, None] < i[None]) * 1.0
    c["expiota"] = np.tile(np.arange(NEXP) - 64, (P, 1))
    c["lanes"] = np.tile(i[:, None], (1, 8)) + 128.0 * np.arange(8)[None]
    c["ovi"] = np.tile(np.arange(16), (P, 1))
    return np.concatenate([c[n] for n, _ in CONSTS], 1).astype(np.float32)


def _positions():
    import numpy as np

    t = np.arange(TS)
    q = D // 4
    f = (1.0 / (np.float32(10000.0) ** (np.arange(q, dtype=np.float32) / np.float32(q)))).astype(np.float32)
    a = (t // 64).astype(np.float32)[:, None] * f
    b = (t % 64).astype(np.float32)[:, None] * f
    return np.concatenate([np.sin(a), np.cos(a), np.sin(b), np.cos(b)], 1).astype(np.float32)


_INS = ("x_prompt", "x_sample", "state_rwkv", "c", "c_ctx", "ada_w", "ada_b", "norm1_g", "w_in", "tshift_mu",
        "decay_w0", "decay_lora_b", "iclr_a0", "iclr_lora_b", "key_k", "key_a", "bonus_r_k", "gate_lora_b",
        "gn_g", "gn_b", "conv_dw_w", "conv_dw_b", "conv_ln_g", "conv_ln_b", "w_out", "norm2_g",
        "router_group_w", "router_group_b", "router_expert_w", "router_expert_b",
        "expert_w_gate", "expert_w_up", "expert_w_down", "final_norm_g")
_OUTS = (("y_prompt", (1, TP, D)), ("y_sample", (1, TS, D)), ("new_state", (1, 1, 2, 8, C, C)))


def kernel(**inputs):
    import numpy as np
    import concourse.bacc as bacc
    from concourse.bass_utils import run_bass_kernel_spmd

    nc = bacc.Bacc("TRN2", target_bir_lowering=False, num_devices=1)
    arrays = {f"in_{name}": np.ascontiguousarray(inputs[name]) for name in _INS}
    arrays["table_constants"] = _constants()
    arrays["table_positions"] = _positions()
    aps = {name: nc.dram_tensor(name, a.shape, mybir.dt.from_np(a.dtype), kind="ExternalInput").ap()
           for name, a in arrays.items()}
    outs = {name: nc.dram_tensor(f"out_{name}", shape, F32, kind="ExternalOutput").ap() for name, shape in _OUTS}
    build(nc, {name: aps[f"in_{name}"] for name in _INS}, aps["table_constants"], aps["table_positions"], outs)
    results = run_bass_kernel_spmd(nc, [arrays], core_ids=[0]).results[0]
    return tuple(results[f"out_{name}"] for name, _ in _OUTS)
```

```python
from contextlib import ExitStack

import concourse.bass as bass
from concourse import mybir

F32 = mybir.dt.float32
I32 = mybir.dt.int32
U32 = mybir.dt.uint32
ALU = mybir.AluOpType
ACT = mybir.ActivationFunctionType
AX_X = mybir.AxisListType.X

P = 128
D = 1024
KD = D // P
TP, TS = 128, 512
T = TP + TS
TILES = T // P
DR = 512
PAIRS = DR // P
C = 64
LORA_COL = 3 * DR
IN_COLS = 2816
CONV_COL = LORA_COL + 256
CW = 31
NEXP, NGRP, EPG, DE = 32, 4, 8, 256
RMS_EPS, LN_EPS, GN_EPS = 1e-6, 1e-5, 64e-5
KAPPA = 0.6065306597126334

ZT = T + 3
ZP, ZS = 1, TP + 2
UT = T + 45
UP, US = 15, TP + 30
CT = T + 15

PAR_ROWS = [("mu", 26), ("w0", 8), ("a0", 8), ("kk", 8), ("ka", 8), ("rk", 8), ("gng", 4), ("gnb", 4),
            ("cb", 4), ("clg", 4), ("clb", 4), ("n1g", 8)]
PAR = {}
_at = 0
for _name, _n in PAR_ROWS:
    PAR[_name] = _at
    _at += _n
NPAR = _at

CONSTS = [("ident", 128), ("headones", 128), ("ones", 128), ("gmask", 128), ("scanmask", 512),
          ("before", 128), ("expiota", 32), ("lanes", 8), ("ovi", 16)]
COFF = {}
_at = 0
for _name, _n in CONSTS:
    COFF[_name] = _at
    _at += _n
NCONST = _at


class Chain:

    def __init__(self, eng, sem):
        self.eng, self.sem, self.n = eng, sem, 0

    def __call__(self, ins):
        self.n += 1
        ins.then_inc(self.sem, 1)
        self.eng.wait_ge(self.sem, self.n)

    def announce(self, ins, sem, n):
        ins.then_inc(sem, 1)
        self.eng.wait_ge(sem, n)


def build(nc, ins, consts, pos, outs):
    ctx = ExitStack()
    with ctx:
        def sem(name):
            return ctx.enter_context(nc.semaphore(name))

        def dram(name, shape, dt=F32):
            return nc.dram_tensor(name, shape, dt, kind="Internal").ap()

        ARENA = 53200
        arena = ctx.enter_context(nc.sbuf_tensor("arena", [P, ARENA], F32))
        psum = [ctx.enter_context(nc.psum_tensor(f"bank{i}", [P, 512], F32)) for i in range(8)]

        def view(off, *shape):
            n = 1
            for s in shape:
                n *= s
            v = arena[:, off:off + n]
            if len(shape) == 2:
                v = v.rearrange("p (a b) -> p a b", b=shape[1])
            if len(shape) == 3:
                v = v.rearrange("p (a b c) -> p a b c", b=shape[1], c=shape[2])
            return v

        class Region:
            def __init__(self, start, end=ARENA):
                self.at, self.end = start, end

            def take(self, *shape):
                n = 1
                for s in shape:
                    n *= s
                off = self.at
                self.at += n
                assert self.at <= self.end, (self.at, self.end)
                return view(off, *shape)

        keep = Region(0)
        cst = keep.take(NCONST)
        par = keep.take(NPAR)
        convw = keep.take(CW * 4)
        oneminus = keep.take(34)
        condT = keep.take(16)
        modcol = keep.take(2, 16)
        small = keep.take(32)
        lorab = keep.take(2, DR)

        def const(name):
            return cst[:, COFF[name]:COFF[name] + dict(CONSTS)[name]]

        ident, headones, ones = const("ident"), const("headones"), const("ones")
        n1g = par[:, PAR["n1g"]:PAR["n1g"] + 8]

        regz = Region(keep.at)
        zbase = regz.at
        zrkv = regz.take(3 * PAIRS, ZT)
        zlora = regz.take(ZT)
        xlora = regz.take(2, T)
        ysum = regz.take(PAIRS, T)
        wbase = regz.at

        regw = Region(wbase)
        w_in = regw.take(KD, IN_COLS)
        hT = regw.take(KD, T)
        modblk = regw.take(3, 512)
        adab = regw.take(3, 512)
        rows = regw.take(3, P)
        parrow, convrow, crow = rows[:, 0, :], rows[:, 1, :], rows[:, 2, :]
        sqr = regw.take(D)
        gbuf = regw.take(T)
        convbuf = regw.take(2, T)
        rega = Region(zbase, wbase)
        adaw = rega.take(2, KD * 512)
        xt = rega.take(2, D)
        post = rega.take(D)

        modrows = dram("modrows", [2, 6 * D])
        uconv, gsigd = dram("uconv", [4, P, T]), dram("gate_sigmoids", [P, T])

        s_const, s_rows, s_lora = sem("constants_landed"), sem("rows_landed"), sem("lora_landed")
        s_adaw = [sem(f"ada_block_landed{b}") for b in range(2)]
        s_adab = [sem(f"ada_bias_landed{b}") for b in range(3)]
        s_win = [sem(f"w_in_landed{b}") for b in range(6)]
        s_xt = [sem(f"tokens_landed{b}") for b in range(2)]
        s_pos = sem("positions_landed")
        s_modst = [sem(f"mod_block_stored{b}") for b in range(3)]
        s_ust = [sem(f"conv_input_stored{b}") for b in range(2)]
        d_self, a_self, g_self = sem("vector_step"), sem("scalar_step"), sem("pool_step")
        s_silu, s_gst = sem("cond_silu_done"), sem("gate_sigmoids_stored")
        s_rowsT = sem("rows_transposed")
        s_condT = sem("cond_columns_ready")
        s_adamm = sem("ada_block_summed")
        s_modblk = sem("mod_block_ready")
        s_modT = sem("mod_columns_transposed")
        s_modcol = sem("mod_columns_ready")
        s_posadd, s_xstat = sem("position_added"), sem("square_sum_ready")
        s_var, s_std, s_xn = sem("variance_ready"), sem("deviation_ready"), sem("tokens_normed")
        s_xT = sem("tokens_transposed")
        s_hTa, s_hTd = sem("hT_low_ready"), sem("hT_high_ready")
        s_zmm = sem("z_tile_summed")
        s_zeva, s_zevd = sem("z_tile_taken_by_scalar"), sem("z_tile_taken_by_vector")
        s_pads = sem("pads_zeroed")
        block = ctx.enter_context(nc.Block())

        def tok_src(i):
            return ins["x_prompt"][0] if i == 0 else ins["x_sample"][0, (i - 1) * P:i * P, :]

        WIN_BLOCKS = [(1536, 1792), (0, 512), (512, 1024), (1024, 1536), (1792, 2304), (2304, 2816)]
        ZTILES = [("lora", 12, 0), ("gate", 13, 0)]
        ZTILES += [(("r", "k", "v")[m], 4 * m + j, 1 + m) for m in range(3) for j in range(4)]
        ZTILES += [(n, 14 + j + 4 * (n == "cb"), 5) for j in range(4) for n in ("cb", "ca")]
        HALF = T // 2

        def sp_front():
            sp = nc.sync
            sp.dma_start(cst, consts).then_inc(s_const, 16)
            sp.dma_start(crow[0:8, :], ins["c_ctx"].rearrange("(k p) -> k p", p=P)).then_inc(s_rows, 16)
            sp.dma_start(crow[8:16, :], ins["c"][0].rearrange("(k p) -> k p", p=P)).then_inc(s_rows, 16)

            def ada_block(n):
                if n >= 2:
                    sp.wait_ge(s_adamm, n - 1)
                sp.dma_start(adaw[:, n % 2].rearrange("p (k n) -> p k n", k=KD),
                             ins["ada_w"][0, :, n * 512:(n + 1) * 512].rearrange("(k p) n -> p k n", p=P)
                             ).then_inc(s_adaw[n % 2], 16)
                if n >= 3:
                    sp.wait_ge(s_modblk, n - 2)
                sp.dma_start(adab[0:2, n % 3],
                             ins["ada_b"][0:1, n * 512:(n + 1) * 512].broadcast_to([2, 512])
                             ).then_inc(s_adab[n % 3], 16)

            def token_tile(i):
                if i >= 2:
                    sp.wait_ge(s_xT, i - 1)
                sp.dma_start(xt[:, i % 2], tok_src(i)).then_inc(s_xt[i % 2], 16)
                if i >= 1:
                    if i >= 2:
                        sp.wait_ge(s_posadd, i - 1)
                    sp.dma_start(post, pos[(i - 1) * P:i * P, :]).then_inc(s_pos, 16)

            def win_block(b):
                lo, hi = WIN_BLOCKS[b]
                sp.dma_start(w_in[:, :, lo:hi], ins["w_in"][0, :, lo:hi].rearrange("(k p) n -> p k n", p=P)
                             ).then_inc(s_win[b], 16)

            ada_block(0)
            ada_block(1)
            token_tile(0)
            token_tile(1)
            for n in range(2, 6):
                ada_block(n)
            win_block(0)
            for i in range(2, TILES):
                token_tile(i)
                ada_block(4 + i)
            win_block(1)
            for n in range(4 + TILES, 12):
                ada_block(n)
            for b in range(2, 6):
                win_block(b)

        def act_front():
            act, chain = nc.scalar, Chain(nc.scalar, a_self)
            at = 0
            for name, src in [("tshift_mu", "o (a b) -> (o a) b"), ("decay_w0", "o (a b) -> (o a) b"),
                              ("iclr_a0", "o (a b) -> (o a) b"), ("key_k", "o (a b) -> (o a) b"),
                              ("key_a", "o (a b) -> (o a) b"), ("bonus_r_k", None), ("gn_g", 1), ("gn_b", 1),
                              ("conv_dw_b", 1), ("conv_ln_g", 1), ("conv_ln_b", 1), ("norm1_g", 1)]:
                a = ins[name][0]
                if name == "bonus_r_k":
                    a = a.rearrange("o (j h) d -> (o j) (h d)", h=2)
                elif src == 1:
                    a = a.rearrange("(a b) -> a b", b=P)
                else:
                    a = a.rearrange(src, b=P)
                act.dma_start(parrow[at:at + a.shape[0], :], a).then_inc(s_rows, 16)
                at += a.shape[0]
            assert at == NPAR
            act.dma_start(convrow[0:CW * 4, :], ins["conv_dw_w"][0].rearrange("t (j p) -> (t j) p", p=P)
                          ).then_inc(s_rows, 16)
            act.dma_start(lorab[0:64], ins["decay_lora_b"][0].rearrange("o l c -> l o c")).then_inc(s_lora, 16)
            act.dma_start(lorab[64:128], ins["iclr_lora_b"][0].rearrange("o l c -> l o c")).then_inc(s_lora, 16)
            act.wait_ge(s_rows, ROWS_ALL)
            nc.scalar.activation(crow[0:16, :], crow[0:16, :], ACT.Silu).then_inc(s_silu, 1)
            def square_sum(i):
                act.wait_ge(s_xt[i % 2], 16 * (i // 2 + 1))
                if i:
                    act.wait_ge(s_posadd, i)
                chain.announce(nc.scalar.activation(sqr, xt[:, i % 2], ACT.Square, accum_out=small[:, i:i + 1]),
                             s_xstat, i + 1)
                act.wait_ge(s_var, i + 1)
                nc.scalar.activation(small[:, 8 + i:9 + i], small[:, i:i + 1], ACT.Sqrt).then_inc(s_std, 1)

            square_sum(0)
            for i in range(TILES):
                if i + 1 < TILES:
                    square_sum(i + 1)
                act.wait_ge(s_xT, i + 1)
                act.wait_ge(s_modcol, 1)
                cond = int(i > 0)
                for k in range(4):
                    last = nc.scalar.activation(hT[:, k, i * P:(i + 1) * P], psum[6][:, k * P:(k + 1) * P],
                                                ACT.Identity, bias=modcol[:, 0, 2 * k + cond:2 * k + cond + 1],
                                                scale=modcol[:, 1, 2 * k + cond:2 * k + cond + 1])
                    if k < 3:
                        last.then_inc(a_self, 1)
                        chain.n += 1
                last.then_inc(s_hTa, 1)
            for n, (kind, tile, _) in enumerate(ZTILES):
                act.wait_ge(s_zmm, n + 1)
                lo = psum[2 * (n % 2)]
                hi = psum[2 * (n % 2) + 1]
                if kind == "gate":
                    chain(nc.scalar.activation(gbuf[:, 0:HALF], lo[:, 0:HALF], ACT.Sigmoid))
                    chain.announce(nc.scalar.activation(gbuf[:, HALF:T], hi[:, 0:HALF], ACT.Sigmoid), s_zeva, n + 1)
                    act.dma_start(gsigd, gbuf).then_inc(s_gst, 16)
                elif kind == "cb":
                    b = (n // 2) % 2
                    if n >= 18:
                        act.wait_ge(s_ust[b], 16 * ((n - 14) // 4))
                    chain(nc.scalar.activation(convbuf[:, b, 0:HALF], lo[:, 0:HALF], ACT.Sigmoid))
                    nc.scalar.activation(convbuf[:, b, HALF:T], hi[:, 0:HALF], ACT.Sigmoid).then_inc(s_zeva, 1)
                elif kind == "ca":
                    act.wait_ge(s_zevd, n + 1)
                    act.dma_start(uconv[tile - 14], convbuf[:, (n // 2) % 2, :]).then_inc(s_ust[(n // 2) % 2], 16)
                    act.sem_inc(s_zeva, 1)
                else:
                    dst = zlora if kind == "lora" else zrkv[:, tile, :]
                    chain(nc.scalar.activation(dst[:, ZP:ZP + TP], lo[:, 0:TP], ACT.Copy))
                    nc.scalar.activation(dst[:, ZS:ZS + HALF - TP], lo[:, TP:HALF], ACT.Copy).then_inc(s_zeva, 1)
            act.wait_ge(s_zeva, len(ZTILES))
            return chain

        ROWS_ALL = 16 * 15

        def dve_front():
            dve, chain = nc.vector, Chain(nc.vector, d_self)
            dve.wait_ge(s_rowsT, 1)
            chain.announce(nc.vector.tensor_copy(condT, psum[4][:, 0:16]), s_condT, 1)
            chain(nc.vector.tensor_copy(par, psum[2][:, 0:NPAR]))
            chain(nc.vector.tensor_copy(convw, psum[3][:, 0:CW * 4]))
            chain(nc.vector.tensor_scalar(oneminus[:, 0:26], par[:, 0:26], -1.0, 1.0, ALU.mult, ALU.add))
            chain(nc.vector.tensor_scalar(oneminus[:, 26:34], par[:, PAR["ka"]:PAR["ka"] + 8], -1.0, 1.0,
                                          ALU.mult, ALU.add))

            def mod_block(n):
                dve.wait_ge(s_adamm, n + 1)
                dve.wait_ge(s_adab[n % 3], 16 * (n // 3 + 1))
                if n >= 3:
                    dve.wait_ge(s_modst[n % 3], 16 * (n // 3))
                chain.announce(nc.vector.tensor_tensor(modblk[0:2, n % 3], psum[n % 2][0:2, :], adab[0:2, n % 3],
                                                     ALU.add), s_modblk, n + 1)

            for n in range(4):
                mod_block(n)
            dve.wait_ge(s_modT, 4)
            chain(nc.vector.tensor_copy(modcol[:, 0], psum[5][:, 0:16]))
            chain.announce(nc.vector.scalar_tensor_tensor(
                modcol[:, 1].rearrange("p (k c) -> p k c", c=2), psum[5][:, 16:32].rearrange("p (k c) -> p k c", c=2),
                1.0, n1g.unsqueeze(2).broadcast_to([P, 8, 2]), ALU.add, ALU.mult), s_modcol, 1)

            def normed(i):
                x = xt[:, i % 2]
                if i:
                    dve.wait_ge(s_xt[i % 2], 16 * (i // 2 + 1))
                    dve.wait_ge(s_pos, 16 * i)
                    chain.announce(nc.vector.tensor_tensor(x, x, post, ALU.add), s_posadd, i)
                dve.wait_ge(s_xstat, i + 1)
                chain.announce(nc.vector.tensor_scalar(small[:, i:i + 1], small[:, i:i + 1], 1.0 / D, RMS_EPS,
                                                     ALU.mult, ALU.add), s_var, i + 1)
                dve.wait_ge(s_std, i + 1)
                chain(nc.vector.reciprocal(small[:, 16 + i:17 + i], small[:, 8 + i:9 + i]))
                chain.announce(nc.vector.tensor_scalar(x, x, small[:, 16 + i:17 + i], None, ALU.mult), s_xn, i + 1)

            normed(0)
            for i in range(TILES):
                mod_block(4 + i)
                if i + 1 < TILES:
                    normed(i + 1)
                dve.wait_ge(s_xT, i + 1)
                cond = int(i > 0)
                for k in range(4, 8):
                    last = nc.vector.tensor_scalar(hT[:, k, i * P:(i + 1) * P], psum[7][:, (k - 4) * P:(k - 3) * P],
                                                   modcol[:, 1, 2 * k + cond:2 * k + cond + 1],
                                                   modcol[:, 0, 2 * k + cond:2 * k + cond + 1], ALU.mult, ALU.add)
                    if k < 7:
                        chain(last)
                chain.announce(last, s_hTd, i + 1)
            for n in range(4 + TILES, 12):
                mod_block(n)
            for z in [zrkv[:, j, :] for j in range(12)] + [zlora]:
                for c in (0, TP + 1, ZT - 1):
                    last = nc.vector.memset(z[:, c:c + 1], 0.0)
                    chain(last)
            for n, (kind, tile, _) in enumerate(ZTILES):
                dve.wait_ge(s_zmm, n + 1)
                lo, hi = psum[2 * (n % 2)], psum[2 * (n % 2) + 1]
                if kind in ("gate", "cb"):
                    dve.sem_inc(s_zevd, 1)
                elif kind == "ca":
                    dve.wait_ge(s_zeva, n)
                    u = convbuf[:, (n // 2) % 2]
                    chain(nc.vector.tensor_tensor(u[:, 0:HALF], u[:, 0:HALF], lo[:, 0:HALF], ALU.mult))
                    chain.announce(nc.vector.tensor_tensor(u[:, HALF:T], u[:, HALF:T], hi[:, 0:HALF], ALU.mult),
                                 s_zevd, n + 1)
                else:
                    dst = zlora if kind == "lora" else zrkv[:, tile, :]
                    chain.announce(nc.vector.tensor_copy(dst[:, ZS + HALF - TP:ZS + TS], hi[:, 0:HALF]),
                                 s_zevd, n + 1)
            return chain

        def pool_front():
            for n in range(12):
                nc.gpsimd.wait_ge(s_modblk, n + 1)
                nc.gpsimd.dma_start(modrows[:, n * 512:(n + 1) * 512], modblk[0:2, n % 3]).then_inc(s_modst[n % 3], 16)

        def pe_front():
            pe = nc.tensor
            pe.wait_ge(s_const, 16)
            pe.wait_ge(s_silu, 1)
            nc.tensor.transpose(psum[2][:, 0:NPAR], parrow[0:NPAR, :], ident[0:NPAR, 0:NPAR])
            nc.tensor.transpose(psum[3][:, 0:CW * 4], convrow[0:CW * 4, :], ident[0:CW * 4, 0:CW * 4])
            nc.tensor.transpose(psum[4][:, 0:16], crow[0:16, :], ident[0:16, 0:16]).then_inc(s_rowsT, 1)
            pe.wait_ge(s_condT, 1)

            def ada_block(n):
                pe.wait_ge(s_adaw[n % 2], 16 * (n // 2 + 1))
                if n >= 2:
                    pe.wait_ge(s_modblk, n - 1)
                w = adaw[:, n % 2].rearrange("p (k n) -> p k n", k=KD)
                for k in range(KD):
                    mm = nc.tensor.matmul(psum[n % 2][0:2, :], condT[:, k:16:8], w[:, k, :],
                                          start=(k == 0), stop=(k == KD - 1))
                mm.then_inc(s_adamm, 1)

            def mod_columns(n):
                pe.wait_ge(s_modblk, n + 1)
                for j in range(4):
                    at = 2 * (4 * n + j)
                    mm = nc.tensor.transpose(psum[5][:, at:at + 2], modblk[0:2, n % 3, j * P:(j + 1) * P],
                                             ident[0:2, 0:2])
                mm.then_inc(s_modT, 1)

            def transpose_tile(i):
                pe.wait_ge(s_xn, i + 1)
                if i:
                    pe.wait_ge(s_hTa, i)
                    pe.wait_ge(s_hTd, i)
                for k in range(KD):
                    mm = nc.tensor.transpose(psum[6 + k // 4][:, (k % 4) * P:(k % 4 + 1) * P],
                                             xt[:, i % 2, k * P:(k + 1) * P], ident)
                mm.then_inc(s_xT, 1)

            for n in range(4):
                ada_block(n)
                if n:
                    mod_columns(n - 1)
            mod_columns(3)
            ada_block(4)
            for i in range(TILES):
                transpose_tile(i)
                ada_block(5 + i)
            for n in range(5 + TILES, 12):
                ada_block(n)
            pe.wait_ge(s_hTa, TILES)
            pe.wait_ge(s_hTd, TILES)
            pe.wait_ge(s_modblk, 12)
            for n, (kind, tile, wb) in enumerate(ZTILES):
                for b in (wb, 4) if kind in ("ca", "cb") else (wb,):
                    pe.wait_ge(s_win[b], 16)
                if n >= 2:
                    pe.wait_ge(s_zeva, n - 1)
                    pe.wait_ge(s_zevd, n - 1)
                for half in range(2):
                    for k in range(KD):
                        mm = nc.tensor.matmul(psum[2 * (n % 2) + half][:, 0:HALF], w_in[:, k, tile * P:(tile + 1) * P],
                                              hT[:, k, half * HALF:(half + 1) * HALF],
                                              start=(k == 0), stop=(k == KD - 1))
                mm.then_inc(s_zmm, 1)

        GC = 16
        COLS = GC * C
        regr = Region(wbase)
        XR, XK, SG, AV, CS, T0 = (regr.take(COLS) for _ in range(6))
        E1 = regr.take(GC, C + 1)
        VP = regr.take(C + COLS)
        BK = regr.take(GC, 2 * C)
        EI = SG
        KN = CS
        inva, invb = regr.take(COLS), regr.take(COLS)
        UL = inva.rearrange("p (s t) -> p s t", t=32)
        WI, WTMP = (x.rearrange("p (s j) -> p s j", j=16) for x in (invb[:, 0:512], invb[:, 512:1024]))
        WB = invb.rearrange("p (n q j) -> p n q j", q=2, j=16)
        TA = Y1 = inva.rearrange("p (n t) -> p n t", t=32)
        AR = [regr.take(GC, 2 * C) for _ in range(2)]
        BKT = [regr.take(GC, P) for _ in range(2)]
        SAV = [regr.take(GC, P) for _ in range(2)]
        GM = [regr.take(2 * GC, 2 * C) for _ in range(2)]
        PC = [regr.take(GC) for _ in range(2)]
        ST = regr.take(2, 8, C)
        SP_ = regr.take(8, C)
        S0 = zlora[:, 0:8 * C].rearrange("p (a b) -> p a b", b=C)
        XS = regr.take(2 * 8 * C)
        SL = XS.rearrange("p (a b) -> p a b", b=P)
        uin = regr.take(UT)
        cacc = regr.take(CT)
        cprod = regr.take(2, CT)

        wout = view(zbase, KD, D)
        gateb, gsig = view(zbase + 3 * PAIRS * ZT + ZT, DR), view(zbase + 3 * PAIRS * ZT + ZT + DR, T)
        s_wout, s_gateb = sem("w_out_landed"), sem("gate_lora_landed")

        udiag = dram("udiag", [5, 64, 1024])
        winv = dram("winv", [5, 2, 64, 512])
        cout = dram("conv_out", [4, P, CT])

        UNITS = [[(d, j, ZS, TS, (j - j0) * TS) for j in (j0, j0 + 1)] for d in range(2) for j0 in (0, 2)]
        UNITS.append([(d, j, ZP, TP, (4 * d + j) * TP) for d in range(2) for j in range(4)])
        NU = len(UNITS)

        def steps(u):
            return 2 if u == NU - 1 else 8

        def step_at(u, i):
            return 8 * u + i

        def chunks(u, i):
            return list(range(i, GC, steps(u)))

        def pcol(name, d, j):
            c = PAR[name] + 4 * d + j
            return par[:, c:c + 1]

        def current(z, seg):
            d, _, off, n, _ = seg
            return z[:, off:off + n][:, ::-1] if d else z[:, off:off + n]

        def previous(z, seg):
            d, _, off, n, _ = seg
            return z[:, off + 1:off + 1 + n][:, ::-1] if d else z[:, off - 1:off - 1 + n]

        def halves(u):
            return [[s for s in UNITS[u] if s[4] // 512 == h] for h in range(2)]

        EARLY = ["shift_r", "shift_k", "shift_v", "lora_w", "lora_a", "square", "scan", "norm", "exp", "kn", "kp"]
        FILL = ["ar", "bk", "gram0", "gram1", "gram2", "gram3", "invload", "bonus", "scale", "turn_bk", "turn_v", "mv"]
        INVERT = ["inv0", "inv1", "inv2", "inv3", "inv4", "invstore", "place", "merge_y", "merge_z"]
        CHAIN = ["X", "T", "S", "Y"]
        ENGINES = ("pe", "act", "dve", "sp", "pool")
        PLACES = {
            "ar": (-0.122, -0.167, -0.029, -0.109, -0.119),
            "bk": (0.131, -0.081, 0.057, -0.107, -0.084),
            "gram0": (0.154, -0.035, 0.128, 0.039, -0.037),
            "gram1": (0.189, 0.074, 0.146, 0.072, -0.024),
            "gram2": (0.198, 0.111, 0.161, 0.143, 0.080),
            "gram3": (0.240, 0.220, 0.199, 0.152, 0.232),
            "invload": (0.278, 0.260, 0.215, 0.182, 0.239),
            "bonus": (0.306, 0.301, 0.264, 0.245, 0.247),
            "scale": (0.309, 0.351, 0.365, 0.272, 0.252),
            "turn_bk": (0.353, 0.364, 0.395, 0.280, 0.322),
            "turn_v": (0.381, 0.383, 0.455, 0.349, 0.398),
            "mv": (0.456, 0.472, 0.800, 0.398, 0.435),
            "inv0": (0.452, 0.301, 0.319, 0.429, 0.347),
            "inv1": (0.552, 0.519, 0.376, 0.523, 0.479),
            "inv2": (0.566, 0.593, 0.383, 0.537, 0.518),
            "inv3": (0.626, 0.597, 0.534, 0.724, 0.649),
            "inv4": (0.646, 0.602, 0.707, 0.739, 0.736),
            "invstore": (0.688, 0.701, 0.782, 0.889, 0.748),
            "place": (0.923, 0.815, 0.808, 0.976, 0.879),
            "merge_y": (0.961, 0.886, 0.925, 1.053, 0.979),
            "merge_z": (1.014, 0.937, 0.987, 1.060, 0.991),
            "shift_r": (0.432, 0.384, 0.477, 0.352, 0.452),
            "shift_k": (0.438, 0.393, 0.517, 0.398, 0.456),
            "shift_v": (0.486, 0.502, 0.592, 0.446, 0.467),
            "lora_w": (0.563, 0.520, 0.623, 0.482, 0.546),
            "lora_a": (0.569, 0.573, 0.651, 0.549, 0.547),
            "square": (0.572, 0.594, 0.689, 0.572, 0.561),
            "scan": (0.584, 0.644, 0.692, 0.604, 0.641),
            "norm": (0.666, 0.696, 0.695, 0.689, 0.665),
            "exp": (0.681, 0.749, 0.738, 0.701, 0.681),
            "kn": (0.768, 0.807, 0.778, 0.748, 0.827),
            "kp": (0.824, 0.817, 0.886, 0.765, 0.845),
            "X": (0.238, 0.396, -0.015, 0.869, 0.501),
            "T": (0.519, 0.404, 0.135, 0.886, 0.740),
            "S": (0.989, 0.727, 0.687, 1.263, 0.947),
            "Y": (1.027, 0.744, 0.832, 1.461, 1.292),
        }
        TAP_PLACES = (-0.93, 4.39)
        TAPS = [(j, k) for j in range(4) for k in range(CW)]

        def order(engine):
            col = ENGINES.index(engine)
            placed = [(u - 2 + PLACES[ev][col], (ev, u, 0)) for u in range(NU) for ev in EARLY]
            placed += [(u - 1 + PLACES[ev][col], (ev, u, 0)) for u in range(NU) for ev in FILL + INVERT]
            placed += [(u + (i + PLACES[ev][col]) / steps(u), (ev, u, i))
                       for u in range(NU) for i in range(steps(u)) for ev in CHAIN]
            if engine in ("act", "pool"):
                lo, hi = TAP_PLACES
                placed += [(lo + (hi - lo) * n / len(TAPS), ("tap", j, k)) for n, (j, k) in enumerate(TAPS)]
            return [("init", 0, 0)] + [e for _, e in sorted(placed, key=lambda x: x[0])] + [("final", NU - 1, 0)]

        def by_scalar(k):
            return k % 2 == 1

        def scalar_taps(j, k):
            return j * (CW // 2) + k // 2

        USES = {"lora_w": [("lw0", 0), ("lw1", 1)], "lora_a": [("la0", 2), ("la1", 3)],
                "norm": [("n0", 0), ("n1", 1)],
                "gram0": [("g0", 0), ("g1", 1)], "gram1": [("g2", 2), ("g3", 3)],
                "gram2": [("g4", 0), ("g5", 1)], "gram3": [("g6", 2), ("g7", 3)],
                "bonus": [("b0", 2), ("b1", 3)], "turn_bk": [(f"t{q}", q) for q in range(4)],
                "turn_v": [(f"v{q}", q) for q in range(4)], "mv": [(f"m{q}", q) for q in range(4)],
                "place": [("ta0", 0), ("ta1", 1)], "merge_y": [("y0", 2), ("y1", 3)],
                "merge_z": [("z0", 0), ("z1", 1)]}
        BANK = {use: bank for uses in USES.values() for use, bank in uses}
        FILLED, READ = {}, {}
        for _ev, _u, _ in order("pe"):
            for _use, _bank in USES.get(_ev, ()):
                FILLED[_u, _use] = len(FILLED) + 1
                READ[_u, _use] = 1 + sum(BANK[x] == _bank for _, x in READ)

        def read_count(u, use):
            return READ[u, use]

        s_read = [sem(f"prep_bank_read{b}") for b in range(4)]

        def wait_read(eng, u, use):
            eng.wait_ge(s_read[BANK[use]], read_count(u, use))

        def wait_free(pe, u, use):
            if read_count(u, use) > 1:
                pe.wait_ge(s_read[BANK[use]], read_count(u, use) - 1)

        s_summed = sem("prep_bank_filled")

        def wait_filled(eng, u, use):
            eng.wait_ge(s_summed, FILLED[u, use])

        s_shiftA = sem("shift_scaled")
        s_shiftD = sem("shift_done")
        s_xlA, s_xlD, s_xl = sem("lora_shift_scaled"), sem("lora_shift_done"), sem("lora_input_ready")
        s_sq, s_cs, s_exp, s_rk = sem("squares_ready"), sem("log_decay_summed"), sem("decays_ready"), sem("rk_ready")
        s_ar, s_bk, s_bkh = sem("ar_ready"), sem("bk_ready"), sem("bk_scaled")
        s_ud, s_ul, s_wd, s_wb = sem("udiag_stored"), sem("udiag_loaded"), sem("winv_stored"), sem("winv_loaded")
        s_inv = sem("inverse_done")
        s_wcopy = sem("inverse_blocks_placed")
        s_sl, s_slT, s_s0 = sem("states_loaded"), sem("states_turned"), sem("initial_states_ready")
        s_X, s_XS, s_SA, s_SAS = sem("x_summed"), sem("x_taken"), sem("removals_summed"), sem("removals_taken")
        s_S, s_ST, s_Y, s_YS = sem("state_summed"), sem("state_ready"), sem("y_summed"), sem("y_added")
        s_fin, s_finc, s_finst = sem("final_states_turned"), sem("final_states_taken"), sem("final_states_stored")
        s_uin, s_cprod, s_cadd = sem("conv_tile_loaded"), sem("conv_products_ready"), sem("conv_products_added")
        s_cacc, s_cst = sem("conv_tile_done"), sem("conv_tile_stored")

        NZ = len(ZTILES)

        def sp_mix():
            sp = nc.sync
            sp.wait_ge(s_zmm, NZ)
            sp.wait_ge(s_ust[0], 32)
            sp.wait_ge(s_ust[1], 32)
            sp.wait_ge(s_gst, 16)
            for b in range(3):
                sp.wait_ge(s_modst[b], 64)
            for a in range(8):
                sp.dma_start(SL[0:64, a].rearrange("v (h k) -> v h k", h=2),
                             ins["state_rwkv"][0, 0, a // 4, 2 * (a % 4):2 * (a % 4) + 2].rearrange("h v k -> v h k")
                             ).then_inc(s_sl, 16)
            for ev, u, i in order("sp"):
                if ev == "gram3":
                    wait_read(sp, u, "g7")
                    for r in range(3):
                        wait_read(sp, u, f"g{4 + r}")
                    for b in range(2):
                        sp.dma_start(udiag[u, 32 * b:32 * b + 32].rearrange("n (s t) -> s n t", t=32),
                                     GM[u % 2][32 * b:32 * b + 32, :, 32 * b:32 * b + 32]).then_inc(s_ud, 16)
                elif ev == "invload":
                    sp.wait_ge(s_ud, 32 * (u + 1))
                    if u:
                        wait_read(sp, u - 1, "z0")
                        wait_read(sp, u - 1, "z1")
                    for q in range(2):
                        sp.dma_start(UL[64 * q:64 * q + 64].rearrange("p s t -> p (s t)"), udiag[u]
                                     ).then_inc(s_ul, 16)
                elif ev == "invstore":
                    sp.wait_ge(s_inv, u + 1)
                    sp.dma_start(winv[u].rearrange("q n f -> (q n) f"), WI.rearrange("p s j -> p (s j)")
                                 ).then_inc(s_wd, 16)
                    sp.wait_ge(s_wd, 16 * (u + 1))
                    for b in range(2):
                        for q in range(2):
                            sp.dma_start(WB[32 * b:32 * b + 32, :, q, :],
                                         winv[u, q, 32 * b:32 * b + 32].rearrange("n (s j) -> s n j", j=16)
                                         ).then_inc(s_wb, 16)
                elif ev == "final":
                    for use in ("la0", "la1"):
                        wait_read(sp, u, use)
                    sp.dma_start(gateb, ins["gate_lora_b"][0]).then_inc(s_gateb, 16)
                    sp.dma_start(gsig, gsigd).then_inc(s_gateb, 16)
                    sp.wait_ge(s_shiftD, 3 * NU)
                    sp.wait_ge(s_shiftA, 3 * NU)
                    sp.wait_ge(s_ST, step_at(NU - 2, 0) + NU - 1)
                    sp.dma_start(wout, ins["w_out"][0].rearrange("(k p) n -> p k n", p=P)).then_inc(s_wout, 16)
                    sp.wait_ge(s_finc, 1)
                    for a in range(8):
                        sp.dma_start(outs["new_state"][0, 0, a // 4, 2 * (a % 4):2 * (a % 4) + 2]
                                     .rearrange("h v k -> v h k"),
                                     SL[0:64, a].rearrange("v (h k) -> v h k", h=2)).then_inc(s_finst, 16)

        def act_mix(chain):
            act = nc.scalar
            act.wait_ge(s_zevd, NZ)
            for d in range(2):
                for n, (off, ln, at) in enumerate([(ZP, TP, 0), (ZS, TS, TP)]):
                    seg = (d, 0, off, ln, 0)
                    c = PAR["mu"] + 13 * d + 12
                    chain.announce(nc.scalar.activation(xlora[:, d, at:at + ln], previous(zlora, seg), ACT.Copy,
                                                      scale=par[:, c:c + 1]), s_xlA, 2 * d + n + 1)
            act.wait_ge(s_xlD, 4)
            for d in range(2):
                chain.announce(nc.scalar.activation(xlora[0:64, d], xlora[0:64, d], ACT.Tanh), s_xl, d + 1)
            act.wait_ge(s_zmm, NZ)
            for ev, u, i in order("act"):
                if ev == "tap":
                    j, k = u, i
                    if not by_scalar(k):
                        continue
                    n = scalar_taps(j, k)
                    act.wait_ge(s_uin, 32 * (j + 1))
                    if n:
                        act.wait_ge(s_cadd, n)
                    chain.announce(nc.scalar.activation(cprod[:, 1], uin[:, k:k + CT], ACT.Copy,
                                                        scale=convw[:, 4 * k + j:4 * k + j + 1]), s_cprod, n + 1)
                    continue
                b = u % 2
                segs = UNITS[u]
                if ev in ("shift_r", "shift_k", "shift_v"):
                    m = ("shift_r", "shift_k", "shift_v").index(ev)
                    if m == 0 and u:
                        act.wait_ge(s_ar, u)
                        for use in ("b0", "b1", "v0", "v1", "v2", "v3"):
                            wait_read(act, u - 1, use)
                    X = (XR, XK, VP[:, C:])[m]
                    for n, s in enumerate(segs):
                        c = PAR["mu"] + 13 * s[0] + 4 * m + s[1]
                        ins_ = nc.scalar.activation(X[:, s[4]:s[4] + s[3]], previous(zrkv[:, 4 * m + s[1], :], s),
                                                    ACT.Copy, scale=par[:, c:c + 1])
                        if n < len(segs) - 1:
                            chain(ins_)
                    chain.announce(ins_, s_shiftA, 3 * u + m + 1)
                elif ev in ("lora_w", "lora_a"):
                    for name, dst, bias in ((("lw", SG, "w0"),) if ev == "lora_w" else (("la", AV, "a0"),)):
                        for h, part in enumerate(halves(u)):
                            wait_filled(act, u, f"{name}{h}")
                            for s in part:
                                ins_ = nc.scalar.activation(
                                    dst[:, s[4]:s[4] + s[3]], psum[BANK[f"{name}{h}"]][:, s[4] % 512:s[4] % 512 + s[3]],
                                    ACT.Sigmoid, bias=pcol(bias, s[0], s[1]))
                                if s is not part[-1]:
                                    chain(ins_)
                            chain.announce(ins_, s_read[BANK[f"{name}{h}"]], read_count(u, f"{name}{h}"))
                elif ev == "square":
                    act.wait_ge(s_shiftD, 3 * u + 2)
                    for n, s in enumerate(segs):
                        ins_ = nc.scalar.activation(T0[:, s[4]:s[4] + s[3]], XK[:, s[4]:s[4] + s[3]], ACT.Square,
                                                    scale=pcol("kk", s[0], s[1]))
                        if n < len(segs) - 1:
                            chain(ins_)
                    chain.announce(ins_, s_sq, u + 1)
                elif ev == "norm":
                    for h in range(2):
                        wait_read(act, u, f"n{h}")
                    chain(nc.scalar.activation(T0, T0, ACT.Ln))
                    chain.announce(nc.scalar.activation(T0, T0, ACT.Exp, scale=-0.5), s_exp, 3 * u + 1)
                elif ev == "exp":
                    act.wait_ge(s_cs, u + 1)
                    cs = CS.rearrange("p (g c) -> p g c", c=C)
                    if u == 0:
                        act.wait_ge(s_pads, 1)
                    chain.announce(nc.scalar.activation(E1[:, :, 1:C + 1], cs, ACT.Exp, scale=-KAPPA), s_exp, 3 * u + 2)
                    chain.announce(nc.scalar.activation(EI, CS, ACT.Exp, scale=KAPPA), s_exp, 3 * u + 3)
                elif ev in ("turn_bk", "turn_v"):
                    name = "t" if ev == "turn_bk" else "v"
                    for q in range(4):
                        wait_filled(act, u, f"{name}{q}")
                        src = psum[BANK[f"{name}{q}"]][:, :].rearrange("p (g c) -> p g c", c=P)
                        if name == "t":
                            ins_ = nc.scalar.activation(BKT[b][:, 4 * q:4 * q + 4, :], src, ACT.Copy)
                        else:
                            ins_ = nc.scalar.activation(SAV[b][64:128, 4 * q:4 * q + 4, :], src[64:128], ACT.Copy)
                        chain.announce(ins_, s_read[BANK[f"{name}{q}"]], read_count(u, f"{name}{q}"))
                elif ev == "place":
                    act.wait_ge(s_wb, 64 * (u + 1))
                    for k in range(2):
                        r = slice(32 * k, 32 * k + 32)
                        chain.announce(nc.scalar.activation(
                            GM[b][r, :, 32 * k:32 * k + 32].rearrange("p n (j q) -> p n j q", q=2),
                            WB[r].rearrange("p n q j -> p n j q"), ACT.Copy), s_wcopy, 2 * u + k + 1)
                    for h in range(2):
                        wait_filled(act, u, f"ta{h}")
                        chain.announce(nc.scalar.activation(
                            TA[0:32, 16 * h:16 * h + 16, :],
                            psum[BANK[f"ta{h}"]][0:32, :].rearrange("p (n t) -> p n t", t=32), ACT.Copy),
                            s_read[BANK[f"ta{h}"]], read_count(u, f"ta{h}"))
                elif ev == "mv":
                    for q in range(4):
                        wait_filled(act, u, f"m{q}")
                        h, g0 = q // 2, 8 * (q % 2)
                        chain.announce(nc.scalar.activation(
                            SAV[b][0:64, g0:g0 + 8, C * h:C * h + C],
                            psum[BANK[f"m{q}"]][0:64, :].rearrange("p (n c) -> p n c", c=C), ACT.Copy),
                            s_read[BANK[f"m{q}"]], read_count(u, f"m{q}"))
                elif ev == "T":
                    g, n = step_at(u, i), len(chunks(u, i))
                    act.wait_ge(s_SA, g + 1)
                    for h in range(2):
                        ins_ = nc.scalar.activation(SAV[b][0:64, i::steps(u), C * h:C * h + C],
                                                    psum[6 + h][0:64, 0:n * C].rearrange("p (n c) -> p n c", c=C),
                                                    ACT.Copy)
                        if h == 0:
                            chain(ins_)
                    chain.announce(ins_, s_SAS, g + 1)
                elif ev == "final":
                    act.wait_ge(s_fin, 1)
                    chain(nc.scalar.activation(SL[0:64, 0:4], psum[6][0:64, :].rearrange("p (a b) -> p a b", b=P),
                                               ACT.Copy))
                    chain.announce(nc.scalar.activation(SL[0:64, 4:8], psum[7][0:64, :].rearrange("p (a b) -> p a b", b=P),
                                                      ACT.Copy), s_finc, 1)

        def dve_mix(chain):
            dve = nc.vector

            def gc(x):
                return x.rearrange("p (g c) -> p g c", c=C)

            for k, (d, off, ln, at) in enumerate([(d, *x) for d in range(2) for x in ((ZP, TP, 0), (ZS, TS, TP))]):
                dve.wait_ge(s_zeva, 1)
                dve.wait_ge(s_xlA, k + 1)
                x = xlora[:, d, at:at + ln]
                c = 13 * d + 12
                chain.announce(nc.vector.scalar_tensor_tensor(x, current(zlora, (d, 0, off, ln, 0)), oneminus[:, c:c + 1],
                                                            x, ALU.mult, ALU.add), s_xlD, k + 1)
            dve.wait_ge(s_zmm, NZ)
            dve.wait_ge(s_ust[0], 32)
            dve.wait_ge(s_ust[1], 32)
            chain(nc.vector.memset(VP[:, 0:C], 0.0))
            chain.announce(nc.vector.memset(E1[:, :, 0:1], 1.0), s_pads, 1)
            for ev, u, i in order("dve"):
                b = u % 2
                segs = UNITS[u]
                if ev == "init":
                    dve.wait_ge(s_slT, 1)
                    chain.announce(nc.vector.tensor_copy(S0, psum[5][:, :].rearrange("p (a b) -> p a b", b=C)), s_s0, 1)
                elif ev in ("shift_r", "shift_k", "shift_v"):
                    m = ("shift_r", "shift_k", "shift_v").index(ev)
                    X = (XR, XK, VP[:, C:])[m]
                    dve.wait_ge(s_shiftA, 3 * u + m + 1)
                    for n, s in enumerate(segs):
                        c = 13 * s[0] + 4 * m + s[1]
                        x = X[:, s[4]:s[4] + s[3]]
                        ins_ = nc.vector.scalar_tensor_tensor(x, current(zrkv[:, 4 * m + s[1], :], s),
                                                              oneminus[:, c:c + 1], x, ALU.mult, ALU.add)
                        if n < len(segs) - 1:
                            chain(ins_)
                    chain.announce(ins_, s_shiftD, 3 * u + m + 1)
                elif ev == "scan":
                    for h in range(2):
                        wait_read(dve, u, f"lw{h}")
                        ins_ = nc.vector.tensor_tensor_scan(CS[:, 512 * h:512 * h + 512], const("scanmask"),
                                                            SG[:, 512 * h:512 * h + 512], 0.0, ALU.mult, ALU.add)
                        if h == 0:
                            chain(ins_)
                    chain.announce(ins_, s_cs, u + 1)
                elif ev == "norm":
                    for h in range(2):
                        wait_filled(dve, u, f"n{h}")
                        chain.announce(nc.vector.tensor_scalar(T0[:, 512 * h:512 * h + 512], psum[BANK[f"n{h}"]][:, :],
                                                               1e-24, None, ALU.max),
                                       s_read[BANK[f"n{h}"]], read_count(u, f"n{h}"))
                elif ev == "kn":
                    dve.wait_ge(s_exp, 3 * u + 3)
                    for s in segs:
                        c = slice(s[4], s[4] + s[3])
                        chain(nc.vector.scalar_tensor_tensor(KN[:, c], XK[:, c], pcol("kk", s[0], s[1]), T0[:, c],
                                                             ALU.mult, ALU.mult))
                elif ev == "kp":
                    for h in range(2):
                        wait_read(dve, u, f"la{h}")
                    for s in segs:
                        c = slice(s[4], s[4] + s[3])
                        o = 26 + 4 * s[0] + s[1]
                        chain(nc.vector.tensor_scalar(T0[:, c], AV[:, c], pcol("ka", s[0], s[1]),
                                                      oneminus[:, o:o + 1], ALU.mult, ALU.add))
                    chain(nc.vector.tensor_tensor(XK, XK, T0, ALU.mult))
                    chain(nc.vector.tensor_tensor(AV, AV, KN, ALU.mult))
                elif ev == "ar":
                    if u >= 2:
                        dve.wait_ge(s_Y, step_at(u - 1, 0))
                    chain(nc.vector.scalar_tensor_tensor(AR[b][:, :, 0:C], gc(KN), -1.0, E1[:, :, 0:C],
                                                         ALU.mult, ALU.mult))
                    chain(nc.vector.tensor_copy(PC[b].unsqueeze(2), E1[:, :, C:C + 1]))
                    chain.announce(nc.vector.tensor_tensor(AR[b][:, :, C:2 * C], gc(XR), E1[:, :, 1:C + 1], ALU.mult),
                                 s_ar, u + 1)
                elif ev == "bk":
                    chain(nc.vector.tensor_tensor(BK[:, :, 0:C], gc(AV), gc(EI), ALU.mult))
                    chain.announce(nc.vector.tensor_tensor(BK[:, :, C:2 * C], gc(XK), gc(EI), ALU.mult), s_bk, u + 1)
                    for n, s in enumerate(segs):
                        c = slice(s[4], s[4] + s[3])
                        ins_ = nc.vector.scalar_tensor_tensor(T0[:, c], XR[:, c], pcol("rk", s[0], s[1]), XK[:, c],
                                                              ALU.mult, ALU.mult)
                        if n < len(segs) - 1:
                            chain(ins_)
                    chain.announce(ins_, s_rk, u + 1)
                elif ev.startswith("gram"):
                    for q in (2 * int(ev[4:]), 2 * int(ev[4:]) + 1):
                        wait_filled(dve, u, f"g{q}")
                        chain.announce(nc.vector.tensor_tensor(
                            GM[b][:, GC * (q % 2) + 4 * (q // 2):GC * (q % 2) + 4 * (q // 2) + 4, :], psum[BANK[f"g{q}"]][:, :].rearrange("p (n c) -> p n c", c=P),
                            const("gmask").unsqueeze(1).broadcast_to([P, 4, P]), ALU.mult),
                            s_read[BANK[f"g{q}"]], read_count(u, f"g{q}"))
                elif ev == "bonus":
                    for h, part in enumerate(halves(u)):
                        wait_filled(dve, u, f"b{h}")
                        todo_ = []
                        for s in part:
                            d, j, off, n, c0 = s
                            v = VP[:, C + c0:C + c0 + n]
                            sums = psum[BANK[f"b{h}"]][:, c0 % 512:c0 % 512 + n]
                            t0 = 0 if off == ZP else TP
                            y = ysum[:, j, t0:t0 + n]
                            if d == 0:
                                ins_ = nc.vector.tensor_tensor(y, sums, v, ALU.mult)
                            else:
                                ins_ = nc.vector.tensor_tensor(T0[:, c0:c0 + n], sums, v, ALU.mult)
                                todo_.append((y[:, ::-1], T0[:, c0:c0 + n]))
                            if s is not part[-1]:
                                chain(ins_)
                            elif not todo_:
                                chain.announce(ins_, s_read[BANK[f"b{h}"]], read_count(u, f"b{h}"))
                            else:
                                chain(ins_)
                        for n, (y, t) in enumerate(todo_):
                            ins_ = nc.vector.tensor_tensor(y, y, t, ALU.add)
                            if n < len(todo_) - 1:
                                chain(ins_)
                            else:
                                chain.announce(ins_, s_read[BANK[f"b{h}"]], read_count(u, f"b{h}"))
                elif ev.startswith("inv") and ev[3:].isdigit():
                    part = int(ev[3:])
                    if part == 0:
                        dve.wait_ge(s_ul, 32 * (u + 1))
                        if u:
                            dve.wait_ge(s_wcopy, 2 * u)
                        chain(nc.vector.memset(invb[:, 0:512], 0.0))
                        for q in range(2):
                            chain(nc.vector.memset(invb[64 * q:64 * q + 64, 16 * q:512:33], 1.0))
                    cuts = [31, 26, 20, 14, 7, 0]
                    for t in range(cuts[part], cuts[part + 1], -1):
                        j0 = t // 2
                        w = [P, t, 16 - j0]
                        tmp = WTMP[:, 0:t, j0:16]
                        chain(nc.vector.tensor_tensor(tmp, UL[:, 0:t, t:t + 1].broadcast_to(w),
                                                      WI[:, t:t + 1, j0:16].broadcast_to(w), ALU.mult))
                        ins_ = nc.vector.tensor_tensor(WI[:, 0:t, j0:16], WI[:, 0:t, j0:16], tmp, ALU.add)
                        if t > 1:
                            chain(ins_)
                        else:
                            chain.announce(ins_, s_inv, u + 1)
                elif ev == "merge_y":
                    for h in range(2):
                        wait_filled(dve, u, f"y{h}")
                        chain.announce(nc.vector.tensor_copy(
                            Y1[32:64, 16 * h:16 * h + 16, :],
                            psum[BANK[f"y{h}"]][32:64, :].rearrange("p (n t) -> p n t", t=32)),
                            s_read[BANK[f"y{h}"]], read_count(u, f"y{h}"))
                elif ev == "merge_z":
                    for h in range(2):
                        wait_filled(dve, u, f"z{h}")
                        chain.announce(nc.vector.tensor_copy(
                            GM[b][0:32, 16 * h:16 * h + 16, 32:64],
                            psum[BANK[f"z{h}"]][0:32, :].rearrange("p (n t) -> p n t", t=32)),
                            s_read[BANK[f"z{h}"]], read_count(u, f"z{h}"))
                elif ev == "X":
                    g, n = step_at(u, i), len(chunks(u, i))
                    if i == 0:
                        if u == NU - 1:
                            ins_ = nc.vector.memset(ST[:, 0, 0:n], 0.0)
                        else:
                            ins_ = nc.vector.tensor_copy(ST[:, 0, 0:n], S0[:, 2 * u:2 * u + 2])
                        chain.announce(ins_, s_ST, g + u + 1)
                    dve.wait_ge(s_X, g + 1)
                    for h in range(2):
                        ins_ = nc.vector.tensor_tensor(
                            XS[0:64, 8 * C * h:8 * C * h + n * C].rearrange("p (n c) -> p n c", c=C),
                            psum[6 + h][0:64, 0:n * C].rearrange("p (n c) -> p n c", c=C),
                            SAV[b][0:64, i::steps(u), C * h:C * h + C], ALU.add)
                        if h == 0:
                            chain(ins_)
                    chain.announce(ins_, s_XS, g + 1)
                elif ev == "T":
                    n = len(chunks(u, i))
                    pc = PC[b][:, i::steps(u)].unsqueeze(2).broadcast_to([P, n, C])
                    chain(nc.vector.tensor_tensor(SP_[:, 0:n], ST[:, i % 2, 0:n], pc, ALU.mult))
                elif ev == "S":
                    g, n = step_at(u, i), len(chunks(u, i))
                    dve.wait_ge(s_S, g + 1)
                    if g:
                        dve.wait_ge(s_Y, g)
                    chain.announce(nc.vector.tensor_tensor(
                        ST[:, (i + 1) % 2, 0:n], psum[5][:, 0:n * C].rearrange("p (n c) -> p n c", c=C), SP_[:, 0:n],
                        ALU.add), s_ST, g + u + 2)
                elif ev == "Y":
                    g, n = step_at(u, i), len(chunks(u, i))
                    dve.wait_ge(s_Y, g + 1)
                    y = psum[4][:, 0:n * C].rearrange("p (n c) -> p n c", c=C)
                    if u == NU - 1:
                        a = ysum[:, :, i * C:(i + 1) * C]
                        chain(nc.vector.tensor_tensor(a, a, y[:, 0:4], ALU.add))
                        a = ysum[:, :, TP - (i + 1) * C:TP - i * C][:, :, ::-1]
                        ins_ = nc.vector.tensor_tensor(a, a, y[:, 4:8], ALU.add)
                    else:
                        d, j = segs[0][0], segs[0][1]
                        a = ysum[:, j:j + 2, TP + i * C:TP + (i + 1) * C]
                        if d:
                            a = ysum[:, j:j + 2, T - (i + 1) * C:T - i * C][:, :, ::-1]
                        ins_ = nc.vector.tensor_tensor(a, a, y, ALU.add)
                    chain.announce(ins_, s_YS, g + 1)

        def pool_mix(chain):
            pool = nc.gpsimd
            pool.wait_ge(s_zmm, NZ)
            for s in s_ust:
                pool.wait_ge(s, 32)
            for lo in (0, UP + TP, US + TS):
                chain(nc.gpsimd.memset(uin[:, lo:lo + 15], 0.0))

            def load_tile(j):
                pool.dma_start(uin[:, UP:UP + TP], uconv[j][:, 0:TP]).then_inc(s_uin, 16)
                pool.dma_start(uin[:, US:US + TS], uconv[j][:, TP:T]).then_inc(s_uin, 16)

            load_tile(0)

            def tap(j, k):
                if k == 0:
                    pool.wait_ge(s_uin, 32 * (j + 1))
                    if j:
                        pool.wait_ge(s_cst, 16 * j)
                u_, w = uin[:, k:k + CT], convw[:, 4 * k + j:4 * k + j + 1]
                if k == 0:
                    chain(nc.gpsimd.tensor_scalar(cacc, u_, w, par[:, PAR["cb"] + j:PAR["cb"] + j + 1],
                                                  ALU.mult, ALU.add))
                    return
                if by_scalar(k):
                    n = scalar_taps(j, k)
                    pool.wait_ge(s_cprod, n + 1)
                    chain.announce(nc.gpsimd.tensor_tensor(cacc, cacc, cprod[:, 1], ALU.add), s_cadd, n + 1)
                    return
                chain(nc.gpsimd.tensor_scalar(cprod[:, 0], u_, w, None, ALU.mult))
                ins_ = nc.gpsimd.tensor_tensor(cacc, cacc, cprod[:, 0], ALU.add)
                if k < CW - 1:
                    chain(ins_)
                    return
                chain.announce(ins_, s_cacc, j + 1)
                pool.dma_start(cout[j], cacc).then_inc(s_cst, 16)
                if j + 1 < 4:
                    load_tile(j + 1)

            for ev, u, i in order("pool"):
                if ev == "tap":
                    tap(u, i)
                elif ev == "scale":
                    b = u % 2
                    wait_filled(pool, u, "g7")
                    pool.wait_ge(s_bk, u + 1)
                    chain.announce(nc.gpsimd.tensor_tensor(BK, BK, PC[b].unsqueeze(2).broadcast_to([P, GC, 2 * C]),
                                                           ALU.mult), s_bkh, u + 1)

        def pe_mix():
            pe = nc.tensor
            for ev, u, i in order("pe"):
                b = u % 2
                segs = UNITS[u]
                if ev == "init":
                    pe.wait_ge(s_sl, 16 * 8)
                    for a in range(8):
                        mm = nc.tensor.transpose(psum[5][:, a * C:(a + 1) * C], SL[0:64, a], ident[0:64, 0:64])
                    mm.then_inc(s_slT, 1)
                elif ev in ("lora_w", "lora_a"):
                    pe.wait_ge(s_xl, 2)
                    pe.wait_ge(s_lora, 32)
                    if u == 0:
                        pe.wait_ge(s_zeva, NZ)
                        pe.wait_ge(s_zevd, NZ)
                    for name, r in ((("lw", slice(0, 64)),) if ev == "lora_w" else (("la", slice(64, 128)),)):
                        for h, part in enumerate(halves(u)):
                            wait_free(pe, u, f"{name}{h}")
                            for d, j, off, n, c0 in part:
                                t0 = 0 if off == ZP else TP
                                mm = nc.tensor.matmul(psum[BANK[f"{name}{h}"]][:, c0 % 512:c0 % 512 + n],
                                                      lorab[r, d, j * P:(j + 1) * P], xlora[r, d, t0:t0 + n],
                                                      start=True, stop=True)
                            mm.then_inc(s_summed, 1)
                elif ev in ("norm", "bonus"):
                    name = ev[0]
                    pe.wait_ge(s_sq if name == "n" else s_rk, u + 1)
                    for h in range(2):
                        wait_free(pe, u, f"{name}{h}")
                        nc.tensor.matmul(psum[BANK[f"{name}{h}"]][:, :], headones, T0[:, 512 * h:512 * h + 512],
                                         start=True, stop=True).then_inc(s_summed, 1)
                elif ev.startswith("gram"):
                    pe.wait_ge(s_ar, u + 1)
                    pe.wait_ge(s_bk, u + 1)
                    for q in (2 * int(ev[4:]),):
                        wait_free(pe, u, f"g{q}")
                        wait_free(pe, u, f"g{q + 1}")
                        for n in range(4):
                            gc_ = 2 * q + n
                            for h in range(2):
                                r = slice(64 * h, 64 * h + 64)
                                mm = nc.tensor.matmul(psum[BANK[f"g{q + h}"]][:, n * P:(n + 1) * P], BK[r, gc_, :],
                                                      AR[b][r, gc_, :], start=True, stop=True)
                                if n == 3:
                                    mm.then_inc(s_summed, 1)
                elif ev in ("turn_bk", "turn_v"):
                    name = "t" if ev == "turn_bk" else "v"
                    pe.wait_ge(s_bkh if name == "t" else s_shiftD, (u + 1) * (1 if name == "t" else 3))
                    for q in range(4):
                        wait_free(pe, u, f"{name}{q}")
                        for n in range(4):
                            g_ = 4 * q + n
                            src = BK[:, g_, :] if name == "t" else VP[:, g_ * C:g_ * C + P]
                            mm = nc.tensor.transpose(psum[BANK[f"{name}{q}"]][:, n * P:(n + 1) * P], src, ident)
                        mm.then_inc(s_summed, 1)
                elif ev == "mv":
                    for q in range(4):
                        wait_read(pe, u, f"v{q}")
                    for q in range(4):
                        wait_free(pe, u, f"m{q}")
                        for n in range(8):
                            gc_, h = 8 * (q % 2) + n, q // 2
                            mm = nc.tensor.matmul(psum[BANK[f"m{q}"]][0:64, n * C:(n + 1) * C],
                                                  GM[b][64:128, GC * h + gc_, 0:C],
                                                  SAV[b][64:128, gc_, C * h:C * h + C], start=True, stop=True)
                        mm.then_inc(s_summed, 1)
                elif ev in ("place", "merge_y", "merge_z"):
                    pe.wait_ge(s_wcopy, 2 * (u + 1))
                    lo, hi = slice(0, 32), slice(32, 64)
                    for name in ({"place": "ta", "merge_y": "y", "merge_z": "z"}[ev],):
                        for h in range(2):
                            wait_free(pe, u, f"{name}{h}")
                            if name == "y":
                                wait_read(pe, u, f"ta{h}")
                            if name == "z":
                                wait_read(pe, u, f"y{h}")
                            for n in range(16):
                                p_ = 16 * h + n
                                c = slice(32 * n, 32 * n + 32)
                                bank = psum[BANK[f"{name}{h}"]]
                                if name == "ta":
                                    mm = nc.tensor.matmul(bank[lo, c], GM[b][lo, p_, 0:32], ident[lo, 0:32],
                                                          start=True, stop=True)
                                elif name == "y":
                                    mm = nc.tensor.matmul(bank[hi, c], GM[b][lo, p_, 32:64], TA[lo, p_, :],
                                                          start=True, stop=True)
                                else:
                                    mm = nc.tensor.matmul(bank[lo, c], Y1[hi, p_, :], GM[b][hi, p_, 32:64],
                                                          start=True, stop=True)
                            mm.then_inc(s_summed, 1)
                elif ev == "X":
                    g = step_at(u, i)
                    pe.wait_ge(s_ST, g + u + 1)
                    if i == 0:
                        for use in ("z0", "z1", "m2", "m3"):
                            wait_read(pe, u, use)
                    if g:
                        pe.wait_ge(s_SAS, g)
                    for k, gc_ in enumerate(chunks(u, i)):
                        for h in range(2):
                            r = slice(64 * h, 64 * h + 64)
                            mm = nc.tensor.matmul(psum[6 + h][0:64, k * C:(k + 1) * C], AR[b][r, gc_, 0:C],
                                                  ST[r, i % 2, k, :], start=True, stop=True)
                    mm.then_inc(s_X, 1)
                elif ev == "T":
                    g = step_at(u, i)
                    pe.wait_ge(s_XS, g + 1)
                    for k, gc_ in enumerate(chunks(u, i)):
                        for h in range(2):
                            at = 8 * C * h + C * k
                            mm = nc.tensor.matmul(psum[6 + h][0:64, k * C:(k + 1) * C], GM[b][0:64, GC * h + gc_, 0:C],
                                                  XS[0:64, at:at + C], start=True, stop=True)
                    mm.then_inc(s_SA, 1)
                elif ev == "S":
                    g = step_at(u, i)
                    pe.wait_ge(s_SAS, g + 1)
                    for k, gc_ in enumerate(chunks(u, i)):
                        for h in range(2):
                            hc = slice(C * h, C * h + C)
                            mm = nc.tensor.matmul(psum[5][64 * h:64 * h + 64, k * C:(k + 1) * C],
                                                  BKT[b][:, gc_, hc], SAV[b][:, gc_, hc], start=True, stop=True)
                    mm.then_inc(s_S, 1)
                elif ev == "Y":
                    g = step_at(u, i)
                    if g:
                        pe.wait_ge(s_YS, g)
                    for part in range(2):
                        for k, gc_ in enumerate(chunks(u, i)):
                            for h in range(2):
                                r = slice(64 * h, 64 * h + 64)
                                out = psum[4][r, k * C:(k + 1) * C]
                                if part == 0:
                                    nc.tensor.matmul(out, SAV[b][:, gc_, C * h:C * h + C],
                                                     GM[b][:, GC * h + gc_, C:2 * C],
                                                     start=(k == 0), stop=False, skip_group_check=True)
                                else:
                                    mm = nc.tensor.matmul(out, ST[r, i % 2, k, :], AR[b][r, gc_, C:2 * C],
                                                          start=False, stop=True, skip_group_check=True)
                    mm.then_inc(s_Y, 1)
                elif ev == "final":
                    pe.wait_ge(s_ST, step_at(u, 1) + u + 2)
                    for a in range(8):
                        mm = nc.tensor.transpose(psum[6 + a // 4][0:64, (a % 4) * P:(a % 4 + 1) * P],
                                                 ST[:, 0, a, :], ident)
                    mm.then_inc(s_fin, 1)
        EXPERT = 3 * 2048
        NB = 5
        ebuf = [ARENA - (n + 1) * EXPERT for n in range(NB)]
        regp = Region(wbase, ebuf[NB - 1])
        x2 = regp.take(TILES, D)
        NOV = 9
        NSLOT = NEXP + NOV
        tab = regp.take(NSLOT, 4)
        ovid = regp.take(16)
        regs = Region(ebuf[NB - 1], ebuf[1])
        conv = regs.take(4, CT)
        sq2 = regs.take(2, CT)
        rstd = regs.take(CT)
        g1b, gain2, sh2b = regs.take(2, D), regs.take(2, D), regs.take(2, D)
        h2 = regs.take(D)
        xtmp, xsq, sq_pos = regs.take(D), regs.take(D), regs.take(D)
        rw_, rw_e, rb = regs.take(KD, 4), regs.take(KD, 32), regs.take(36)
        h2T = view(zbase + 3 * PAIRS * ZT + ZT, KD, P)
        routing = Region(ebuf[NB - 1], ebuf[NB - 1] + 4 * CT + 3 * CT)
        h2d = dram("tokens_for_experts", [T, D])
        slots = dram("slots", [NSLOT * P, 4], I32)
        yexp = dram("expert_rows", [2 * T, D])

        s_modb, s_conv_in = sem("mod_rows_landed"), sem("conv_landed")
        s_rw = sem("router_landed")
        s_gmean, s_gvar, s_gate = sem("head_means"), sem("head_variances"), sem("gates_summed")
        s_gd, s_gsq, s_gstd, s_gv, s_mixa = (sem(n) for n in (
            "head_centred", "head_squares", "head_deviation", "head_variance_taken", "rwkv_mixed"))
        s_cn, s_mixc = sem("conv_normed"), sem("conv_mixed")
        s_x2in, s_pos2 = sem("residual_landed"), sem("positions_landed_again")
        s_wo, s_x2, s_h2, s_h2st = (sem(n) for n in (
            "w_out_summed", "residual_ready", "expert_input_ready", "expert_input_stored"))
        s_h2t, s_h2Ta, s_h2Td, s_lg = (sem(n) for n in (
            "expert_input_turned", "h2T_low_ready", "h2T_high_ready", "logits_summed"))
        HC = [(0, 328), (328, CT)]

        def conv_tokens(i):
            at = 0 if i == 0 else P + 15 + (i - 1) * P
            return slice(at, at + P)

        def sp_out():
            sp = nc.sync
            sp.wait_ge(s_finst, 128)
            sp.wait_ge(s_Y, step_at(NU - 1, 2))
            sp.wait_ge(s_YS, step_at(NU - 1, 2))
            sp.wait_ge(s_cst, 64)
            for j in range(4):
                sp.dma_start(conv[:, j], cout[j]).then_inc(s_conv_in, 16)
            sp.dma_start(rw_, ins["router_group_w"][0].rearrange("(k p) n -> p k n", p=P)).then_inc(s_rw, 16)
            sp.dma_start(rw_e, ins["router_expert_w"][0].rearrange("(k p) n -> p k n", p=P)).then_inc(s_rw, 16)
            sp.dma_start(rb[:, 0:4], ins["router_group_b"].broadcast_to([P, 4])).then_inc(s_rw, 16)
            sp.dma_start(rb[:, 4:36], ins["router_expert_b"].broadcast_to([P, 32])).then_inc(s_rw, 16)
            for i in range(TILES):
                sp.dma_start(x2[:, i], tok_src(i)).then_inc(s_x2in, 16)
            for c in range(2):
                for dst, m in ((g1b, 2), (sh2b, 3), (gain2, 4)):
                    sp.dma_start(dst[:, c], modrows[c:c + 1, m * D:(m + 1) * D].broadcast_to([P, D])
                                 ).then_inc(s_modb, 16)
            sp.dma_start(h2, ins["norm2_g"].broadcast_to([P, D])).then_inc(s_modb, 16)

        def experts_load(n):
            sp = nc.sync
            b = ebuf[n % NB]
            if n >= NB:
                sp.wait_ge(s_edown, n - NB + 1)
            for m, name in enumerate(("expert_w_gate", "expert_w_up", "expert_w_down")):
                sp.dma_start(view(b + 2048 * m, 2048), ins[name][0, n].rearrange("(p c) f -> p (c f)", p=P)
                             ).then_inc(s_ew[n % NB], 16)

        def pe_out():
            pe = nc.tensor
            pe.wait_ge(s_YS, step_at(NU - 1, 2))
            pe.wait_ge(s_finc, 1)
            for j in range(PAIRS + 1):
                if j < PAIRS:
                    if j:
                        pe.wait_ge(s_gd, j)
                    for h in range(2):
                        mm = nc.tensor.matmul(psum[h][:, 0:HALF], headones, ysum[:, j, h * HALF:(h + 1) * HALF],
                                              start=True, stop=True)
                    mm.then_inc(s_gmean, 1)
                if j == 0:
                    pe.wait_ge(s_gateb, 32)
                    continue
                pe.wait_ge(s_gsq, j)
                if j > 1:
                    pe.wait_ge(s_gv, j - 1)
                for h in range(2):
                    mm = nc.tensor.matmul(psum[2 + h][:, 0:HALF], headones,
                                          sq2[:, (j - 1) % 2, h * HALF:(h + 1) * HALF], start=True, stop=True)
                mm.then_inc(s_gvar, 1)
                if j > 1:
                    pe.wait_ge(s_mixa, j - 1)
                for h in range(2):
                    mm = nc.tensor.matmul(psum[4 + h][:, 0:HALF], gateb[:, (j - 1) * P:j * P],
                                          gsig[:, h * HALF:(h + 1) * HALF], start=True, stop=True)
                mm.then_inc(s_gate, 1)
            pe.wait_ge(s_conv_in, 64)
            for h, (lo, hi) in enumerate(HC):
                for j in range(4):
                    mm = nc.tensor.matmul(psum[6 + h][:, 0:hi - lo], ones, conv[:, j, lo:hi],
                                          start=(j == 0), stop=(j == 3))
            mm.then_inc(s_gmean, 1)
            pe.wait_ge(s_gd, PAIRS + 4)
            for j in range(4):
                pe.wait_ge(s_gsq, PAIRS + j + 1)
                for h, (lo, hi) in enumerate(HC):
                    mm = nc.tensor.matmul(psum[6 + h][:, 0:hi - lo], ones, sq2[:, j % 2, lo:hi],
                                          start=(j == 0), stop=(j == 3))
                mm.then_inc(s_gvar, 1)
            pe.wait_ge(s_mixa, 4)
            pe.wait_ge(s_mixc, 4)
            pe.wait_ge(s_wout, 16)

            def turn(i):
                pe.wait_ge(s_h2, i + 1)
                if i:
                    pe.wait_ge(s_h2Ta, i)
                    pe.wait_ge(s_h2Td, i)
                for k in range(KD):
                    mm = nc.tensor.transpose(psum[4 + k // 4][:, (k % 4) * P:(k % 4 + 1) * P],
                                             h2[:, k * P:(k + 1) * P], ident)
                mm.then_inc(s_h2t, 1)
                pe.wait_ge(s_h2Ta, i + 1)
                pe.wait_ge(s_h2Td, i + 1)
                if i == 0:
                    pe.wait_ge(s_rw, 64)
                for lo, hi, w in ((0, 4, rw_), (4, 36, rw_e)):
                    for k in range(KD):
                        mm = nc.tensor.matmul(psum[6][:, 36 * i + lo:36 * i + hi], h2T[:, k], w[:, k],
                                              start=(k == 0), stop=(k == KD - 1))
                mm.then_inc(s_lg, 1)

            for i in range(TILES):
                for n in range(2):
                    if i >= 2:
                        pe.wait_ge(s_x2, i - 1)
                    for c in range(8):
                        lhs = ysum[:, c, i * P:(i + 1) * P] if c < 4 else conv[:, c - 4, conv_tokens(i)]
                        mm = nc.tensor.matmul(psum[2 * (i % 2) + n][:, :], lhs, wout[:, c, n * 512:(n + 1) * 512],
                                              start=(c == 0), stop=(c == 7))
                mm.then_inc(s_wo, 1)
                if i:
                    turn(i - 1)
            turn(TILES - 1)

        def dve_out(chain):
            dve = nc.vector
            def centre(j):
                y = ysum[:, j]
                dve.wait_ge(s_gmean, j + 1)
                for h in range(2):
                    c = slice(h * HALF, (h + 1) * HALF)
                    ins_ = nc.vector.scalar_tensor_tensor(y[:, c], psum[h][:, 0:HALF], -1.0 / 64, y[:, c],
                                                          ALU.mult, ALU.add)
                    if h == 0:
                        chain(ins_)
                chain.announce(ins_, s_gd, j + 1)

            centre(0)
            for j in range(PAIRS):
                if j + 1 < PAIRS:
                    centre(j + 1)
                y = ysum[:, j]
                dve.wait_ge(s_gvar, j + 1)
                chain(nc.vector.tensor_scalar(rstd[:, 0:HALF], psum[2][:, 0:HALF], 1.0 / 64, GN_EPS, ALU.mult, ALU.add))
                chain.announce(nc.vector.tensor_scalar(rstd[:, HALF:T], psum[3][:, 0:HALF], 1.0 / 64, GN_EPS,
                                                       ALU.mult, ALU.add), s_gv, j + 1)
                dve.wait_ge(s_gstd, j + 1)
                g, b_ = PAR["gng"] + j, PAR["gnb"] + j
                chain(nc.vector.scalar_tensor_tensor(y, y, par[:, g:g + 1], rstd[:, 0:T], ALU.mult, ALU.mult))
                dve.wait_ge(s_gate, j + 1)
                for h in range(2):
                    c = slice(h * HALF, (h + 1) * HALF)
                    ins_ = nc.vector.scalar_tensor_tensor(y[:, c], y[:, c], par[:, b_:b_ + 1], psum[4 + h][:, 0:HALF],
                                                          ALU.add, ALU.mult)
                    if h == 0:
                        chain(ins_)
                chain.announce(ins_, s_mixa, j + 1)
            dve.wait_ge(s_gmean, PAIRS + 1)
            for j in range(4):
                for h, (lo, hi) in enumerate(HC):
                    ins_ = nc.vector.scalar_tensor_tensor(conv[:, j, lo:hi], psum[6 + h][:, 0:hi - lo], -1.0 / 512,
                                                          conv[:, j, lo:hi], ALU.mult, ALU.add)
                    if h == 0:
                        chain(ins_)
                chain.announce(ins_, s_gd, PAIRS + j + 1)
            dve.wait_ge(s_gvar, PAIRS + 4)
            for h, (lo, hi) in enumerate(HC):
                ins_ = nc.vector.tensor_scalar(rstd[:, lo:hi], psum[6 + h][:, 0:hi - lo], 1.0 / 512, LN_EPS,
                                               ALU.mult, ALU.add)
                if h == 0:
                    chain(ins_)
            chain.announce(ins_, s_gv, PAIRS + 1)
            dve.wait_ge(s_gstd, PAIRS + 1)
            for j in range(4):
                chain.announce(nc.vector.tensor_tensor(conv[:, j], conv[:, j], rstd, ALU.mult), s_cn, j + 1)
            dve.wait_ge(s_modb, 16 * 7)
            for c in range(2):
                chain(nc.vector.scalar_tensor_tensor(gain2[:, c], gain2[:, c], 1.0, h2, ALU.add, ALU.mult))
            dve.wait_ge(s_x2in, 16 * TILES)

            def taken(i):
                dve.wait_ge(s_h2t, i + 1)
                chain.announce(nc.vector.tensor_copy(h2T[:, 4:8], psum[5][:, :].rearrange("p (k t) -> p k t", t=P)),
                             s_h2Td, i + 1)

            for i in range(TILES):
                c = int(i > 0)
                dve.wait_ge(s_wo, i + 1)
                if i:
                    dve.wait_ge(s_pos2, 16 * i)
                    chain(nc.vector.tensor_tensor(x2[:, i], x2[:, i], sq_pos, ALU.add))
                for n in range(2):
                    o = slice(n * 512, n * 512 + 512)
                    chain(nc.vector.tensor_tensor(xtmp[:, o], psum[2 * (i % 2) + n][:, :], g1b[:, c, o], ALU.mult))
                chain.announce(nc.vector.tensor_tensor(x2[:, i], x2[:, i], xtmp, ALU.add), s_x2, i + 1)
                dve.wait_ge(s_xstat, TILES + i + 1)
                chain.announce(nc.vector.tensor_scalar(small[:, i:i + 1], small[:, i:i + 1], 1.0 / D, RMS_EPS,
                                                     ALU.mult, ALU.add), s_var, TILES + i + 1)
                dve.wait_ge(s_std, TILES + i + 1)
                chain(nc.vector.reciprocal(small[:, 16 + i:17 + i], small[:, 8 + i:9 + i]))
                if i:
                    dve.wait_ge(s_h2t, i)
                    dve.wait_ge(s_h2st, 16 * i)
                chain(nc.vector.scalar_tensor_tensor(h2, x2[:, i], small[:, 16 + i:17 + i], gain2[:, c],
                                                     ALU.mult, ALU.mult))
                chain.announce(nc.vector.tensor_tensor(h2, h2, sh2b[:, c], ALU.add), s_h2, i + 1)
                taken(i)

        def act_out(chain):
            act = nc.scalar
            def square(j):
                act.wait_ge(s_gd, j + 1)
                if j >= 2:
                    act.wait_ge(s_gvar, j - 1)
                chain.announce(nc.scalar.activation(sq2[:, j % 2, 0:T], ysum[:, j], ACT.Square), s_gsq, j + 1)

            square(0)
            for j in range(PAIRS):
                if j + 1 < PAIRS:
                    square(j + 1)
                act.wait_ge(s_gv, j + 1)
                chain(nc.scalar.activation(rstd[:, 0:T], rstd[:, 0:T], ACT.Ln))
                chain.announce(nc.scalar.activation(rstd[:, 0:T], rstd[:, 0:T], ACT.Exp, scale=-0.5), s_gstd, j + 1)
            for j in range(4):
                act.wait_ge(s_gd, PAIRS + j + 1)
                if j >= 2:
                    act.wait_ge(s_gvar, PAIRS + j - 1)
                else:
                    act.wait_ge(s_gvar, 4)
                chain.announce(nc.scalar.activation(sq2[:, j % 2], conv[:, j], ACT.Square), s_gsq, PAIRS + j + 1)
            act.wait_ge(s_gv, PAIRS + 1)
            chain(nc.scalar.activation(rstd, rstd, ACT.Ln))
            chain.announce(nc.scalar.activation(rstd, rstd, ACT.Exp, scale=-0.5), s_gstd, PAIRS + 1)
            for j in range(4):
                act.wait_ge(s_cn, j + 1)
                g, b_ = PAR["clg"] + j, PAR["clb"] + j
                chain.announce(nc.scalar.activation(conv[:, j], conv[:, j], ACT.Silu, bias=par[:, b_:b_ + 1],
                                                  scale=par[:, g:g + 1]), s_mixc, j + 1)
            for i in range(TILES):
                if i:
                    if i >= 2:
                        act.wait_ge(s_x2, i)
                    act.dma_start(sq_pos, pos[(i - 1) * P:i * P, :]).then_inc(s_pos2, 16)
                act.wait_ge(s_x2, i + 1)
                chain.announce(nc.scalar.activation(xsq, x2[:, i], ACT.Square, accum_out=small[:, i:i + 1]),
                             s_xstat, TILES + i + 1)
                act.wait_ge(s_var, TILES + i + 1)
                chain.announce(nc.scalar.activation(small[:, 8 + i:9 + i], small[:, i:i + 1], ACT.Sqrt), s_std, TILES + i + 1)
                act.wait_ge(s_h2, i + 1)
                act.dma_start(h2d[i * P:(i + 1) * P, :], h2).then_inc(s_h2st, 16)
                act.wait_ge(s_h2t, i + 1)
                chain.announce(nc.scalar.activation(h2T[:, 0:4], psum[4][:, :].rearrange("p (k t) -> p k t", t=P),
                                                  ACT.Copy), s_h2Ta, i + 1)

        NLANE = 2 * TILES
        lg = routing.take(TILES, 36)
        oh = routing.take(2, TILES, 32)
        ohg = routing.take(TILES, 4)
        sel, seq_ = routing.take(TILES, 32), routing.take(TILES, 32)
        both, base = routing.take(TILES, 32), routing.take(TILES + 1, 32)
        pick = routing.take(2, TILES, 32)
        iot = routing.take(32)
        mx, mn = routing.take(2, TILES), routing.take(2, TILES)
        gexp = routing.take(TILES, 4)
        t1, t2, t3, t4 = (routing.take(TILES) for _ in range(4))
        r_, ob, kk_, big, tl = (routing.take(2, TILES) for _ in range(5))
        nt, inc, ovb = routing.take(32), routing.take(32), routing.take(32)
        ova, ovc = routing.take(NOV, 32), routing.take(NOV, 32)
        oint = routing.take(16)
        ent = routing.take(NLANE, 4)
        sloti = routing.take(NLANE)
        initt = routing.take(NSLOT, 4)
        MISS = 1 << 20

        NG = 4
        regm = Region(zbase, wbase)
        xe, xeT = regm.take(NG, D), regm.take(2, KD, P)
        hid, hidT = regm.take(2, 256), regm.take(2, 2, P)
        eo = regm.take(2, D)
        ovtab = regm.take(4)
        OVB = NEXP % NB
        OVFILLS = NEXP // NB
        rege = Region(zbase, wbase)
        NF = 3
        ya, yb = rege.take(NF, D), rege.take(NF, D)
        g2b, fgain, fsq = rege.take(2, D), rege.take(D), rege.take(D)

        s_ew = [sem(f"expert_landed{b}") for b in range(NB)]
        s_mx, s_ge, s_oh, s_rank, s_ent = (sem(n) for n in (
            "gate_logits_centred", "gate_exponentials", "experts_picked", "ranks_summed", "slot_entries_ready"))
        s_tinit0, s_tinit, s_scat, s_tab, s_ovst = (sem(n) for n in (
            "slot_blank_ready", "slots_blank", "slots_filled", "slots_read", "overflow_list_ready"))
        s_gat = [sem(f"expert_rows_gathered{b}") for b in range(NG)]
        s_escat = [sem(f"expert_out_scattered{b}") for b in range(2)]
        s_fst = [sem(f"final_stored{b}") for b in range(NF)]
        s_et, s_eTa, s_eTd = (sem(n) for n in (
            "expert_rows_turned", "xeT_low_ready", "xeT_high_ready"))
        s_gu, s_silu2, s_hid, s_ht, s_hT, s_edown, s_eoa, s_eod = (sem(n) for n in (
            "gate_up_summed", "gate_silu_done", "hidden_ready", "hidden_turned", "hiddenT_ready", "down_summed",
            "expert_out_low", "expert_out_high"))
        s_fin_in = [sem(f"rows_back{b}") for b in range(NF)]
        s_ysum = sem("two_experts_summed")
        s_ovgo = sem("overflow_dma_may_start")
        s_fg, s_xf, s_fout = sem("final_gains_landed"), sem("final_sum_ready"), sem("final_ready")
        from concourse.bass import IndirectOffsetOnAxis as At

        def dve_route(chain):
            dve = nc.vector
            B5 = [P, TILES, 32]
            iotam = const("expiota")
            dve.wait_ge(s_lg, TILES)
            dve.wait_ge(s_h2st, 16 * TILES)
            chain(nc.vector.memset(initt[:, :, 2:4], 0.0))
            chain.announce(nc.vector.memset(initt[:, :, 0:2].bitcast(I32), MISS), s_tinit0, 1)
            chain(nc.vector.tensor_tensor(lg, psum[6][:, 0:36 * TILES].rearrange("p (i e) -> p i e", e=36),
                                          rb.unsqueeze(1).broadcast_to([P, TILES, 36]), ALU.add))
            chain(nc.vector.tensor_scalar(iot, iotam, 64.0, None, ALU.add))
            lgg, lge = lg[:, :, 0:4], lg[:, :, 4:36]

            def first_max(vals, n, out, top, low):
                sh = [P, TILES, n]
                im = iotam[:, 0:n].unsqueeze(1).broadcast_to(sh)
                cand = seq_[:, :, 0:n]
                chain(nc.vector.tensor_reduce(top, vals, AX_X, ALU.max))
                chain(nc.vector.tensor_tensor(cand, vals, top.unsqueeze(2).broadcast_to(sh), ALU.is_ge))
                chain(nc.vector.tensor_tensor(cand, cand, im, ALU.mult))
                chain(nc.vector.tensor_reduce(low, cand, AX_X, ALU.min))
                chain(nc.vector.tensor_tensor(out, im, low.unsqueeze(2).broadcast_to(sh), ALU.is_equal))

            first_max(lgg, 4, ohg, t1, t2)
            chain.announce(nc.vector.tensor_tensor(gexp, lgg, t1.unsqueeze(2).broadcast_to([P, TILES, 4]),
                                                 ALU.subtract), s_mx, 1)
            g4 = ohg.unsqueeze(3).broadcast_to([P, TILES, 4, 8])
            s4 = sel.rearrange("p i (g e) -> p i g e", g=4)
            chain(nc.vector.tensor_tensor(s4, lge.rearrange("p i (g e) -> p i g e", g=4), g4, ALU.mult))
            chain(nc.vector.tensor_scalar(ohg, ohg, 1.0, 1e30, ALU.subtract, ALU.mult))
            chain(nc.vector.tensor_tensor(s4, s4, g4, ALU.add))
            first_max(sel, 32, oh[:, 0], mx[:, 0], mn[:, 0])
            chain(nc.vector.scalar_tensor_tensor(sel, oh[:, 0], -1e30, sel, ALU.mult, ALU.add))
            first_max(sel, 32, oh[:, 1], mx[:, 1], mn[:, 1])
            chain.announce(nc.vector.tensor_tensor(both, oh[:, 0], oh[:, 1], ALU.add), s_oh, 1)
            chain.announce(nc.vector.tensor_tensor(t3, mx[:, 1], mx[:, 0], ALU.subtract), s_mx, 2)
            dve.wait_ge(s_ge, 2)
            chain(nc.vector.tensor_reduce(t1, gexp, AX_X, ALU.add))
            chain(nc.vector.scalar_tensor_tensor(t2, t3, 1.0, t1, ALU.add, ALU.mult))
            chain(nc.vector.reciprocal(t2, t2))
            chain(nc.vector.tensor_copy(ent[:, 0:TILES, 2], t2))
            chain(nc.vector.tensor_tensor(ent[:, TILES:NLANE, 2], t2, t3, ALU.mult))
            chain(nc.vector.memset(ent[:, :, 3], 0.0))
            dve.wait_ge(s_rank, 1)
            chain(nc.vector.memset(base[:, 0], 0.0))
            tot = psum[3][:, 0:160].rearrange("p (i e) -> p i e", e=32)
            for i in range(TILES):
                chain(nc.vector.tensor_tensor(base[:, i + 1], base[:, i], tot[:, i], ALU.add))
            chain(nc.vector.tensor_tensor(both, psum[2][:, 0:160].rearrange("p (i e) -> p i e", e=32),
                                          base[:, 0:TILES], ALU.add))
            n_e = base[:, TILES]
            chain(nc.vector.tensor_scalar(nt, n_e, float(P), None, ALU.is_gt))
            for c in range(2, 5):
                chain(nc.vector.scalar_tensor_tensor(nt, n_e, float(P * c), nt, ALU.is_gt, ALU.add))
            chain(nc.vector.tensor_tensor_scan(inc, const("ones")[:, 0:32], nt, 0.0, ALU.mult, ALU.add))
            chain(nc.vector.tensor_tensor(ovb, inc, nt, ALU.subtract))
            four = [P, 2, TILES, 32]
            chain(nc.vector.tensor_tensor(pick, oh, both.unsqueeze(1).broadcast_to(four), ALU.mult))
            chain(nc.vector.tensor_reduce(r_, pick, AX_X, ALU.add))
            chain(nc.vector.tensor_tensor(pick, oh, ovb.unsqueeze(1).unsqueeze(1).broadcast_to(four), ALU.mult))
            chain(nc.vector.tensor_reduce(ob, pick, AX_X, ALU.add))
            chain(nc.vector.tensor_scalar(kk_, r_, float(P), None, ALU.is_ge))
            for c in range(2, 5):
                chain(nc.vector.scalar_tensor_tensor(kk_, r_, float(P * c), kk_, ALU.is_ge, ALU.add))
            chain(nc.vector.tensor_scalar(big, kk_, 1.0, None, ALU.min))
            chain(nc.vector.tensor_scalar(mn, mn, 64.0, None, ALU.add))
            chain(nc.vector.tensor_tensor(tl, ob, kk_, ALU.add))
            chain(nc.vector.scalar_tensor_tensor(tl, tl, float(NEXP - 1), mn, ALU.add, ALU.subtract))
            chain(nc.vector.tensor_tensor(tl, tl, big, ALU.mult))
            chain(nc.vector.tensor_tensor(tl, tl, mn, ALU.add))
            chain(nc.vector.scalar_tensor_tensor(tl, r_, float(NSLOT), tl, ALU.mult, ALU.add))
            chain(nc.vector.scalar_tensor_tensor(tl, kk_, float(-P * NSLOT), tl, ALU.mult, ALU.add))
            chain(nc.vector.tensor_copy(sloti.bitcast(I32), tl.rearrange("p a b -> p (a b)")))
            tok = const("lanes")[:, 0:TILES]
            e2 = ent.bitcast(I32)
            for k in range(2):
                chain(nc.vector.tensor_copy(e2[:, k * TILES:(k + 1) * TILES, 0], tok))
                ins_ = nc.vector.tensor_scalar(e2[:, k * TILES:(k + 1) * TILES, 1], tok, float(k * T), None, ALU.add)
                if k == 0:
                    chain(ins_)
            chain.announce(ins_, s_ent, 1)
            so = [P, NOV, 32]
            m_ = const("ovi")[:, 0:NOV].unsqueeze(2).broadcast_to(so)
            chain(nc.vector.tensor_tensor(ova, ovb.unsqueeze(1).broadcast_to(so), m_, ALU.is_le))
            chain(nc.vector.tensor_tensor(ovc, inc.unsqueeze(1).broadcast_to(so), m_, ALU.is_gt))
            chain(nc.vector.tensor_tensor(ova, ova, ovc, ALU.mult))
            chain(nc.vector.tensor_tensor(ova, ova, iot.unsqueeze(1).broadcast_to(so), ALU.mult))
            chain(nc.vector.tensor_reduce(oint[:, 0:NOV], ova, AX_X, ALU.add))
            chain(nc.vector.tensor_copy(ovid[:, 0:NOV].bitcast(I32), oint[:, 0:NOV]))
            chain.announce(nc.vector.tensor_copy(ovid[:, 15:16].bitcast(I32), inc[:, 31:32]), s_ovst, 1)

        def act_route(chain):
            act = nc.scalar
            act.wait_ge(s_mx, 1)
            chain.announce(nc.scalar.activation(gexp, gexp, ACT.Exp), s_ge, 1)
            act.wait_ge(s_mx, 2)
            chain.announce(nc.scalar.activation(t3, t3, ACT.Exp), s_ge, 2)

        def pe_route():
            pe = nc.tensor
            pe.wait_ge(s_oh, 1)
            flat = both.rearrange("p i e -> p (i e)")
            nc.tensor.matmul(psum[2][:, 0:160], const("before"), flat, start=True, stop=True)
            nc.tensor.matmul(psum[3][:, 0:160], ones, flat, start=True, stop=True).then_inc(s_rank, 1)

        def pool_route(chain):
            pool = nc.gpsimd
            pool.wait_ge(s_tinit0, 1)
            pool.dma_start(slots.rearrange("(p a) b -> p a b", p=P), initt.bitcast(I32)).then_inc(s_tinit, 16)
            pool.wait_ge(s_wo, TILES)
            pool.wait_ge(s_lg, TILES)
            chain(nc.gpsimd.memset(xe, 0.0))
            pool.wait_ge(s_tinit, 16)
            pool.wait_ge(s_ent, 1)
            for n in range(NLANE):
                pool.indirect_dma_start(out=slots, out_offset=At(ap=sloti[:, n:n + 1].bitcast(U32), axis=0),
                                        in_=ent[:, n, :].bitcast(I32), in_offset=None).then_inc(s_scat, 16)

        def sp_table():
            sp = nc.sync
            sp.wait_ge(s_scat, 16 * NLANE)
            sp.dma_start(tab.bitcast(I32), slots.rearrange("(p a) b -> p a b", p=P)).then_inc(s_tab, 16)

        def gather(pool, n):
            if n >= NG:
                pool.wait_ge(s_et, n - NG + 1)
            pool.indirect_dma_start(out=xe[:, n % NG], out_offset=None, in_=h2d,
                                    in_offset=At(ap=tab[:, n, 0:1].bitcast(U32), axis=0),
                                    bounds_check=T - 1, oob_is_err=False).then_inc(s_gat[n % NG], 16)

        def pool_experts(chain):
            pool = nc.gpsimd
            pool.wait_ge(s_tab, 16)
            pool.wait_ge(s_h2st, 16 * TILES)
            for n in range(NG - 1):
                gather(pool, n)
            for n in range(NEXP):
                if n + NG - 1 < NEXP:
                    gather(pool, n + NG - 1)
                pool.wait_ge(s_eoa, n + 1)
                pool.wait_ge(s_eod, n + 1)
                pool.indirect_dma_start(out=yexp, out_offset=At(ap=tab[:, n, 1:2].bitcast(U32), axis=0),
                                        in_=eo[:, n % 2], in_offset=None,
                                        bounds_check=2 * T - 1, oob_is_err=False).then_inc(s_escat[n % 2], 16)

        def overflow_count(engine):
            engine.wait_ge(s_ovst, 1)
            return engine.value_load(ovid[0:1, 15:16].bitcast(I32), min_val=0, max_val=NOV)

        def sp_overflow():
            sp = nc.sync
            count = overflow_count(sp)
            w = ebuf[OVB]
            with sp.Fori(0, count) as m:
                sp.wait_ge(s_edown, m + NEXP)
                e = sp.value_load(ovid[0:1, bass.ds(m, 1)].bitcast(I32), min_val=0, max_val=NEXP - 1)
                for j, name in enumerate(("expert_w_gate", "expert_w_up", "expert_w_down")):
                    sp.dma_start(view(w + 2048 * j, 2048), ins[name][0, bass.ds(e, 1)].rearrange(
                        "o (p c) f -> p (o c f)", p=P)).then_inc(s_ew[OVB], 16)
                sp.wait_ge(s_escat[0], m * 16 + 8 * NEXP)
                sp.dma_start(ovtab.bitcast(I32), slots.rearrange("(p a) b -> p a b", p=P)[:, bass.ds(m + NEXP, 1), :]
                             ).then_inc(s_tab, 16)
            sp.wait_ge(s_escat[0], count * 16 + 8 * NEXP)
            sp.wait_ge(s_escat[0], 8 * NEXP + 16)
            sp.wait_ge(s_escat[1], 8 * NEXP)

        def pool_overflow():
            pool = nc.gpsimd
            count = overflow_count(pool)
            last_token, last_row = pool.to_reg(T - 1), pool.to_reg(2 * T - 1)
            with pool.Fori(0, count) as m:
                pool.wait_ge(s_tab, m * 16 + 32)
                pool.wait_ge(s_et, m + NEXP)
                pool.sem_inc(s_ovgo, 1)
                pool.indirect_dma_start(out=xe[:, 0], out_offset=None, in_=h2d,
                                        in_offset=At(ap=ovtab[:, 0:1].bitcast(U32), axis=0),
                                        bounds_check=last_token, oob_is_err=False).then_inc(s_gat[0], 16)
                pool.wait_ge(s_eoa, m + NEXP + 1)
                pool.wait_ge(s_eod, m + NEXP + 1)
                pool.sem_inc(s_ovgo, 1)
                pool.indirect_dma_start(out=yexp, out_offset=At(ap=ovtab[:, 1:2].bitcast(U32), axis=0),
                                        in_=eo[:, 0], in_offset=None,
                                        bounds_check=last_row, oob_is_err=False).then_inc(s_escat[0], 16)

        def pe_overflow():
            pe = nc.tensor
            gu, wd = wview(OVB)
            with pe.Fori(0, overflow_count(pe)) as m:
                pe.wait_ge(s_gat[0], m * 16 + (16 // NG) * NEXP + 16)
                pe.wait_ge(s_eTa, m + NEXP)
                pe.wait_ge(s_eTd, m + NEXP)
                for c in range(KD):
                    mm = nc.tensor.transpose(psum[c // 4][:, (c % 4) * P:(c % 4 + 1) * P], xe[:, 0, c::KD], ident)
                mm.then_inc(s_et, 1)
                pe.wait_ge(s_eTa, m + NEXP + 1)
                pe.wait_ge(s_eTd, m + NEXP + 1)
                pe.wait_ge(s_ew[OVB], (m + OVFILLS + 1) * 48)
                pe.wait_ge(s_hid, m + NEXP)
                for c in range(KD):
                    mm = nc.tensor.matmul(psum[2][:, :], xeT[:, 0, c], gu[:, :, c, :], start=(c == 0), stop=(c == KD - 1))
                mm.then_inc(s_gu, 1)
                pe.wait_ge(s_hid, m + NEXP + 1)
                for c in range(2):
                    mm = nc.tensor.transpose(psum[4][:, c * P:(c + 1) * P], hid[:, 0, c::2], ident)
                mm.then_inc(s_ht, 1)
                pe.wait_ge(s_hT, m + NEXP + 1)
                pe.wait_ge(s_eoa, m + NEXP)
                pe.wait_ge(s_eod, m + NEXP)
                for h in range(2):
                    for c in range(2):
                        mm = nc.tensor.matmul(psum[5 + h][:, :], hidT[:, 0, c], wd[:, c, h * 512:(h + 1) * 512],
                                              start=(c == 0), stop=(c == 1))
                mm.then_inc(s_edown, 1)

        def act_overflow():
            act = nc.scalar
            with act.Fori(0, overflow_count(act)) as m:
                act.wait_ge(s_et, m + NEXP + 1)
                nc.scalar.activation(xeT[:, 0, 0:4], psum[0][:, :].rearrange("p (k t) -> p k t", t=P),
                                     ACT.Copy).then_inc(s_eTa, 1)
                act.wait_ge(s_gu, m + NEXP + 1)
                nc.scalar.activation(hid[:, 0], psum[2][:, 0:256], ACT.Silu).then_inc(s_silu2, 1)
                act.wait_ge(s_edown, m + NEXP + 1)
                act.wait_ge(s_escat[0], m * 16 + 8 * NEXP)
                nc.scalar.activation(eo[:, 0, 0:512], psum[5][:, :], ACT.Copy, scale=ovtab[:, 2:3]).then_inc(s_eoa, 1)

        def dve_overflow():
            dve = nc.vector
            with dve.Fori(0, overflow_count(dve)) as m:
                dve.wait_ge(s_et, m + NEXP + 1)
                nc.vector.tensor_copy(xeT[:, 0, 4:8], psum[1][:, :].rearrange("p (k t) -> p k t", t=P)
                                      ).then_inc(s_eTd, 1)
                dve.wait_ge(s_silu2, m + NEXP + 1)
                nc.vector.tensor_tensor(hid[:, 0], hid[:, 0], psum[2][:, 256:512], ALU.mult).then_inc(s_hid, 1)
                dve.wait_ge(s_ht, m + NEXP + 1)
                nc.vector.tensor_copy(hidT[:, 0], psum[4][:, 0:256].rearrange("p (k t) -> p k t", t=P)
                                      ).then_inc(s_hT, 1)
                dve.wait_ge(s_edown, m + NEXP + 1)
                dve.wait_ge(s_escat[0], m * 16 + 8 * NEXP)
                nc.vector.tensor_scalar(eo[:, 0, 512:1024], psum[6][:, :], ovtab[:, 2:3], None, ALU.mult
                                        ).then_inc(s_eod, 1)

        def wview(n):
            b = ebuf[n % NB]
            gu = view(b, 4096).rearrange("p (m c f) -> p m c f", m=2, c=KD)
            return gu, view(b + 4096, 2, D)

        def pe_experts():
            pe = nc.tensor

            def turn(n):
                pe.wait_ge(s_gat[n % NG], 16 * (n // NG + 1))
                if n:
                    pe.wait_ge(s_eTa, n)
                    pe.wait_ge(s_eTd, n)
                for c in range(KD):
                    mm = nc.tensor.transpose(psum[c // 4][:, (c % 4) * P:(c % 4 + 1) * P], xe[:, n % NG, c::KD], ident)
                mm.then_inc(s_et, 1)

            def gate_up(n):
                pe.wait_ge(s_eTa, n + 1)
                pe.wait_ge(s_eTd, n + 1)
                pe.wait_ge(s_ew[n % NB], 48 * (n // NB + 1))
                if n >= 2:
                    pe.wait_ge(s_hid, n - 1)
                gu, _ = wview(n)
                for c in range(KD):
                    mm = nc.tensor.matmul(psum[2 + n % 2][:, :], xeT[:, n % 2, c], gu[:, :, c, :],
                                          start=(c == 0), stop=(c == KD - 1))
                mm.then_inc(s_gu, 1)

            def down(n):
                pe.wait_ge(s_hid, n + 1)
                if n:
                    pe.wait_ge(s_hT, n)
                for c in range(2):
                    mm = nc.tensor.transpose(psum[4][:, c * P:(c + 1) * P], hid[:, n % 2, c::2], ident)
                mm.then_inc(s_ht, 1)
                pe.wait_ge(s_hT, n + 1)
                if n:
                    pe.wait_ge(s_eoa, n)
                    pe.wait_ge(s_eod, n)
                _, wd = wview(n)
                for h in range(2):
                    for c in range(2):
                        mm = nc.tensor.matmul(psum[5 + h][:, :], hidT[:, n % 2, c], wd[:, c, h * 512:(h + 1) * 512],
                                              start=(c == 0), stop=(c == 1))
                mm.then_inc(s_edown, 1)

            pe.wait_ge(s_ent, 1)
            turn(0)
            for n in range(NEXP):
                gate_up(n)
                if n + 1 < NEXP:
                    turn(n + 1)
                if n:
                    down(n - 1)
            down(NEXP - 1)

        def act_experts(chain):
            act = nc.scalar

            def turned(n):
                act.wait_ge(s_et, n + 1)
                if n >= 2:
                    act.wait_ge(s_gu, n - 1)
                chain.announce(nc.scalar.activation(xeT[:, n % 2, 0:4], psum[0][:, :].rearrange("p (k t) -> p k t", t=P),
                                                  ACT.Copy), s_eTa, n + 1)

            def out(n):
                act.wait_ge(s_edown, n + 1)
                if n >= 2:
                    act.wait_ge(s_escat[n % 2], 16 * (n // 2))
                chain.announce(nc.scalar.activation(eo[:, n % 2, 0:512], psum[5][:, :], ACT.Copy,
                                                  scale=tab[:, n, 2:3]), s_eoa, n + 1)

            turned(0)
            for n in range(NEXP):
                if n + 1 < NEXP:
                    turned(n + 1)
                act.wait_ge(s_gu, n + 1)
                chain.announce(nc.scalar.activation(hid[:, n % 2], psum[2 + n % 2][:, 0:256], ACT.Silu), s_silu2, n + 1)
                if n:
                    out(n - 1)
            out(NEXP - 1)

        def dve_experts(chain):
            dve = nc.vector

            def turned(n):
                dve.wait_ge(s_et, n + 1)
                if n >= 2:
                    dve.wait_ge(s_gu, n - 1)
                chain.announce(nc.vector.tensor_copy(xeT[:, n % 2, 4:8], psum[1][:, :].rearrange("p (k t) -> p k t", t=P)),
                             s_eTd, n + 1)

            def out(n):
                dve.wait_ge(s_ht, n + 1)
                chain.announce(nc.vector.tensor_copy(hidT[:, n % 2], psum[4][:, 0:256].rearrange("p (k t) -> p k t", t=P)),
                             s_hT, n + 1)
                dve.wait_ge(s_edown, n + 1)
                if n >= 2:
                    dve.wait_ge(s_escat[n % 2], 16 * (n // 2))
                chain.announce(nc.vector.tensor_scalar(eo[:, n % 2, 512:1024], psum[6][:, :], tab[:, n, 2:3], None,
                                                     ALU.mult), s_eod, n + 1)

            dve.wait_ge(s_tab, 16)
            turned(0)
            for n in range(NEXP):
                if n + 1 < NEXP:
                    turned(n + 1)
                dve.wait_ge(s_silu2, n + 1)
                chain.announce(nc.vector.tensor_tensor(hid[:, n % 2], hid[:, n % 2], psum[2 + n % 2][:, 256:512],
                                                     ALU.mult), s_hid, n + 1)
                if n:
                    out(n - 1)
            out(NEXP - 1)

        def tok_dst(i):
            return outs["y_prompt"][0] if i == 0 else outs["y_sample"][0, (i - 1) * P:i * P, :]

        def sp_end():
            sp = nc.sync
            for c in range(2):
                sp.dma_start(g2b[:, c], modrows[c:c + 1, 5 * D:6 * D].broadcast_to([P, D])).then_inc(s_fg, 16)
            sp.dma_start(fgain, ins["final_norm_g"].rearrange("(o n) -> o n", o=1).broadcast_to([P, D])
                         ).then_inc(s_fg, 16)
            for i in range(TILES):
                if i >= NF:
                    sp.wait_ge(s_fst[i % NF], 16 * (i // NF))
                for k, dst in enumerate((ya, yb)):
                    sp.dma_start(dst[:, i % NF], yexp[k * T + i * P:k * T + (i + 1) * P, :]).then_inc(s_fin_in[i % NF], 16)

        def dve_end(chain):
            dve = nc.vector
            dve.wait_ge(s_fg, 48)

            def residual(i):
                y = ya[:, i % NF]
                dve.wait_ge(s_ysum, i + 1)
                chain(nc.vector.tensor_tensor(y, y, g2b[:, int(i > 0)], ALU.mult))
                chain.announce(nc.vector.tensor_tensor(x2[:, i], x2[:, i], y, ALU.add), s_xf, i + 1)

            residual(0)
            for i in range(TILES):
                if i + 1 < TILES:
                    residual(i + 1)
                y = ya[:, i % NF]
                dve.wait_ge(s_xstat, 2 * TILES + i + 1)
                chain.announce(nc.vector.tensor_scalar(small[:, i:i + 1], small[:, i:i + 1], 1.0 / D, RMS_EPS,
                                                     ALU.mult, ALU.add), s_var, 2 * TILES + i + 1)
                dve.wait_ge(s_std, 2 * TILES + i + 1)
                chain(nc.vector.reciprocal(small[:, 16 + i:17 + i], small[:, 8 + i:9 + i]))
                chain.announce(nc.vector.scalar_tensor_tensor(y, x2[:, i], small[:, 16 + i:17 + i], fgain,
                                                            ALU.mult, ALU.mult), s_fout, i + 1)

        def act_end(chain):
            act = nc.scalar
            for i in range(TILES):
                act.wait_ge(s_xf, i + 1)
                chain.announce(nc.scalar.activation(fsq, x2[:, i], ACT.Square, accum_out=small[:, i:i + 1]),
                             s_xstat, 2 * TILES + i + 1)
                act.wait_ge(s_var, 2 * TILES + i + 1)
                chain.announce(nc.scalar.activation(small[:, 8 + i:9 + i], small[:, i:i + 1], ACT.Sqrt), s_std, 2 * TILES + i + 1)
                act.wait_ge(s_fout, i + 1)
                act.dma_start(tok_dst(i), ya[:, i % NF]).then_inc(s_fst[i % NF], 16)
            for b, stored in enumerate(s_fst):
                act.wait_ge(stored, 16 * len(range(b, TILES, NF)))

        def pool_end(chain):
            pool = nc.gpsimd
            for i in range(TILES):
                pool.wait_ge(s_fin_in[i % NF], 32 * (i // NF + 1))
                chain.announce(nc.gpsimd.tensor_tensor(ya[:, i % NF], ya[:, i % NF], yb[:, i % NF], ALU.add),
                               s_ysum, i + 1)

        @block.sync
        def _(sp):
            sp_front()
            sp_mix()
            sp_out()
            for n in range(2):
                experts_load(n)
            sp_table()
            sp.wait_ge(s_ovst, 1)
            for gathered in s_gat[0:2]:
                sp.wait_ge(gathered, 16)
            for n in range(2, NEXP):
                experts_load(n)
            sp_overflow()
            sp_end()

        @block.scalar
        def _(act):
            chain = act_front()
            act_mix(chain)
            act_out(chain)
            act_route(chain)
            act_experts(chain)
            act_overflow()
            act_end(chain)

        @block.vector
        def _(dve):
            chain = dve_front()
            dve_mix(chain)
            dve_out(chain)
            dve_route(chain)
            dve_experts(chain)
            dve_overflow()
            dve_end(chain)

        @block.gpsimd
        def _(pool):
            chain = Chain(nc.gpsimd, g_self)
            pool_front()
            pool_mix(chain)
            pool_route(chain)
            pool_experts(chain)
            pool_overflow()
            pool_end(chain)

        @block.tensor
        def _(pe):
            pe_front()
            pe_mix()
            pe_out()
            pe_route()
            pe_experts()
            pe_overflow()


def _constants():
    import numpy as np

    c = {}
    i = np.arange(P)
    c["ident"] = np.eye(P)
    c["headones"] = (i[:, None] // 64 == i[None] // 64) * 1.0
    c["ones"] = np.ones((P, P))
    s, t = i[:, None] % C, np.arange(C)[None]
    c["gmask"] = np.concatenate([s < t, s <= t], 1) * 1.0
    c["scanmask"] = np.tile((np.arange(512) % C != 0) * 1.0, (P, 1))
    c["before"] = (i[:, None] < i[None]) * 1.0
    c["expiota"] = np.tile(np.arange(NEXP) - 64, (P, 1))
    c["lanes"] = np.tile(i[:, None], (1, 8)) + 128.0 * np.arange(8)[None]
    c["ovi"] = np.tile(np.arange(16), (P, 1))
    return np.concatenate([c[n] for n, _ in CONSTS], 1).astype(np.float32)


def _positions():
    import numpy as np

    t = np.arange(TS)
    q = D // 4
    f = (1.0 / (np.float32(10000.0) ** (np.arange(q, dtype=np.float32) / np.float32(q)))).astype(np.float32)
    a = (t // 64).astype(np.float32)[:, None] * f
    b = (t % 64).astype(np.float32)[:, None] * f
    return np.concatenate([np.sin(a), np.cos(a), np.sin(b), np.cos(b)], 1).astype(np.float32)


_INS = ("x_prompt", "x_sample", "state_rwkv", "c", "c_ctx", "ada_w", "ada_b", "norm1_g", "w_in", "tshift_mu",
        "decay_w0", "decay_lora_b", "iclr_a0", "iclr_lora_b", "key_k", "key_a", "bonus_r_k", "gate_lora_b",
        "gn_g", "gn_b", "conv_dw_w", "conv_dw_b", "conv_ln_g", "conv_ln_b", "w_out", "norm2_g",
        "router_group_w", "router_group_b", "router_expert_w", "router_expert_b",
        "expert_w_gate", "expert_w_up", "expert_w_down", "final_norm_g")
_OUTS = (("y_prompt", (1, TP, D)), ("y_sample", (1, TS, D)), ("new_state", (1, 1, 2, 8, C, C)))


def kernel(**inputs):
    import numpy as np
    import concourse.bacc as bacc
    from concourse.bass_utils import run_bass_kernel_spmd

    nc = bacc.Bacc("TRN2", target_bir_lowering=False, num_devices=1)
    arrays = {f"in_{name}": np.ascontiguousarray(inputs[name]) for name in _INS}
    arrays["table_constants"] = _constants()
    arrays["table_positions"] = _positions()
    aps = {name: nc.dram_tensor(name, a.shape, mybir.dt.from_np(a.dtype), kind="ExternalInput").ap()
           for name, a in arrays.items()}
    outs = {name: nc.dram_tensor(f"out_{name}", shape, F32, kind="ExternalOutput").ap() for name, shape in _OUTS}
    build(nc, {name: aps[f"in_{name}"] for name in _INS}, aps["table_constants"], aps["table_positions"], outs)
    results = run_bass_kernel_spmd(nc, [arrays], core_ids=[0]).results[0]
    return tuple(results[f"out_{name}"] for name, _ in _OUTS)
```
